# Optimizing a Trainium2 kernel written in Bass

```python
import jax, jax.numpy as jnp
from jax import lax
import numpy as np

D_MODEL = 1024
BATCH = 1
SEQ = 512
DEPTH = 2

MIX_WIDTH = D_MODEL
SGU_CHUNK = 128
SGU_WIDTH = MIX_WIDTH // 2
SGU_GROUPS = 4
SGU_GROUP_DIM = SGU_WIDTH // SGU_GROUPS
ATT_WIDTH = MIX_WIDTH - SGU_WIDTH
ATT_HEAD_DIM = 64
ATT_HEADS = ATT_WIDTH // ATT_HEAD_DIM
IDX_HEADS = 4
IDX_HEAD_DIM = 64
TOPK_MAX = 256
ROPE_THETA = 500000.0
ROPE_FRACTION = 4
D_FF = 2816
Q_BLOCK = 128
RMS_EPS = 1e-6
N_MOD = 9

OFF_SGU_U = 0
OFF_SGU_V = OFF_SGU_U + SGU_WIDTH
OFF_Q = OFF_SGU_V + SGU_WIDTH
OFF_K = OFF_Q + ATT_WIDTH
OFF_V = OFF_K + ATT_WIDTH
OFF_IQ = OFF_V + ATT_WIDTH
OFF_IK = OFF_IQ + IDX_HEADS * IDX_HEAD_DIM
OFF_IW = OFF_IK + IDX_HEAD_DIM
PROJ_WIDTH = OFF_IW + IDX_HEADS


def rms_norm(x, g):
    xf = x.astype(jnp.float32)
    y = xf * lax.rsqrt(jnp.mean(xf * xf, axis=-1, keepdims=True) + RMS_EPS)
    return (y * g.astype(jnp.float32)).astype(x.dtype)

def modulate(h, shift, scale):
    return h * (1 + scale[:, None, :]) + shift[:, None, :]

def swiglu(h, w_in, w_out):
    g, u = jnp.split(h @ w_in, 2, axis=-1)
    return (jax.nn.silu(g) * u) @ w_out

def rope_tables(positions, rot_dim):
    inv_freq = ROPE_THETA ** (-jnp.arange(0, rot_dim, 2, dtype=jnp.float32) / rot_dim)
    ang = positions.astype(jnp.float32)[..., None] * inv_freq
    return jnp.cos(ang)[:, :, None, :], jnp.sin(ang)[:, :, None, :]

def partial_rope(x, cos, sin):
    half = cos.shape[-1]
    rot = 2 * half
    xr = x[..., :rot].astype(jnp.float32)
    x1, x2 = xr[..., :half], xr[..., half:]
    out = jnp.concatenate([x1 * cos - x2 * sin, x2 * cos + x1 * sin], axis=-1).astype(x.dtype)
    return jnp.concatenate([out, x[..., rot:]], axis=-1)

def chunked_sgu(u, v, w_s, b_s):
    B, S, _ = u.shape
    n_chunk = S // SGU_CHUNK
    v = v.reshape(B, n_chunk, SGU_CHUNK, SGU_GROUPS, SGU_GROUP_DIM)
    causal = jnp.tril(jnp.ones((SGU_CHUNK, SGU_CHUNK), dtype=bool))
    w = jnp.where(causal[None], w_s, 0).astype(v.dtype)
    mixed = jnp.einsum('gts,bnsgc->bntgc', w, v) + b_s.T[None, None, :, :, None].astype(v.dtype)
    return u * mixed.reshape(B, S, SGU_WIDTH)

def dsa_attention(q, k, v, qi, ki, wi):
    B, S = q.shape[0], q.shape[1]
    top_k = min(TOPK_MAX, S // 4)
    n_blk = S // Q_BLOCK

    def to_blocks(a):
        return a.reshape((B, n_blk, Q_BLOCK) + a.shape[2:]).swapaxes(0, 1)

    t_blocks = jnp.arange(S, dtype=jnp.int32).reshape(n_blk, Q_BLOCK)
    key_pos = jnp.arange(S, dtype=jnp.int32)
    ki_f = ki.astype(jnp.float32)
    scale = ATT_HEAD_DIM ** -0.5

    def one_block(args):
        qb, qib, wib, tb = args
        logits = jax.nn.relu(jnp.einsum('bqhd,bsd->bqhs', qib.astype(jnp.float32), ki_f))
        score = jnp.einsum('bqh,bqhs->bqs', wib.astype(jnp.float32), logits)
        causal = key_pos[None, :] <= tb[:, None]
        score = jnp.where(causal[None], score, -jnp.inf)
        _, idx = lax.top_k(score, top_k)
        valid = idx <= tb[None, :, None]
        kg = jax.vmap(lambda kb, ib: kb[ib])(k, idx)
        vg = jax.vmap(lambda vb, ib: vb[ib])(v, idx)
        s = jnp.einsum('bqhd,bqkhd->bhqk', qb, kg).astype(jnp.float32) * scale
        s = jnp.where(valid[:, None], s, -jnp.inf)
        p = jax.nn.softmax(s, axis=-1).astype(vg.dtype)
        return jnp.einsum('bhqk,bqkhd->bqhd', p, vg)

    out = lax.map(one_block, (to_blocks(q), to_blocks(qi), to_blocks(wi), t_blocks))
    return out.swapaxes(0, 1).reshape(B, S, ATT_WIDTH)

def token_mix(h, cos, sin, w_in, sgu_w, sgu_b, w_out):
    B, S, _ = h.shape
    p = h @ w_in
    u = jax.nn.gelu(p[..., OFF_SGU_U:OFF_SGU_V], approximate=False)
    va = jax.nn.gelu(p[..., OFF_SGU_V:OFF_Q], approximate=False)
    a_out = chunked_sgu(u, va, sgu_w, sgu_b)
    q = partial_rope(p[..., OFF_Q:OFF_K].reshape(B, S, ATT_HEADS, ATT_HEAD_DIM), cos, sin)
    k = partial_rope(p[..., OFF_K:OFF_V].reshape(B, S, ATT_HEADS, ATT_HEAD_DIM), cos, sin)
    v = p[..., OFF_V:OFF_IQ].reshape(B, S, ATT_HEADS, ATT_HEAD_DIM)
    qi = partial_rope(p[..., OFF_IQ:OFF_IK].reshape(B, S, IDX_HEADS, IDX_HEAD_DIM), cos, sin)
    ki = partial_rope(p[..., OFF_IK:OFF_IW][:, :, None, :], cos, sin)[:, :, 0, :]
    wi = p[..., OFF_IW:PROJ_WIDTH]
    b_out = dsa_attention(q, k, v, qi, ki, wi)
    return jnp.concatenate([a_out, b_out], axis=-1) @ w_out

def first_inputs(seed: int = 0) -> dict:
    key = jax.random.key(seed)
    ks = jax.random.split(key, 24)
    f32 = jnp.float32
    L, D = DEPTH, D_MODEL

    def nrm(k, shape, scale):
        return jax.random.normal(k, shape, f32) * scale

    x = jax.random.normal(ks[0], (BATCH, SEQ, D), f32)
    c = jax.random.normal(ks[1], (BATCH, D), f32)
    positions = (jnp.arange(SEQ, dtype=jnp.int32)[None, :]
                 + jax.random.randint(ks[2], (BATCH, 1), 0, 4096, dtype=jnp.int32))
    return {
        "x": x,
        "c": c,
        "positions": positions,
        "ada_w": nrm(ks[3], (L, D, N_MOD * D), 0.5 * D ** -0.5),
        "ada_b": nrm(ks[4], (L, N_MOD * D), 0.01),
        "norm_ffn1": 1.0 + nrm(ks[5], (L, D), 0.02),
        "ffn1_w_in": nrm(ks[6], (L, D, 2 * D_FF), D ** -0.5),
        "ffn1_w_out": nrm(ks[7], (L, D_FF, D), D_FF ** -0.5),
        "norm_mix": 1.0 + nrm(ks[8], (L, D), 0.02),
        "mix_w_in": nrm(ks[9], (L, D, PROJ_WIDTH), D ** -0.5),
        "sgu_w": nrm(ks[10], (L, SGU_GROUPS, SGU_CHUNK, SGU_CHUNK), SGU_CHUNK ** -0.5),
        "sgu_b": 1.0 + nrm(ks[11], (L, SGU_GROUPS, SGU_CHUNK), 0.02),
        "mix_w_out": nrm(ks[12], (L, MIX_WIDTH, D), MIX_WIDTH ** -0.5),
        "norm_ffn2": 1.0 + nrm(ks[13], (L, D), 0.02),
        "ffn2_w_in": nrm(ks[14], (L, D, 2 * D_FF), D ** -0.5),
        "ffn2_w_out": nrm(ks[15], (L, D_FF, D), D_FF ** -0.5),
        "final_norm": 1.0 + nrm(ks[16], (D,), 0.02),
    }

def first_block(x, c, positions, ada_w, ada_b, norm_ffn1, ffn1_w_in, ffn1_w_out,
              norm_mix, mix_w_in, sgu_w, sgu_b, mix_w_out,
              norm_ffn2, ffn2_w_in, ffn2_w_out, final_norm):
    cos, sin = rope_tables(positions, ATT_HEAD_DIM // ROPE_FRACTION)
    cos, sin = cos.astype(x.dtype), sin.astype(x.dtype)
    c_act = jax.nn.silu(c)
    for l in range(DEPTH):
        mod = c_act @ ada_w[l] + ada_b[l]
        sh1, sc1, g1, sh2, sc2, g2, sh3, sc3, g3 = jnp.split(mod, N_MOD, axis=-1)
        h = modulate(rms_norm(x, norm_ffn1[l]), sh1, sc1)
        x = x + 0.5 * g1[:, None, :] * swiglu(h, ffn1_w_in[l], ffn1_w_out[l])
        h = modulate(rms_norm(x, norm_mix[l]), sh2, sc2)
        x = x + g2[:, None, :] * token_mix(h, cos, sin, mix_w_in[l], sgu_w[l], sgu_b[l], mix_w_out[l])
        h = modulate(rms_norm(x, norm_ffn2[l]), sh3, sc3)
        x = x + 0.5 * g3[:, None, :] * swiglu(h, ffn2_w_in[l], ffn2_w_out[l])
    return rms_norm(x, final_norm)


DEPTH_2 = 1

MEM_LEN = 256
HEAD_DIM = 64
LRU_WIDTH = D_MODEL // 2
LRU_BLOCKS = 8
LRU_BLOCK_W = LRU_WIDTH // LRU_BLOCKS
CONV_W = 4
LRU_C = 8.0
MOBA_HEADS = 4
MOBA_WIDTH = MOBA_HEADS * HEAD_DIM
MOBA_BLOCK = 256
MOBA_TOPK = 3
Q_CHUNK = 128
MEM_HEADS = 4
MEM_WIDTH = MEM_HEADS * HEAD_DIM
MIX_WIDTH_2 = LRU_WIDTH + MOBA_WIDTH + MEM_WIDTH
IN_WIDTH = 2 * LRU_WIDTH + 3 * MOBA_WIDTH + MEM_WIDTH
D_FF_2 = ((8 * D_MODEL // 3 + 127) // 128) * 128
NORM_EPS = 1e-6


def rms_norm_2(x, g):
    xf = x.astype(jnp.float32)
    y = xf * lax.rsqrt(jnp.mean(xf * xf, axis=-1, keepdims=True) + NORM_EPS)
    return (y * g.astype(jnp.float32)).astype(x.dtype)

def swiglu_2(x, w_in, w_out):
    a, b = jnp.split(x @ w_in, 2, axis=-1)
    return (jax.nn.silu(a) * b) @ w_out

def alibi_slopes(n_heads):
    return 2.0 ** (-8.0 * jnp.arange(1, n_heads + 1, dtype=jnp.float32) / n_heads)

def split_heads(t, n_heads):
    b, s, _ = t.shape
    return t.reshape(b, s, n_heads, HEAD_DIM).transpose(0, 2, 1, 3)

def merge_heads(t):
    b, h, s, d = t.shape
    return t.transpose(0, 2, 1, 3).reshape(b, s, h * d)

def causal_depthwise_conv(x, w, bias):
    c = x.shape[-1]
    y = lax.conv_general_dilated(
        x, w[:, None, :].astype(x.dtype), window_strides=(1,), padding=[(CONV_W - 1, 0)],
        dimension_numbers=("NWC", "WIO", "NWC"), feature_group_count=c)
    return y + bias.astype(x.dtype)

def rg_lru(xb, a_w, a_b, x_w, x_b, lam):
    b, s, c = xb.shape
    xf = xb.astype(jnp.float32)
    xblk = xf.reshape(b, s, LRU_BLOCKS, LRU_BLOCK_W)
    r = jax.nn.sigmoid(jnp.einsum("bsnc,ncd->bsnd", xblk, a_w.astype(jnp.float32)) + a_b.astype(jnp.float32)).reshape(b, s, c)
    i = jax.nn.sigmoid(jnp.einsum("bsnc,ncd->bsnd", xblk, x_w.astype(jnp.float32)) + x_b.astype(jnp.float32)).reshape(b, s, c)
    log_a = -LRU_C * r * jax.nn.softplus(-lam.astype(jnp.float32))
    a = jnp.exp(log_a)
    mult = jnp.sqrt(-jnp.expm1(2.0 * log_a))
    mult = jnp.where(jnp.arange(s)[None, :, None] == 0, 1.0, mult)
    bt = mult * i * xf

    def combine(left, right):
        a1, b1 = left
        a2, b2 = right
        return a1 * a2, a2 * b1 + b2

    _, h = lax.associative_scan(combine, (a, bt), axis=1)
    return h

def moba_attention(q, k, v):
    b, h, s, hd = q.shape
    n_blk = -(-s // MOBA_BLOCK)
    s_pad = n_blk * MOBA_BLOCK
    pad = s_pad - s
    if pad:
        widths = ((0, 0), (0, 0), (0, pad), (0, 0))
        q, k, v = jnp.pad(q, widths), jnp.pad(k, widths), jnp.pad(v, widths)
    kb = k.reshape(b, h, n_blk, MOBA_BLOCK, hd)
    vb = v.reshape(b, h, n_blk, MOBA_BLOCK, hd)
    k_mean = jnp.mean(kb.astype(jnp.float32), axis=3)
    gate = jnp.einsum("bhsd,bhnd->bhsn", q.astype(jnp.float32), k_mean)
    q_blk = jnp.arange(s_pad) // MOBA_BLOCK
    fully_past = jnp.arange(n_blk)[None, :] < q_blk[:, None]
    gate = jnp.where(fully_past, gate, -jnp.inf)
    n_sel = min(MOBA_TOPK, n_blk)
    gate_top, sel = lax.top_k(gate, n_sel)
    sel_ok = gate_top > -jnp.inf
    slopes = alibi_slopes(h)
    scale = hd ** -0.5
    offs = jnp.arange(MOBA_BLOCK)
    gather_blocks = jax.vmap(jax.vmap(lambda blocks, idx: blocks[idx]))

    def chunk(c):
        start = c * Q_CHUNK
        qc = lax.dynamic_slice_in_dim(q, start, Q_CHUNK, axis=2)
        selc = lax.dynamic_slice_in_dim(sel, start, Q_CHUNK, axis=2)
        okc = lax.dynamic_slice_in_dim(sel_ok, start, Q_CHUNK, axis=2)
        own = start // MOBA_BLOCK
        k_own = lax.dynamic_index_in_dim(kb, own, axis=2, keepdims=False)
        v_own = lax.dynamic_index_in_dim(vb, own, axis=2, keepdims=False)
        k_sel = gather_blocks(kb, selc)
        v_sel = gather_blocks(vb, selc)
        t_q = start + jnp.arange(Q_CHUNK)
        s_own = jnp.einsum("bhqd,bhkd->bhqk", qc, k_own).astype(jnp.float32) * scale
        d_own = t_q[:, None] - (own * MOBA_BLOCK + offs)[None, :]
        s_own = jnp.where(d_own >= 0, s_own - slopes[:, None, None] * d_own.astype(jnp.float32), -jnp.inf)
        s_sel = jnp.einsum("bhqd,bhqjkd->bhqjk", qc, k_sel).astype(jnp.float32) * scale
        d_sel = t_q[None, None, :, None, None] - (selc[..., None] * MOBA_BLOCK + offs)
        s_sel = jnp.where(okc[..., None], s_sel - slopes[None, :, None, None, None] * d_sel.astype(jnp.float32), -jnp.inf)
        scores = jnp.concatenate([s_sel.reshape(b, h, Q_CHUNK, n_sel * MOBA_BLOCK), s_own], axis=-1)
        p = jax.nn.softmax(scores, axis=-1)
        p_sel = p[..., :n_sel * MOBA_BLOCK].reshape(b, h, Q_CHUNK, n_sel, MOBA_BLOCK).astype(v.dtype)
        p_own = p[..., n_sel * MOBA_BLOCK:].astype(v.dtype)
        return (jnp.einsum("bhqjk,bhqjkd->bhqd", p_sel, v_sel)
                + jnp.einsum("bhqk,bhkd->bhqd", p_own, v_own))

    out = lax.map(chunk, jnp.arange(s_pad // Q_CHUNK))
    out = out.transpose(1, 2, 0, 3, 4).reshape(b, h, s_pad, hd)
    return out[:, :, :s]

def memory_attention(q, k, v):
    scores = jnp.einsum("bhsd,bhmd->bhsm", q, k).astype(jnp.float32) * (HEAD_DIM ** -0.5)
    p = jax.nn.softmax(scores, axis=-1)
    return jnp.einsum("bhsm,bhmd->bhsd", p.astype(v.dtype), v)

def second_inputs(seed: int = 0) -> dict:
    key = jax.random.key(seed)
    ks = jax.random.split(key, 24)

    def normal(k, shape, scale):
        return jax.random.normal(k, shape, jnp.float32) * scale

    def gain(k, n):
        return 1.0 + 0.02 * jax.random.normal(k, (DEPTH_2, n), jnp.float32)

    u = jax.random.uniform(ks[12], (DEPTH_2, LRU_WIDTH), jnp.float32, minval=0.9, maxval=0.999)
    a0 = u ** (1.0 / LRU_C)
    lam = jnp.log(a0) - jnp.log1p(-a0)
    return {
        "x": normal(ks[0], (BATCH, SEQ, D_MODEL), 1.0),
        "mem": normal(ks[1], (BATCH, MEM_LEN, D_MODEL), 1.0),
        "ffn1_norm": gain(ks[2], D_MODEL),
        "ffn1_w_in": normal(ks[3], (DEPTH_2, D_MODEL, 2 * D_FF_2), D_MODEL ** -0.5),
        "ffn1_w_out": normal(ks[4], (DEPTH_2, D_FF_2, D_MODEL), D_FF_2 ** -0.5),
        "mix_norm": gain(ks[5], D_MODEL),
        "mem_norm": gain(ks[6], D_MODEL),
        "w_in": normal(ks[7], (DEPTH_2, D_MODEL, IN_WIDTH), D_MODEL ** -0.5),
        "lru_conv_w": normal(ks[8], (DEPTH_2, CONV_W, LRU_WIDTH), CONV_W ** -0.5),
        "lru_conv_b": normal(ks[9], (DEPTH_2, LRU_WIDTH), 0.01),
        "lru_a_w": normal(ks[10], (DEPTH_2, LRU_BLOCKS, LRU_BLOCK_W, LRU_BLOCK_W), LRU_BLOCK_W ** -0.5),
        "lru_a_b": normal(ks[11], (DEPTH_2, LRU_BLOCKS, LRU_BLOCK_W), 0.01),
        "lru_x_w": normal(ks[13], (DEPTH_2, LRU_BLOCKS, LRU_BLOCK_W, LRU_BLOCK_W), LRU_BLOCK_W ** -0.5),
        "lru_x_b": normal(ks[14], (DEPTH_2, LRU_BLOCKS, LRU_BLOCK_W), 0.01),
        "lru_lambda": lam,
        "moba_q_norm": gain(ks[15], HEAD_DIM),
        "moba_k_norm": gain(ks[16], HEAD_DIM),
        "mem_w_kv": normal(ks[17], (DEPTH_2, D_MODEL, 2 * MEM_WIDTH), D_MODEL ** -0.5),
        "mem_q_norm": gain(ks[18], HEAD_DIM),
        "mem_k_norm": gain(ks[19], HEAD_DIM),
        "w_out": normal(ks[20], (DEPTH_2, MIX_WIDTH_2, D_MODEL), MIX_WIDTH_2 ** -0.5),
        "ffn2_norm": gain(ks[21], D_MODEL),
        "ffn2_w_in": normal(ks[22], (DEPTH_2, D_MODEL, 2 * D_FF_2), D_MODEL ** -0.5),
        "ffn2_w_out": normal(ks[23], (DEPTH_2, D_FF_2, D_MODEL), D_FF_2 ** -0.5),
    }

def second_block(x, mem, ffn1_norm, ffn1_w_in, ffn1_w_out, mix_norm, mem_norm, w_in,
              lru_conv_w, lru_conv_b, lru_a_w, lru_a_b, lru_x_w, lru_x_b, lru_lambda,
              moba_q_norm, moba_k_norm, mem_w_kv, mem_q_norm, mem_k_norm, w_out,
              ffn2_norm, ffn2_w_in, ffn2_w_out):
    split_at = np.cumsum([LRU_WIDTH, LRU_WIDTH, MOBA_WIDTH, MOBA_WIDTH, MOBA_WIDTH])
    for l in range(DEPTH_2):
        x = x + 0.5 * swiglu_2(rms_norm_2(x, ffn1_norm[l]), ffn1_w_in[l], ffn1_w_out[l])

        u = rms_norm_2(x, mix_norm[l]) @ w_in[l]
        lru_x, lru_g, mq, mk, mv, cq = jnp.split(u, split_at, axis=-1)

        xb = causal_depthwise_conv(lru_x, lru_conv_w[l], lru_conv_b[l])
        h_lru = rg_lru(xb, lru_a_w[l], lru_a_b[l], lru_x_w[l], lru_x_b[l], lru_lambda[l])
        y_lru = (h_lru * jax.nn.gelu(lru_g.astype(jnp.float32))).astype(x.dtype)

        q = rms_norm_2(split_heads(mq, MOBA_HEADS), moba_q_norm[l])
        k = rms_norm_2(split_heads(mk, MOBA_HEADS), moba_k_norm[l])
        v = split_heads(mv, MOBA_HEADS)
        y_moba = merge_heads(moba_attention(q, k, v))

        mkv = rms_norm_2(mem, mem_norm[l]) @ mem_w_kv[l]
        mem_k, mem_v = jnp.split(mkv, 2, axis=-1)
        qc = rms_norm_2(split_heads(cq, MEM_HEADS), mem_q_norm[l])
        kc = rms_norm_2(split_heads(mem_k, MEM_HEADS), mem_k_norm[l])
        y_mem = merge_heads(memory_attention(qc, kc, split_heads(mem_v, MEM_HEADS)))

        mixed = jnp.concatenate([y_lru, y_moba.astype(x.dtype), y_mem.astype(x.dtype)], axis=-1)
        x = x + mixed @ w_out[l]

        x = x + 0.5 * swiglu_2(rms_norm_2(x, ffn2_norm[l]), ffn2_w_in[l], ffn2_w_out[l])
    return x


def setup_inputs(seed=0):
    out = dict(first_inputs(seed))
    for name, value in second_inputs(seed + 1).items():
        if name != "x":
            out[name + "_2"] = value
    return out


def reference(
    x, c, positions, ada_w, ada_b, norm_ffn1, ffn1_w_in, ffn1_w_out, norm_mix, mix_w_in, sgu_w,
    sgu_b, mix_w_out, norm_ffn2, ffn2_w_in, ffn2_w_out, final_norm, mem_2, ffn1_norm_2,
    ffn1_w_in_2, ffn1_w_out_2, mix_norm_2, mem_norm_2, w_in_2, lru_conv_w_2, lru_conv_b_2,
    lru_a_w_2, lru_a_b_2, lru_x_w_2, lru_x_b_2, lru_lambda_2, moba_q_norm_2, moba_k_norm_2,
    mem_w_kv_2, mem_q_norm_2, mem_k_norm_2, w_out_2, ffn2_norm_2, ffn2_w_in_2, ffn2_w_out_2,
):
    x = first_block(
        x, c, positions, ada_w, ada_b, norm_ffn1, ffn1_w_in, ffn1_w_out, norm_mix, mix_w_in,
        sgu_w, sgu_b, mix_w_out, norm_ffn2, ffn2_w_in, ffn2_w_out, final_norm,
    )
    return second_block(
        x, mem_2, ffn1_norm_2, ffn1_w_in_2, ffn1_w_out_2, mix_norm_2, mem_norm_2, w_in_2,
        lru_conv_w_2, lru_conv_b_2, lru_a_w_2, lru_a_b_2, lru_x_w_2, lru_x_b_2, lru_lambda_2,
        moba_q_norm_2, moba_k_norm_2, mem_w_kv_2, mem_q_norm_2, mem_k_norm_2, w_out_2,
        ffn2_norm_2, ffn2_w_in_2, ffn2_w_out_2,
    )


_drawn_inputs = setup_inputs


def setup_inputs(seed=0):
    import zlib

    import numpy as np

    out = dict(_drawn_inputs(seed))
    spreads = {}
    factors = {'ada_b': 2.798,
     'norm_ffn1': 8.0,
     'norm_mix': 5.538,
     'sgu_b': 8.0,
     'norm_ffn2': 8.0,
     'ffn1_norm_2': 6.474,
     'mix_norm_2': 4.797,
     'mem_norm_2': 8.0,
     'lru_conv_b_2': 10.167,
     'lru_a_b_2': 64.0,
     'lru_x_b_2': 45.988,
     'moba_q_norm_2': 27.766,
     'moba_k_norm_2': 24.904,
     'mem_q_norm_2': 8.0,
     'mem_k_norm_2': 8.0,
     'ffn2_norm_2': 21.596}
    for name, (base, spread) in spreads.items():
        noise = np.random.default_rng([zlib.crc32(name.encode()), seed]).standard_normal(out[name].shape)
        drawn = base * np.exp(spread * noise) if base else spread * noise
        out[name] = __import__('jax').numpy.asarray(drawn.astype(out[name].dtype))
    for name, factor in factors.items():
        out[name] = (out[name] * factor).astype(out[name].dtype)
    return out
```

```python
import numpy as np

import concourse.bass as bass
from concourse import mybir
from concourse.alu_op_type import AluOpType as ALU

F32 = mybir.dt.float32
F32R = mybir.dt.float32r
I32 = mybir.dt.int32
ACT = mybir.ActivationFunctionType
AX = mybir.AxisListType

P = 128
D = 1024
T = 512
TT = T // P
KD = D // P
DFF = 2816
LAYERS = 2
COLS = 256
FT = DFF // P
FT_A = 12
FT_B = FT - FT_A
UNIT = KD * COLS
UNIT_A = FT_A * COLS
UNIT_B = FT_B * COLS
IN_UNITS = 2 * DFF // COLS
IN_A = 2 * FT_A // 2
IN_B = 2 * FT_B // 2
OUT_UNITS = D // COLS
FFN_UNITS = IN_UNITS + 2 * OUT_UNITS
N_MOD = 9
HD = 64
HEADS = 8
IDX_HEADS = 4
TOPK = T // 4
EPS = 1e-6
MOD_SLOTS = 2

MIX1_PROJ = 12
MIX2_PROJ = 8
MEM_UNITS = 2

L_FFN1 = 0
L_MIX = L_FFN1 + FFN_UNITS
L_FFN2 = L_MIX + MIX1_PROJ + OUT_UNITS
S_MEM = 0
S_FFN1 = S_MEM + MEM_UNITS
S_MIX = S_FFN1 + FFN_UNITS
S_FFN2 = S_MIX + MIX2_PROJ + OUT_UNITS

NEG = -1.0e30
BELOW = -3.0e38
TAKEN = -3.4e38
BIG = 3.0e38
MAGIC = 12582912.0
TWO_PI_PARTS = (6.28125, 0.001934051513671875, 1.2556659e-06)

C_IDENT, C_PERM, C_TRI, C_SEL, C_FREQ = 0, P, 2 * P, 3 * P, 3 * P + 2
C_WIDTH = 3 * P + 3
ALIBI_AT = [0, 128, 384, 768]
MASKS = 1280
V_FINAL, V_MEM, V_FFN1, V_MIX, V_FFN2 = 0, 8, 16, 24, 32
V_CONVW, V_CONVB, V_AB, V_XB, V_LAM, V_GAINS, V_WIDTH = 40, 56, 60, 64, 68, 72, 76


class Memory:
    pass


class Signals:
    pass


def memory(nc):
    m = Memory()
    base = -(-nc.sbuf_base // 32) * 32
    K = 1024

    def at(name, offset, shape, dt=F32):
        return nc.alloc_sbuf_tensor_at("m_" + name, [P] + shape, dt, offset=base + offset)

    m.x = at("x", 0, [KD, T])
    m.hH = at("hH", 16 * K, [KD, T], F32R)
    m.hL = at("hL", 32 * K, [KD, T], F32R)
    m.guH = at("guH", 48 * K, [FT_A, T], F32R)
    m.guL = at("guL", 72 * K, [FT_A, T], F32R)
    m.wraw = at("wraw", 96 * K, [2, UNIT_A])
    m.wH = at("wH", 120 * K, [2, UNIT_A], F32R)
    m.wL = at("wL", 144 * K, [2, UNIT_A], F32R)
    m.mod_big = at("mod_big", 48 * K, [3, 4, D])
    m.u = at("u", 56 * K, [4, T])
    m.va = at("va", 80 * K, [TT, T])
    m.lx = at("lx", 56 * K, [4, T])
    m.gl = at("gl", 80 * K, [4, T])
    m.xb = at("xb", 72 * K, [4, T])
    m.q = at("q", 64 * K, [4, T])
    m.k = at("k", 88 * K, [4, T])
    m.cq = at("cq", 88 * K, [2, T])
    m.gatew = at("gatew", 92 * K, [2, 4, P])
    m.mem = at("mem", 72 * K, [KD, 256])
    m.sm = at("sm", 16 * K, [3, T])
    m.p = at("p", 22 * K, [3, T])
    m.pT = at("pT", 28 * K, [3, T])
    m.bn = at("bn", 34 * K, [2, T])
    m.hs = at("hs", 38 * K, [2, T])
    m.rx = at("rx", 42 * K, [2, T])
    m.mdh = at("mdh", 38 * K, [2, T])
    m.mn = at("mn", 46 * K, [32])
    m.sums = at("sums", 46 * K + 128, [32])
    m.rinv = at("rinv", 46 * K + 256, [32])
    m.hv = at("hv", 46 * K + 384, [56])
    m.hr = at("hr", 46 * K + 640, [56])
    m.ht = at("ht", 46 * K + 896, [56])
    o = 168 * K
    m.masks = at("masks", o, [MASKS]); o += 5 * K
    g = o
    m.sg = at("sg", g, [2, T])
    m.gut = at("gut", g + 4 * K, [2, T])
    m.t = at("t", g, [2, T])
    m.hf = at("hf", g + 4 * K, [2, T])
    m.sq = at("sq", g + 8 * K, [2, T])
    m.acc = at("acc", g + 12 * K, [T])
    m.diag = at("diag", g + 4 * K, [TT, P])
    m.qi = at("qi", g, [2, T])
    m.ki = at("ki", g + 4 * K, [T])
    m.rl = at("rl", g + 6 * K, [2, T])
    m.ra = at("ra", g + 10 * K, [T])
    m.rb = at("rb", g + 12 * K, [T])
    m.rg = at("rg", g, [4, T])
    m.ig3 = at("ig3", g + 8 * K, [3, T])
    m.pos = at("pos", g, [T], I32)
    m.ang = at("ang", g + 2 * K, [T])
    m.turn = at("turn", g + 4 * K, [T])
    o += 14 * K
    a = o
    m.mod_w = at("mod_w", a, [MOD_SLOTS, D])
    m.mod_acc = at("mod_acc", a + 8 * K, [D])
    m.v = at("v", a, [TT, T])
    m.sguT = at("sguT", a + 8 * K, [4, P])
    m.sgub = at("sgub", a + 10 * K, [4, P])
    m.memk = at("memk", a, [2, 256])
    m.memv = at("memv", a + 2 * K, [2, 256])
    m.mv = at("mv", a + 4 * K, [TT, 256])
    m.la = at("la", a + 8 * K, [T])
    m.lb = at("lb", a + 10 * K, [T])
    o += 12 * K
    m.cos = at("cos", o, [T])
    m.sin = at("sin", o + 2 * K, [T])
    m.none = at("none", o + 2 * K, [256])
    m.ig1 = at("ig1", o, [1, T])
    o += 4 * K
    def small(name, shape):
        nonlocal o
        here, o = o, o + -(-int(np.prod(shape)) * 4 // 32) * 32
        return at(name, here, shape)

    m.vec = at("vec", o, [V_WIDTH])
    m.mod = small("mod", [N_MOD * KD])
    m.mod_b = small("mod_b", [N_MOD * KD])
    m.cst = small("cst", [C_WIDTH])
    m.ones = small("ones", [P])
    m.gains = small("gains", [3 * KD])
    m.A = small("A", [KD])
    m.gate = small("gate", [KD])
    m.csil = small("csil", [KD])
    m.zero = small("zero", [1])
    m.halfpi = small("halfpi", [1])
    m.wi = small("wi", [4 * TT])
    m.m8 = small("m8", [8])
    m.nv = small("nv", [TT])
    m.nr = small("nr", [TT])
    m.nt = small("nt", [TT])
    m.sp = small("sp", [6, 4])
    assert base + o <= nc.sbuf_usable_end, (base + o, nc.sbuf_usable_end)
    m.ident = m.cst[:, C_IDENT:C_IDENT + P]
    m.perm = m.cst[:, C_PERM:C_PERM + P]
    m.tri = m.cst[:, C_TRI:C_TRI + P]
    m.sel = m.cst[:, C_SEL:C_SEL + 2]
    m.freq = m.cst[:, C_FREQ:C_FREQ + 1]
    m.one = m.ones[:, 0:1]
    m.bank = [nc.alloc_psum_tensor(f"bank{i}", [P, 512], F32) for i in range(8)]
    return m


def f(ap):
    return ap.bitcast(F32)



def sp_units(sp, m, s, src, u0, n, size):
    with sp.Fori(0, n // 2) as i:
        for j in range(2):
            sp.wait_ge(s.low, u0 + 2 * i + j + 1)
            sp.dma_start(m.wraw[:, j, 0:size], src(2 * i + j)).then_inc(s.full[j], 16)


def sp_unit(sp, m, s, src, u, size):
    sp.wait_ge(s.low, u + 1)
    sp.dma_start(m.wraw[:, u % 2, 0:size], src).then_inc(s.full[u % 2], 16)


def pool_low(pool, nc, m, s, u0, n, size):
    with pool.Fori(0, n // 2) as i:
        for j in range(2):
            pool.wait_ge(s.high, u0 + 2 * i + j + 1)
            nc.gpsimd.tensor_tensor(m.wL[:, j, 0:size], m.wraw[:, j, 0:size], f(m.wH[:, j, 0:size]), ALU.subtract)\
                .then_inc(s.low, 1)


def act_high(act, nc, m, s, u, j, pair, size):
    act.wait_ge(s.full[j], 16 * (pair + 1))
    act.wait_ge(s.mm, 2 * u + 2)
    nc.scalar.activation(m.wH[:, j, 0:size], m.wraw[:, j, 0:size], ACT.Copy).then_inc(s.high, 1)


def act_next(act, nc, m, s, u, size):
    if size:
        act_high(act, nc, m, s, u + 2, u % 2, (u + 2) // 2, size)


def pe_3(nc, out, a, b, first, last):
    nc.tensor.matmul(out, a[0], b[0], start=first, stop=False)
    nc.tensor.matmul(out, a[0], b[1], start=False, stop=False)
    return nc.tensor.matmul(out, a[1], b[0], start=False, stop=last)


def pe_tiles(pe, nc, m, s, u, slot, banks, right, rows, waits=None):
    pe.wait_ge(s.low, u + 3)
    for k in range(rows):
        if waits:
            waits(k)
        for j in range(2):
            at = k * COLS + j * P
            w = m.wH[:, slot, at:at + P], m.wL[:, slot, at:at + P]
            mm = pe_3(nc, banks[j], w, right(k), k == 0, k == rows - 1)
            if k == rows - 1:
                mm.then_inc(s.mm, 1)


def pe_rows(pe, nc, m, s, u, left, outs):
    pe.wait_ge(s.low, u + 3)
    for tt, out in enumerate(outs):
        for k in range(KD):
            hi, lo = left(k)
            w = [x[:, u % 2, k * COLS:(k + 1) * COLS] for x in (m.wH, m.wL)]
            mm = pe_3(nc, out, (hi[:, tt * P:(tt + 1) * P], lo[:, tt * P:(tt + 1) * P]), w, k == 0, k == KD - 1)
        if tt % (len(outs) // 2) == len(outs) // 2 - 1:
            mm.then_inc(s.mm, 1)



class Norm:

    def __init__(self, n, a, y0=None, tokens=T, src=None):
        self.n, self.a, self.y0, self.tokens, self.src = n, a, y0, tokens, src or (lambda m: m.x)

    def act_square(self, act, nc, m, s, d):
        n = self.n
        if self.y0 is not None:
            act.wait_ge(s.y, 4 + self.y0 + d + 1)
        if d >= 3:
            act.wait_ge(s.acc, 7 * n + d - 2)
        x = self.src(m)[:, d]
        out = m.acc[:, 0:self.tokens] if d == 0 else m.sq[:, d % 2, 0:self.tokens]
        nc.scalar.activation(out, x, ACT.Square).then_inc(s.sq, 1)

    def dve_add(self, dve, nc, m, s, d):
        if d == 0:
            return
        dve.wait_ge(s.sq, 8 * self.n + d + 1)
        dve.drain()
        w = self.tokens
        nc.vector.tensor_tensor(m.acc[:, 0:w], m.acc[:, 0:w], m.sq[:, d % 2, 0:w], ALU.add).then_inc(s.acc, 1)

    def pe_sum(self, pe, nc, m, s):
        pe.wait_ge(s.acc, 7 * self.n + 7)
        for tt in range(self.tokens // P):
            mm = nc.tensor.matmul(m.bank[6][:, tt:tt + 1], m.acc[:, tt * P:(tt + 1) * P], m.one, start=True, stop=True)
        mm.then_inc(s.ss, 1)

    def dve_rsqrt(self, dve, nc, m, s):
        v, r, t = m.nv[:, 0:self.tokens // P], m.nr[:, 0:self.tokens // P], m.nt[:, 0:self.tokens // P]
        dve.wait_ge(s.ss, self.n + 1)
        dve.drain()
        nc.vector.tensor_scalar(v, m.bank[6][:, 0:self.tokens // P], 1.0 / D, EPS, ALU.mult, ALU.add).then_inc(s.var, 1)
        newton(dve, nc, s.rt, self.n + 1, v, r, t)
        tt = self.tokens // P
        nc.vector.tensor_tensor(m.diag[:, 0:tt], m.ident.unsqueeze(1).to_broadcast([P, tt, P]),
                                r.unsqueeze(2).to_broadcast([P, tt, P]), ALU.mult).then_inc(s.dg, 1)

    def act_sqrt(self, act, nc, m, s):
        tt = self.tokens // P
        act.wait_ge(s.var, self.n + 1)
        nc.scalar.activation(m.nr[:, 0:tt], m.nv[:, 0:tt], ACT.Sqrt).then_inc(s.rt, 1)

    def pe_spread(self, pe, nc, m, s):
        tt = self.tokens // P
        pe.wait_ge(s.dg, self.n + 1)
        nc.tensor.matmul(m.bank[7][:, 0:self.tokens], m.ones[:], m.diag[:, 0:tt].rearrange("p a b -> p (a b)"),
                         start=True, stop=True).then_inc(s.spread, 1)

    def dve_scale(self, dve, nc, m, s, k):
        if k == 0:
            dve.wait_ge(s.spread, self.n + 1)
        if k >= 2:
            dve.wait_ge(s.hh, 16 * self.a + 2 * (k - 2) + 2)
        w = self.tokens
        nc.vector.tensor_tensor(m.t[:, k % 2, 0:w], self.src(m)[:, k], m.bank[7][:, 0:w], ALU.mult)\
            .then_inc(s.tt, 1)

    def dve_low(self, dve, nc, m, s, k, hL, hH):
        dve.wait_ge(s.hh, 16 * self.a + 2 * k + 2)
        nc.vector.tensor_tensor(hL, m.hf[:, k % 2, 0:self.tokens], f(hH), ALU.subtract).then_inc(s.hl, 1)

    def dve_apply(self, dve, nc, m, s, hH, hL):
        self.dve_scale(dve, nc, m, s, 0)
        self.dve_scale(dve, nc, m, s, 1)
        for k in range(KD):
            self.dve_low(dve, nc, m, s, k, hL(k), hH(k))
            if k + 2 < KD:
                self.dve_scale(dve, nc, m, s, k + 2)

    def act_apply(self, act, nc, m, s, hH, scale, bias):
        w = self.tokens
        for k in range(KD):
            act.wait_ge(s.tt, 8 * self.a + k + 1)
            if k >= 2:
                act.wait_ge(s.hl, 8 * self.a + k - 1)
            nc.scalar.activation(m.hf[:, k % 2, 0:w], m.t[:, k % 2, 0:w], ACT.Identity, scale=scale(k), bias=bias(k))\
                .then_inc(s.hh, 1)
            nc.scalar.activation(hH(k), m.t[:, k % 2, 0:w], ACT.Identity, scale=scale(k), bias=bias(k))\
                .then_inc(s.hh, 1)


def newton(dve, nc, roots, count, v, r, t):
    dve.wait_ge(roots, count)
    nc.vector.reciprocal(r, r)
    dve.drain()
    nc.vector.tensor_tensor(t, r, r, ALU.mult)
    dve.drain()
    nc.vector.tensor_tensor(t, t, v, ALU.mult)
    dve.drain()
    nc.vector.tensor_scalar(t, t, -0.5, 1.5, ALU.mult, ALU.add)
    dve.drain()
    nc.vector.tensor_tensor(r, r, t, ALU.mult)
    dve.drain()



class Ffn:

    def __init__(self, n, u0, y0, norm, after, ahead):
        self.n, self.u0, self.y0, self.norm, self.after, self.ahead = n, u0, y0, norm, after, ahead
        self.ua, self.ub = u0 + IN_A, u0 + IN_A + OUT_UNITS
        self.uc = self.ub + IN_B
        self.f0 = FT * n

    def pe_group(self, pe, nc, m, s, u, f, waits=None):
        h = lambda k: (m.hH[:, k], m.hL[:, k])
        pe.wait_ge(s.silu, f + 2)
        pe_tiles(pe, nc, m, s, u, 0, [m.bank[0][:], m.bank[1][:]], h, KD, waits)
        pe.wait_ge(s.ufree, f + 2)
        pe_tiles(pe, nc, m, s, u + 1, 1, [m.bank[2][:], m.bank[3][:]], h, KD)

    def pe_out(self, pe, nc, m, s, u, rows, g0, y):
        gu = lambda k: (m.guH[:, k], m.guL[:, k])

        def waits(k):
            if k in (0, rows - 2):
                pe.wait_ge(s.gu, g0 + (rows - 2 if k == 0 else rows))
        with pe.Fori(0, OUT_UNITS // 2) as i:
            for q in range(2):
                pe.wait_ge(s.y, y + 4 * i + 2 * q + 2)
                pe_tiles(pe, nc, m, s, u + 2 * i + q, q, [m.bank[4 + 2 * q][:], m.bank[5 + 2 * q][:]], gu, rows, waits)

    def pe(self, pe, nc, m, s, modulation=None):
        a = self.norm.a
        first = lambda k: pe.wait_ge(s.hl, 8 * a + k + 1)
        self.pe_group(pe, nc, m, s, self.u0, self.f0, first)
        if modulation:
            modulation.pe_reduce(pe, nc, m, s, 2)
        with pe.Fori(1, IN_A // 2) as i:
            self.pe_group(pe, nc, m, s, self.u0 + 2 * i, self.f0 + 2 * i)
            if modulation:
                modulation.pe_reduce(pe, nc, m, s, 2 + i)
        if modulation:
            pe.wait_ge(s.mod_taken, 8)
        self.pe_out(pe, nc, m, s, self.ua, FT_A, self.f0, self.y0)
        if modulation:
            pe.wait_ge(s.y, 4 + self.y0 + KD)
            modulation.pe_reduce(pe, nc, m, s, 8)
        with pe.Fori(0, IN_B // 2) as i:
            self.pe_group(pe, nc, m, s, self.ub + 2 * i, self.f0 + FT_A + 2 * i)
        self.pe_out(pe, nc, m, s, self.uc, FT_B, self.f0 + FT_A, self.y0 + KD)

    def act_group(self, act, nc, m, s, u, pair, f, size):
        act_high(act, nc, m, s, u + 2, 0, pair + 1, size)
        for j in range(2):
            act.wait_ge(s.mm, 4 + 2 * u + j + 1)
            act.wait_ge(s.ufree, f + j + 1)
            nc.scalar.activation(m.sg[:, j], m.bank[j][:], ACT.Silu).then_inc(s.silu, 1)
        act_high(act, nc, m, s, u + 3, 1, pair + 1, size)

    def act(self, act, nc, m, s):
        for u, n, f, after in ((self.u0, IN_A, self.f0, UNIT_A), (self.ub, IN_B, self.f0 + FT_A, UNIT_B)):
            with act.Fori(0, n // 2 - 1) as i:
                self.act_group(act, nc, m, s, u + 2 * i, u // 2 + i, f + 2 * i, UNIT)
            last = n - 2
            self.act_group(act, nc, m, s, u + last, (u + last) // 2, f + last, after)
            out = u + n
            for q in range(OUT_UNITS):
                size = after if q < OUT_UNITS - 2 else (UNIT if after == UNIT_A else self.ahead)
                act_next(act, nc, m, s, out + q, size)
                if after == UNIT_B and self.after:
                    self.after.act_square(act, nc, m, s, 2 * q)
                    self.after.act_square(act, nc, m, s, 2 * q + 1)

    def dve_group(self, dve, nc, m, s, u, f0, tile):
        dve.drain()
        for j in range(2):
            dve.wait_ge(s.silu, 2 + f0 + j + 1)
            dve.wait_ge(s.mm, 4 + 2 * u + 2 + j + 1)
            nc.vector.tensor_tensor(m.gut[:, j], m.sg[:, j], m.bank[2 + j][:], ALU.mult).then_inc(s.ufree, 1)
        dve.drain()
        for j in range(2):
            nc.vector.tensor_copy(m.guH[:, tile + j], m.gut[:, j])
        dve.drain()
        for j in range(2):
            nc.vector.tensor_tensor(m.guL[:, tile + j], m.gut[:, j], f(m.guH[:, tile + j]), ALU.subtract).then_inc(s.gu, 1)

    def dve(self, dve, nc, m, s, gate, modulation=None):
        with dve.Fori(0, IN_A // 2) as i:
            if modulation:
                modulation.dve_chunk(dve, nc, m, s, i)
            self.dve_group(dve, nc, m, s, self.u0 + 2 * i, self.f0 + 2 * i, 2 * i)
            if modulation:
                modulation.dve_take(dve, nc, m, s, 2 + i)
        if modulation:
            modulation.dve_chunk(dve, nc, m, s, IN_A // 2)
            dve_half_gate(dve, nc, m, 2)
        dve_update(dve, nc, m, s, self.ua, gate)
        if modulation:
            modulation.dve_take(dve, nc, m, s, 8)
        with dve.Fori(0, IN_B // 2) as i:
            self.dve_group(dve, nc, m, s, self.ub + 2 * i, self.f0 + FT_A + 2 * i, 2 * i)
        dve_update(dve, nc, m, s, self.uc, gate, self.after)


def dve_half_gate(dve, nc, m, chunk):
    dve.drain()
    nc.vector.tensor_scalar(m.gate[:], m.mod[:, chunk * KD:(chunk + 1) * KD], 0.5, None, ALU.mult)
    dve.drain()


def dve_update(dve, nc, m, s, u, gate, after=None):
    dve.drain()
    for d in range(KD):
        dve.wait_ge(s.mm, 4 + 2 * u + d + 1)
        nc.vector.scalar_tensor_tensor(out=m.x[:, d], in0=m.bank[4 + d % 4][:], scalar=gate(d), in1=m.x[:, d],
                                       op0=ALU.mult, op1=ALU.add).then_inc(s.y, 1)
        if after and d % 2:
            after.dve_add(dve, nc, m, s, d - 1)
            after.dve_add(dve, nc, m, s, d)



class Modulation:

    def sp_big(self, sp, m, s, w, q):
        if q == 3:
            sp.wait_ge(s.big_used, 1)
        sp.dma_start(m.mod_big[:, q % 3], w[q // 2, 4 * (q % 2):4 * (q % 2) + 4].rearrange("k p n -> p k n"))\
            .then_inc(s.big[q % 3], 16)

    def sp_chunk(self, sp, m, s, w, i):
        for k in range(KD):
            sp.wait_ge(s.mod_used, KD * i + k + 1)
            sp.dma_start(m.mod_w[:, k % 2], w[2 + i, k]).then_inc(s.mod_full[k % 2], 16)

    def dve_big(self, dve, nc, m, s):
        for c in range(2):
            for q in range(2):
                n = 2 * c + q
                for k in range(4):
                    dve.drain()
                    if k == 0:
                        dve.wait_ge(s.big[n % 3], 16 * (n // 3 + 1))
                    last = self.add(dve, nc, m, m.mod_big[:, n % 3, k], 4 * q + k)
                last.then_inc(s.big_used, 1)
            self.dve_take(dve, nc, m, s, c)

    def add(self, dve, nc, m, w, k):
        if k == 0:
            return nc.vector.tensor_scalar(m.mod_acc[:], w, m.csil[:, 0:1], None, ALU.mult)
        return nc.vector.scalar_tensor_tensor(out=m.mod_acc[:], in0=w, scalar=m.csil[:, k:k + 1], in1=m.mod_acc[:],
                                              op0=ALU.mult, op1=ALU.add)

    def dve_chunk(self, dve, nc, m, s, i):
        for k in range(KD):
            dve.drain()
            dve.wait_ge(s.mod_full[k % 2], 16 * (4 * i + k // 2 + 1))
            self.add(dve, nc, m, m.mod_w[:, k % 2], k).then_inc(s.mod_used, 1)

    def pe_reduce(self, pe, nc, m, s, c):
        if isinstance(c, int) and c < 2:
            pe.wait_ge(s.big_used, 2 * c + 2)
        else:
            pe.wait_ge(s.mod_used, KD * (c - 1) + 2)
        for j in range(KD):
            mm = nc.tensor.matmul(m.bank[6][:, 8 + j:9 + j], m.mod_acc[:, j * P:(j + 1) * P], m.one, start=True, stop=True)
        mm.then_inc(s.mod_mm, 1)

    def dve_take(self, dve, nc, m, s, c):
        dve.wait_ge(s.mod_mm, c + 1)
        at = c * KD
        nc.vector.tensor_tensor(m.mod[:, bass.ds(at, KD)], m.bank[6][:, 8:8 + KD], m.mod_b[:, bass.ds(at, KD)], ALU.add)\
            .then_inc(s.mod_taken, 1)



class Attention:

    N = TT * HEADS

    def __init__(self, head, value, cadd=None):
        self.head, self.value = head, value

    def steps(self, n, *stages):
        for lag, stage in stages:
            if 0 <= n - lag < self.N:
                stage(n - lag)

    def of(self, n):
        q, k, mask, tiles = self.head(n % HEADS, n // HEADS)
        return q, k, mask, tiles * P, tiles

    def pe(self, pe, nc, m, s):
        def scores(n):
            q, k, _, w, _ = self.of(n)
            if n >= 3:
                pe.wait_ge(s.sm, n - 2)
            nc.tensor.matmul(m.bank[2 + n % 3][:, 0:w], q, k, start=True, stop=True).then_inc(s.sc, 1)

        def turn(n):
            _, _, _, w, tiles = self.of(n)
            pe.wait_ge(s.ex, n + 1)
            if n >= 3:
                pe.wait_ge(s.pc, n - 2)
            for b in range(tiles):
                mm = nc.tensor.transpose(m.bank[5 + n % 3][:, b * P:(b + 1) * P], m.p[:, n % 3, b * P:(b + 1) * P], m.ident)
            mm.then_inc(s.tr, 1)

        def product(n):
            i, h = n // HEADS, n % HEADS
            _, _, _, w, tiles = self.of(n)
            if h == 0 and i >= 2:
                pe.wait_ge(s.cl, i - 1)
            pe.wait_ge(s.pc, n + 1)
            for b in range(tiles):
                mm = nc.tensor.matmul(m.bank[i % 2][:, h * HD:(h + 1) * HD], m.pT[:, n % 3, b * P:(b + 1) * P],
                                      self.value(h, b), start=(b == 0), stop=(b == tiles - 1))
            mm.then_inc(s.av, 1)

        def out(n):
            if n % HEADS == HEADS - 1:
                i = n // HEADS
                pe.wait_ge(s.on, i + 1)
                for d in range(4):
                    mm = nc.tensor.transpose(m.bank[i % 2][:, d * P:(d + 1) * P], m.bn[:, i % 2, d * P:(d + 1) * P], m.ident)
                mm.then_inc(s.bt, 1)
        for n in range(self.N + 4):
            self.steps(n, (0, scores), (1, turn), (2, product), (4, out))

    def dve(self, dve, nc, m, s, premask=None):
        def mask(n):
            q, k, mask, w, _ = self.of(n)
            dve.wait_ge(s.sc, n + 1)
            if n >= 3:
                dve.wait_ge(s.ex, n - 2)
            if premask:
                premask(n)
            nc.vector.tensor_tensor_reduce(out=m.sm[:, n % 3, 0:w], in0=m.bank[2 + n % 3][:, 0:w], in1=mask,
                                           scale=-(HD ** -0.5), scalar=BIG, op0=ALU.add, op1=ALU.min,
                                           accum_out=m.mn[:, n:n + 1]).then_inc(s.sm, 1)

        def copy(n):
            w = self.of(n)[3]
            dve.wait_ge(s.tr, n + 1)
            if n >= 3:
                dve.wait_ge(s.av, n - 2)
            nc.vector.tensor_copy(m.pT[:, n % 3, 0:w], m.bank[5 + n % 3][:, 0:w]).then_inc(s.pc, 1)

        def normalize(n):
            if n % HEADS == HEADS - 1:
                i = n // HEADS
                r = m.rinv[:, i * HEADS:(i + 1) * HEADS]
                dve.wait_ge(s.av, n + 1)
                nc.vector.reciprocal(r, m.sums[:, i * HEADS:(i + 1) * HEADS])
                dve.drain()
                if i >= 2:
                    dve.wait_ge(s.bt, i - 1)
                nc.vector.tensor_tensor(m.bn[:, i % 2].rearrange("p (h e) -> p h e", h=HEADS),
                                        m.bank[i % 2][:].rearrange("p (h e) -> p h e", h=HEADS),
                                        r.unsqueeze(2).to_broadcast([P, HEADS, HD]), ALU.mult).then_inc(s.on, 1)

        def low(n):
            if n % HEADS == HEADS - 1:
                i = n // HEADS
                dve.wait_ge(s.ch, i + 1)
                nc.vector.tensor_tensor(m.guL[:, 4:8, i * P:(i + 1) * P], m.bank[i % 2][:].rearrange("p (d t) -> p d t", d=4),
                                        f(m.guH[:, 4:8, i * P:(i + 1) * P]), ALU.subtract).then_inc(s.cl, 1)
        for n in range(self.N + 6):
            self.steps(n, (0, mask), (1, copy), (2, normalize), (5, low))

    def act(self, act, nc, m, s):
        def exponential(n):
            w = self.of(n)[3]
            act.wait_ge(s.sm, n + 1)
            if n >= 3:
                act.wait_ge(s.tr, n - 2)
            nc.scalar.activation(m.p[:, n % 3, 0:w], m.sm[:, n % 3, 0:w], ACT.Exp, scale=-1.0, bias=m.mn[:, n:n + 1],
                                 accum_out=m.sums[:, n:n + 1]).then_inc(s.ex, 1)

        def high(n):
            if n % HEADS == HEADS - 1:
                i = n // HEADS
                act.wait_ge(s.bt, i + 1)
                nc.scalar.activation(m.guH[:, 4:8, i * P:(i + 1) * P], m.bank[i % 2][:].rearrange("p (d t) -> p d t", d=4),
                                     ACT.Copy).then_inc(s.ch, 1)
        for n in range(self.N + 5):
            self.steps(n, (0, exponential), (4, high))


def pair(t, h, at, n):
    return t[64 * (h % 2):64 * (h % 2) + 64, h // 2, at:at + n]


class Projections:

    def __init__(self, m, u0, ev0, a):
        self.m, self.u0, self.ev0, self.a = m, u0, ev0, a

    def h(self, k):
        return self.m.hH[:, k], self.m.hL[:, k]

    def banks(self, pe, s, n):
        if n >= 2:
            pe.wait_ge(s.ev, self.ev0 + 2 * n - 2)
        return [self.m.bank[2 * (n % 2) + j][:] for j in range(2)]

    def pe_first(self, pe, s, k):
        pe.wait_ge(s.hl, 8 * self.a + k + 1)

    def pe_tiles(self, pe, nc, s, n, waits=None):
        pe_tiles(pe, nc, self.m, s, self.u0 + n, n % 2, self.banks(pe, s, n), self.h, KD, waits)

    def pe_rows(self, pe, nc, s, n):
        banks = self.banks(pe, s, n)
        outs = [banks[tt // 2][:, (tt % 2) * COLS:(tt % 2 + 1) * COLS] for tt in range(TT)]
        pe_rows(pe, nc, self.m, s, self.u0 + n, self.h, outs)

    def take(self, act, nc, s, n, outs, func=ACT.Copy):
        act_next(act, nc, self.m, s, self.u0 + n, UNIT)
        for j, (out, bank) in enumerate(outs):
            act.wait_ge(s.mm, 4 + 2 * (self.u0 + n) + j + 1)
            nc.scalar.activation(out, bank, func).then_inc(s.ev, 1)

    def cols(self, act, nc, s, n, t, c, func=ACT.Copy):
        self.take(act, nc, s, n, [(t[:, 2 * c + j], self.m.bank[2 * (n % 2) + j][:]) for j in range(2)], func)

    def rows(self, act, nc, s, n, t, c, func=ACT.Copy):
        self.take(act, nc, s, n, [(t[:, 2 * j:2 * j + 2, c * COLS:(c + 1) * COLS],
                                   self.m.bank[2 * (n % 2) + j][:].rearrange("p (t n) -> p t n", t=2))
                                  for j in range(2)], func)



class Mix1:

    def __init__(self, u0, y0, norm, after):
        self.u0, self.y0, self.norm, self.after = u0, y0, norm, after
        self.index = [(i, h) for i in range(1, TT) for h in range(IDX_HEADS)]
        q = lambda h, i: (pair(self.m.q, h, i * P, P), pair(self.m.k, h, 0, (i + 1) * P),
                          self.m.masks[:, ALIBI_AT[i]:ALIBI_AT[i] + (i + 1) * P], i + 1)
        self.attention = Attention(q, lambda h, b: self.m.v[:, b, h * HD:(h + 1) * HD])

    def pe(self, pe, nc, m, s):
        self.m = m
        u0 = self.u0
        proj = Projections(m, u0, 0, self.norm.a)
        h, tiles, rows = proj.h, (lambda n: proj.pe_tiles(pe, nc, s, n)), (lambda n: proj.pe_rows(pe, nc, s, n))

        def turned(bank, x):
            nc.tensor.matmul(m.bank[bank][:], m.perm, x, start=True, stop=True).then_inc(s.pq, 1)

        pe.wait_ge(s.low, u0 + 3)
        for k in range(KD):
            proj.pe_first(pe, s, k)
            mm = pe_3(nc, m.bank[0][:], [w[:, 0, k * COLS:k * COLS + P] for w in (m.wH, m.wL)], h(k), k == 0, k == KD - 1)
        mm.then_inc(s.mm, 1)
        for tt in range(TT):
            for k in range(KD):
                w = [x[:, 0, k * COLS + P:k * COLS + P + IDX_HEADS] for x in (m.wH, m.wL)]
                left = [x[:, tt * P:(tt + 1) * P] for x in h(k)]
                mm = pe_3(nc, m.bank[1][:, 4 * tt:4 * tt + 4], left, w, k == 0, k == KD - 1)
        mm.then_inc(s.mm, 1)
        tiles(1)
        rows(2)
        pe.wait_ge(s.ev, 4)
        turned(4, m.ki[:])
        turned(5, m.qi[:, 0])
        turned(6, m.qi[:, 1])
        rows(3)
        pe.wait_ge(s.rope, 3)
        for n, (i, hh) in enumerate(self.index):
            if n >= 4:
                pe.wait_ge(s.relu, n - 3)
            lo = 64 * (hh % 2)
            nc.tensor.matmul(m.bank[4 + n % 4][:, 0:(i + 1) * P], pair(m.qi, hh, i * P, P), m.ki[lo:lo + 64, 0:(i + 1) * P],
                             start=True, stop=True).then_inc(s.lg, 1)
        tiles(4)
        tiles(5)
        rows(6)
        rows(7)
        pe.wait_ge(s.sgw, 1)
        pe.wait_ge(s.relu, len(self.index))
        for g in range(4):
            for c in range(TT):
                nc.tensor.matmul(m.bank[4 + g][:, c * P:(c + 1) * P], m.ones[0:1, :], m.sgub[0:1, g], start=True, stop=False)
                mm = nc.tensor.matmul(m.bank[4 + g][:, c * P:(c + 1) * P], m.va[:, c, g * P:(g + 1) * P], m.sguT[:, g],
                                      start=False, stop=True)
            mm.then_inc(s.sgu, 1)
        tiles(8)
        tiles(9)
        pe.wait_ge(s.ev, 20)
        for j in range(4):
            pe.wait_ge(s.ao, j + 1)
            turned(4 + j, m.q[:, j])
        tiles(10)
        tiles(11)
        pe.wait_ge(s.ev, 24)
        for j in range(4):
            pe.wait_ge(s.rope, 4 + j)
            turned(4 + j, m.k[:, j])
        pe.wait_ge(s.rope, 11)
        self.attention.pe(pe, nc, m, s)
        pe_mixed_out(pe, nc, m, s, u0 + MIX1_PROJ, self.y0)

    def act(self, act, nc, m, s):
        self.m = m
        u0 = self.u0
        proj = Projections(m, u0, 0, self.norm.a)
        cols = lambda n, t, c, func=ACT.Copy: proj.cols(act, nc, s, n, t, c, func)
        rows = lambda n, t, c, func=ACT.Copy: proj.rows(act, nc, s, n, t, c, func)
        proj.take(act, nc, s, 0, [(m.ki[:], m.bank[0][:]), (m.wi[:], m.bank[1][:, 0:4 * TT])])
        cols(1, m.qi, 0)
        rows(2, m.va, 0, ACT.Gelu)
        rows(3, m.va, 1, ACT.Gelu)
        for n, (i, hh) in enumerate(self.index):
            act.wait_ge(s.lg, n + 1)
            if n >= 2:
                act.wait_ge(s.lacc, n - 1)
            w = (i + 1) * P
            nc.scalar.activation(m.rl[:, n % 2, 0:w], m.bank[4 + n % 4][:, 0:w], ACT.Relu).then_inc(s.relu, 1)
        cols(4, m.u, 0, ACT.Gelu)
        cols(5, m.u, 1, ACT.Gelu)
        rows(6, m.v, 0)
        rows(7, m.v, 1)
        cols(8, m.q, 0)
        cols(9, m.q, 1)
        cols(10, m.k, 0)
        cols(11, m.k, 1)
        self.attention.act(act, nc, m, s)
        act_mixed_out(act, nc, m, s, u0 + MIX1_PROJ, self.after)

    def dve(self, dve, nc, m, s, gate):
        self.m = m

        def rotate(n, x, bank):
            dve.wait_ge(s.pq, n + 1)
            dve.drain()
            nc.vector.tensor_tensor(m.ra[:], x, m.cos[:], ALU.mult)
            nc.vector.tensor_tensor(m.rb[:], m.bank[bank][:], m.sin[:], ALU.mult)
            dve.drain()
            nc.vector.tensor_tensor(x, m.ra[:], m.rb[:], ALU.add).then_inc(s.rope, 1)
        rotate(0, m.ki[:], 4)
        rotate(1, m.qi[:, 0], 5)
        rotate(2, m.qi[:, 1], 6)
        score = [m.masks[:, ALIBI_AT[i]:ALIBI_AT[i] + (i + 1) * P] for i in range(TT)]
        for n, (i, hh) in enumerate(self.index):
            dve.wait_ge(s.relu, n + 1)
            w = m.wi[:, 4 * i + hh:4 * i + hh + 1]
            dve.drain()
            if hh == 0:
                nc.vector.tensor_scalar(score[i], m.rl[:, n % 2, 0:(i + 1) * P], w, None, ALU.mult).then_inc(s.lacc, 1)
            else:
                nc.vector.scalar_tensor_tensor(out=score[i], in0=m.rl[:, n % 2, 0:(i + 1) * P], scalar=w, in1=score[i],
                                               op0=ALU.mult, op1=ALU.add).then_inc(s.lacc, 1)
            if hh == IDX_HEADS - 1:
                dve.drain()
                diagonal = score[i][:, i * P:(i + 1) * P]
                nc.vector.tensor_tensor(diagonal, diagonal, m.tri, ALU.min)
        for i in range(1, TT):
            for _ in range(TOPK // 8):
                dve.drain()
                nc.vector.max(m.m8[:], score[i])
                dve.drain()
                nc.vector.match_replace(score[i], m.m8[:], score[i], TAKEN)
            dve.drain()
            nc.vector.tensor_scalar(score[i], score[i], (BELOW + TAKEN) / 2, NEG, ALU.is_gt, ALU.mult)
        for g in range(4):
            dve.wait_ge(s.sgu, g + 1)
            dve.drain()
            nc.vector.tensor_tensor(m.ra[:], m.u[:, g], m.bank[4 + g][:], ALU.mult).then_inc(s.ao, 1)
            dve.drain()
            nc.vector.tensor_copy(m.guH[:, g], m.ra[:])
            dve.drain()
            nc.vector.tensor_tensor(m.guL[:, g], m.ra[:], f(m.guH[:, g]), ALU.subtract)
        for j in range(4):
            rotate(3 + j, m.q[:, j], 4 + j)
        for j in range(4):
            rotate(7 + j, m.k[:, j], 4 + j)
        self.attention.dve(dve, nc, m, s)
        dve_update(dve, nc, m, s, self.u0 + MIX1_PROJ, gate, self.after)



class Mix2:

    CHAIN = 8

    def __init__(self, u0, y0, norm, after):
        self.u0, self.y0, self.norm, self.after = u0, y0, norm, after

        def head(h, i):
            m = self.m
            if h < 4:
                return (pair(m.q, h, i * P, P), pair(m.q[:, 2:4], h, 0, (i + 1) * P), m.mdh[:, h % 2, 0:(i + 1) * P], i + 1)
            return pair(m.cq, h - 4, i * P, P), pair(m.memk, h - 4, 0, 256), m.none[:], 2

        def value(h, b):
            return self.m.mv[:, b, h * HD:(h + 1) * HD] if h < 4 else self.m.memv[:, b, (h - 4) * HD:(h - 3) * HD]
        self.attention = Attention(head, value)

    def chain(self, r):
        m = self.m
        x = m.q[:, r] if r < 4 else (m.cq[:, r - 4] if r < 6 else m.memk[:, r - 6])
        return x, (4 if r < 6 else 2), (8 * r if r < 7 else 52)

    def pe(self, pe, nc, m, s):
        self.m = m
        proj = Projections(m, self.u0, 4, self.norm.a)
        proj.pe_tiles(pe, nc, s, 0, lambda k: proj.pe_first(pe, s, k))
        for n in range(1, 5):
            proj.pe_tiles(pe, nc, s, n)
        pe.wait_ge(s.gw, 16)
        for g in range(2):
            for c in range(4):
                pe.wait_ge(s.xb, c + 1)
                if g:
                    pe.wait_ge(s.sgm, c + 1)
                nc.tensor.matmul(m.bank[4 + c][:], m.gatew[:, g, c], m.xb[:, c], start=True, stop=True).then_inc(s.ga, 1)
        for n in range(5, 7):
            proj.pe_tiles(pe, nc, s, n)
        proj.pe_rows(pe, nc, s, 7)
        pe.wait_ge(s.sgm, 8)
        for r in range(self.CHAIN):
            _, tiles, at = self.chain(r)
            pe.wait_ge(s.hsq, r + 1)
            for tt in range(tiles):
                mm = nc.tensor.matmul(m.bank[4][:, at + 2 * tt:at + 2 * tt + 2], m.hs[:, r % 2, tt * P:(tt + 1) * P], m.sel,
                                      start=True, stop=True)
            mm.then_inc(s.hss, 1)
        for r in range(self.CHAIN):
            pe.wait_ge(s.rxd, r + 1)
            if r >= 2:
                pe.wait_ge(s.hq, r - 1)
            for tt in range(self.chain(r)[1]):
                mm = nc.tensor.transpose(m.bank[5 + r % 2][:, tt * P:(tt + 1) * P], m.rx[:, r % 2, tt * P:(tt + 1) * P],
                                         m.ident)
            mm.then_inc(s.hx, 1)
        pe.wait_ge(s.hq, self.CHAIN)
        pe.wait_ge(s.ev, 20)
        self.attention.pe(pe, nc, m, s)
        pe_mixed_out(pe, nc, m, s, self.u0 + MIX2_PROJ, self.y0)

    def act(self, act, nc, m, s):
        self.m = m
        proj = Projections(m, self.u0, 4, self.norm.a)
        ig = self.input_gate
        proj.cols(act, nc, s, 0, m.lx, 0)
        proj.cols(act, nc, s, 1, m.lx, 1)
        proj.cols(act, nc, s, 2, m.gl, 0, ACT.Gelu_apprx_tanh)
        proj.cols(act, nc, s, 3, m.gl, 1, ACT.Gelu_apprx_tanh)
        proj.cols(act, nc, s, 4, m.q, 0)
        for c in range(4):
            act.wait_ge(s.ga, c + 1)
            nc.scalar.activation(m.rg[:, c], m.bank[4 + c][:], ACT.Sigmoid, bias=m.vec[:, V_AB + c:V_AB + c + 1])\
                .then_inc(s.sgm, 1)
        for c in range(4):
            act.wait_ge(s.ga, 4 + c + 1)
            nc.scalar.activation(ig(c), m.bank[4 + c][:], ACT.Sigmoid, bias=m.vec[:, V_XB + c:V_XB + c + 1])\
                .then_inc(s.sgm, 1)
        proj.cols(act, nc, s, 5, m.q, 1)
        act.wait_ge(s.c8, 1)
        for c in range(4):
            nc.scalar.activation(m.lx[:, c], m.rg[:, c], ACT.Exp, scale=m.sp[:, 4, c:c + 1]).then_inc(s.et, 1)
        for c in range(4):
            act.wait_ge(s.et, c + 1)
            nc.scalar.activation(m.rg[:, c], m.rg[:, c], ACT.Tanh, scale=m.sp[:, 5, c:c + 1]).then_inc(s.et, 1)
        proj.cols(act, nc, s, 6, m.cq, 0)
        for c in range(4):
            act.wait_ge(s.m2, c + 1)
            nc.scalar.activation(m.rg[:, c], m.rg[:, c], ACT.Sqrt).then_inc(s.mult, 1)
        proj.rows(act, nc, s, 7, m.mv, 0)
        for r in range(self.CHAIN):
            x, tiles, _ = self.chain(r)
            if r >= 2:
                act.wait_ge(s.hss, r - 1)
            act.wait_ge(s.ev, 20)
            nc.scalar.activation(m.hs[:, r % 2, 0:tiles * P], x, ACT.Square).then_inc(s.hsq, 1)
        act.wait_ge(s.hvar, 1)
        nc.scalar.activation(m.hr[:], m.hv[:], ACT.Sqrt).then_inc(s.hrt, 1)
        self.attention.act(act, nc, m, s)
        act_mixed_out(act, nc, m, s, self.u0 + MIX2_PROJ, self.after)

    def input_gate(self, c):
        return self.m.ig3[:, c] if c < 3 else self.m.ig1[:, 0]

    def dve(self, dve, nc, m, s):
        self.m = m
        vec = lambda at: m.vec[:, at:at + 1]
        for c in range(4):
            dve.wait_ge(s.ev, 4 + c + 1)
            nc.vector.tensor_scalar(m.xb[:, c], m.lx[:, c], vec(V_CONVW + 12 + c), vec(V_CONVB + c), ALU.mult, ALU.add)
            for back in range(1, 4):
                dve.drain()
                mm = nc.vector.scalar_tensor_tensor(out=m.xb[:, c, back:], in0=m.lx[:, c, 0:T - back],
                                                    scalar=vec(V_CONVW + 4 * (3 - back) + c), in1=m.xb[:, c, back:],
                                                    op0=ALU.mult, op1=ALU.add)
            mm.then_inc(s.xb, 1)
        for c in range(4):
            dve.drain()
            dve.wait_ge(s.et, 4 + c + 1)
            nc.vector.tensor_tensor(m.la[:], m.lx[:, c], m.lx[:, c], ALU.mult)
            dve.drain()
            nc.vector.scalar_tensor_tensor(out=m.rg[:, c], in0=m.la[:], scalar=1.0, in1=m.rg[:, c], op0=ALU.add,
                                           op1=ALU.mult).then_inc(s.m2, 1)
        dve.wait_ge(s.sgm, 8)
        for c in range(4):
            dve.drain()
            nc.vector.tensor_tensor(m.la[:], m.xb[:, c], self.input_gate(c), ALU.mult)
            dve.wait_ge(s.mult, c + 1)
            nc.vector.memset(m.rg[:, c, 0:1], 1.0)
            dve.drain()
            nc.vector.tensor_tensor(m.la[:], m.la[:], m.rg[:, c], ALU.mult)
            dve.drain()
            nc.vector.tensor_tensor_scan(m.lb[:], m.lx[:, c], m.la[:], 0.0, ALU.mult, ALU.add)
            dve.drain()
            dve.wait_ge(s.ev, 8 + c + 1)
            nc.vector.tensor_tensor(m.la[:], m.lb[:], m.gl[:, c], ALU.mult)
            dve.drain()
            nc.vector.tensor_copy(m.guH[:, c], m.la[:])
            dve.drain()
            nc.vector.tensor_tensor(m.guL[:, c], m.la[:], f(m.guH[:, c]), ALU.subtract)
        dve.wait_ge(s.hss, self.CHAIN)
        nc.vector.tensor_scalar(m.hv[:], m.bank[4][:, 0:56], 1.0 / HD, EPS, ALU.mult, ALU.add).then_inc(s.hvar, 1)
        newton(dve, nc, s.hrt, 1, m.hv[:], m.hr[:], m.ht[:])

        def spread(r):
            _, tiles, at = self.chain(r)
            if r >= 2:
                dve.wait_ge(s.hx, r - 1)
            nc.vector.tensor_copy(m.rx[:, r % 2, 0:tiles * P].rearrange("p (t e) -> p t e", e=HD),
                                  m.hr[:, at:at + 2 * tiles].unsqueeze(2).to_broadcast([P, 2 * tiles, HD])).then_inc(s.rxd, 1)
        spread(0)
        spread(1)
        for r in range(self.CHAIN):
            x, tiles, _ = self.chain(r)
            dve.wait_ge(s.hx, r + 1)
            nc.vector.scalar_tensor_tensor(out=x, in0=x, scalar=vec(V_GAINS + r // 2), in1=m.bank[5 + r % 2][:, 0:tiles * P],
                                           op0=ALU.mult, op1=ALU.mult).then_inc(s.hq, 1)
            if r + 2 < self.CHAIN:
                spread(r + 2)

        def mask_ready(n):
            if n % HEADS < 4:
                dve.wait_ge(s.mkd, n // HEADS * 4 + n % HEADS + 1)
        self.attention.dve(dve, nc, m, s, mask_ready)
        dve_update(dve, nc, m, s, self.u0 + MIX2_PROJ, lambda d: 1.0, self.after)

    def pool_masks(self, pool, nc, m, s):
        for i in range(TT):
            for h in range(4):
                before = HEADS * i + h - 2 if h >= 2 else HEADS * (i - 1) + h + 2
                if h >= 2 or i:
                    pool.wait_ge(s.sm, before + 1)
                else:
                    pool.wait_ge(s.hvar, 1)
                w = (i + 1) * P
                nc.gpsimd.tensor_scalar(m.mdh[:, h % 2, 0:w], m.masks[:, ALIBI_AT[i]:ALIBI_AT[i] + w], 4.0 ** -(h + 1), None,
                                        ALU.mult).then_inc(s.mkd, 1)


def dve_decay_rates(dve, nc, m, s):
    lam, (size, e, z, z2, minus, rate) = m.vec[:, V_LAM:V_LAM + 4], [m.sp[:, j] for j in range(6)]
    nc.vector.scalar_tensor_tensor(out=size, in0=lam, scalar=-1.0, in1=lam, op0=ALU.mult, op1=ALU.max).then_inc(s.lam, 1)
    dve.wait_ge(s.elam, 1)
    nc.vector.tensor_scalar(z, e, 2.0, None, ALU.add)
    dve.drain()
    nc.vector.reciprocal(z, z)
    dve.drain()
    nc.vector.tensor_tensor(z, z, e, ALU.mult)
    dve.drain()
    nc.vector.tensor_tensor(z2, z, z, ALU.mult)
    nc.vector.memset(rate, 1.0 / 17)
    for n in range(15, 0, -2):
        dve.drain()
        nc.vector.tensor_tensor(rate, rate, z2, ALU.mult)
        dve.drain()
        nc.vector.tensor_scalar(rate, rate, 1.0 / n, None, ALU.add)
    nc.vector.tensor_scalar(size, lam, -1.0, 0.0, ALU.mult, ALU.max)
    dve.drain()
    nc.vector.scalar_tensor_tensor(out=rate, in0=rate, scalar=2.0, in1=z, op0=ALU.mult, op1=ALU.mult)
    dve.drain()
    nc.vector.tensor_tensor(rate, rate, size, ALU.add)
    dve.drain()
    nc.vector.tensor_scalar(minus, rate, -8.0, None, ALU.mult)
    nc.vector.tensor_scalar(rate, rate, 8.0, None, ALU.mult).then_inc(s.c8, 1)


def pe_mixed_out(pe, nc, m, s, u, y0):
    pe.wait_ge(s.cl, TT)
    cat = lambda k: (m.guH[:, k], m.guL[:, k])
    for q in range(OUT_UNITS):
        pe.wait_ge(s.y, y0 + 2 * q + 2)
        pe_tiles(pe, nc, m, s, u + q, q % 2, [m.bank[4 + 2 * (q % 2)][:], m.bank[5 + 2 * (q % 2)][:]], cat, KD)


def act_mixed_out(act, nc, m, s, u, after):
    for q in range(OUT_UNITS):
        act_next(act, nc, m, s, u + q, UNIT)
        after.act_square(act, nc, m, s, 2 * q)
        after.act_square(act, nc, m, s, 2 * q + 1)



def signals(nc, tag, first):
    s = Signals()
    s.all = []

    def new(name):
        s.all.append(nc.alloc_semaphore(f"{tag}_{name}"))
        return s.all[-1]
    s.full = [new("full0"), new("full1")]
    s.high = new("high")
    s.low = new("low")
    s.mm = new("mm")
    s.silu = new("silu")
    s.ufree = new("ufree")
    s.gu = new("gu")
    s.y = new("y")
    s.sq = new("sq")
    s.acc = new("acc")
    s.ss = new("ss")
    s.var = new("var")
    s.rt = new("rt")
    s.dg = new("dg")
    s.spread = new("spread")
    s.tt = new("tt")
    s.hh = new("hh")
    s.hl = new("hl")
    s.ev = new("ev")
    s.sm = new("sm")
    s.sc = new("sc")
    s.ex = new("ex")
    s.pc = new("pc")
    s.tr = new("tr")
    s.av = new("av")
    s.on = new("on")
    s.bt = new("bt")
    s.cl = new("cl")
    s.ch = new("ch")
    if first:
        s.mod_full = [new("mod_full0"), new("mod_full1")]
        s.big = [new("big0"), new("big1"), new("big2")]
        s.big_used = new("big_used")
        s.mod_used = new("mod_used")
        s.mod_mm = new("mod_mm")
        s.mod_taken = new("mod_taken")
        s.par = new("par")
        s.pq = new("pq")
        s.rope = new("rope")
        s.lg = new("lg")
        s.relu = new("relu")
        s.lacc = new("lacc")
        s.sgw = new("sgw")
        s.sgu = new("sgu")
        s.ao = new("ao")
    else:
        s.vec = new("vec")
        s.dist = new("dist")
        s.gw = new("gw")
        s.mem = new("mem")
        s.lam = new("lam")
        s.elam = new("elam")
        s.c8 = new("c8")
        s.none = new("none")
        s.xb = new("xb")
        s.ga = new("ga")
        s.sgm = new("sgm")
        s.et = new("et")
        s.m2 = new("m2")
        s.mult = new("mult")
        s.hsq = new("hsq")
        s.hss = new("hss")
        s.hvar = new("hvar")
        s.hrt = new("hrt")
        s.rxd = new("rxd")
        s.hx = new("hx")
        s.hq = new("hq")
        s.mkd = new("mkd")
        s.st = new("st")
    return s


def setup_block(nc, m, a):
    s = Signals()
    s.ld = nc.alloc_semaphore("i_loaded")
    s.cx = nc.alloc_semaphore("i_cx")
    s.ms = nc.alloc_semaphore("i_set")
    s.ang = nc.alloc_semaphore("i_angles")
    with nc.Block() as block:
        @block.sync
        def _(sp):
            sp.dma_start(m.pos[:], a["positions"].partition_broadcast(P)).then_inc(s.ld, 16)
            sp.dma_start(m.cst[:], a["constants"]).then_inc(s.ld, 16)
            sp.dma_start(m.csil[:], a["c"]).then_inc(s.cx, 16)
            sp.dma_start(m.x[:], a["x"]).then_inc(s.cx, 16)
            sp.wait_ge(s.cx, 32)

        @block.vector
        def _(dve):
            nc.vector.memset(m.ones[:], 1.0)
            nc.vector.memset(m.zero[:], 0.0)
            nc.vector.memset(m.halfpi[:], float(np.pi / 2)).then_inc(s.ms, 1)
            dve.wait_ge(s.ld, 32)
            nc.vector.tensor_copy(m.ang[:], m.pos[:])
            dve.drain()
            nc.vector.tensor_scalar(m.ang[:], m.ang[:], m.freq, None, ALU.mult)
            dve.drain()
            nc.vector.tensor_scalar(m.turn[:], m.ang[:], float(1 / (2 * np.pi)), MAGIC, ALU.mult, ALU.add)
            dve.drain()
            nc.vector.tensor_scalar(m.turn[:], m.turn[:], -MAGIC, None, ALU.add)
            for part in TWO_PI_PARTS:
                dve.drain()
                nc.vector.scalar_tensor_tensor(out=m.ang[:], in0=m.turn[:], scalar=-part, in1=m.ang[:], op0=ALU.mult, op1=ALU.add)
            dve.drain()
            nc.vector.tensor_scalar(m.ang[:], m.ang[:], 3.1415925, -3.1415925, ALU.min, ALU.max)
            dve.drain()
            nc.vector.scalar_tensor_tensor(out=m.turn[:], in0=m.ang[:], scalar=-1.0, in1=m.ang[:], op0=ALU.mult, op1=ALU.max)\
                .then_inc(s.ang, 1)

        @block.scalar
        def _(act):
            act.wait_ge(s.cx, 32)
            nc.scalar.activation(m.csil[:], m.csil[:], ACT.Silu)
            act.wait_ge(s.ms, 1)
            act.wait_ge(s.ang, 1)
            nc.scalar.activation(m.sin[:], m.ang[:], ACT.Sin)
            nc.scalar.activation(m.cos[:], m.turn[:], ACT.Sin, scale=-1.0, bias=m.halfpi[:])


def layer_block(nc, m, s, a, l):
    norms = [Norm(0, 0), Norm(1, 1, y0=KD), Norm(2, 2, y0=2 * KD)]
    ffn1 = Ffn(0, L_FFN1, 0, norms[0], norms[1], UNIT)
    mix = Mix1(L_MIX, 2 * KD, norms[1], norms[2])
    ffn2 = Ffn(1, L_FFN2, 3 * KD, norms[2], None, 0)
    mods = Modulation()
    hH, hL = (lambda k: m.hH[:, k]), (lambda k: m.hL[:, k])
    shift = lambda chunk: (lambda k: m.mod[:, chunk * KD + k:chunk * KD + k + 1])
    scale = lambda k: m.A[:, k:k + 1]

    def dve_scale_of(dve, n):
        dve.drain()
        at = (3 * n + 1) * KD
        nc.vector.scalar_tensor_tensor(out=m.A[:], in0=m.mod[:, at:at + KD], scalar=1.0, in1=m.gains[:, n * KD:(n + 1) * KD],
                                       op0=ALU.add, op1=ALU.mult)
        dve.drain()

    with nc.Block() as block:
        @block.sync
        def _(sp):
            w_in = lambda g: (lambda i: a["ffn_in"][(2 * l + g) * IN_UNITS + i])
            w_a = lambda g: (lambda i: a["ffn_out_a"][(2 * l + g) * OUT_UNITS + i])
            w_b = lambda g: (lambda i: a["ffn_out_b"][(2 * l + g) * OUT_UNITS + i])
            mod = a["ada_w"][l]
            for q in range(3):
                mods.sp_big(sp, m, s, mod, q)
            sp.dma_start(m.mod_b[:], a["ada_b"][l]).then_inc(s.par, 16)
            sp.dma_start(m.gains[:], a["gains"][l]).then_inc(s.par, 16)
            sp_unit(sp, m, s, w_in(0)(0), 0, UNIT)
            sp_unit(sp, m, s, w_in(0)(1), 1, UNIT)
            mods.sp_big(sp, m, s, mod, 3)
            with sp.Fori(0, IN_A // 2 - 1) as i:
                for j in range(2):
                    sp.wait_ge(s.low, 2 * i + j + 3)
                    sp.dma_start(m.wraw[:, j, 0:UNIT], w_in(0)(2 * i + 2 + j)).then_inc(s.full[j], 16)
                mods.sp_chunk(sp, m, s, mod, i)
            sp_unit(sp, m, s, w_a(0)(0), IN_A, UNIT_A)
            sp_unit(sp, m, s, w_a(0)(1), IN_A + 1, UNIT_A)
            mods.sp_chunk(sp, m, s, mod, IN_A // 2 - 1)
            mods.sp_chunk(sp, m, s, mod, IN_A // 2)
            sp_unit(sp, m, s, w_a(0)(2), IN_A + 2, UNIT_A)
            sp_unit(sp, m, s, w_a(0)(3), IN_A + 3, UNIT_A)
            sp_units(sp, m, s, lambda i: w_in(0)(IN_A + i), ffn1.ub, IN_B, UNIT)
            sp_units(sp, m, s, w_b(0), ffn1.uc, OUT_UNITS, UNIT_B)
            sp.wait_ge(s.mod_mm, N_MOD)
            sp.dma_start(m.sguT[:], a["sgu_w"][l]).then_inc(s.par, 16)
            sp.dma_start(m.sgub[0:1], a["sgu_b"][l]).then_inc(s.par, 16)
            sp.dma_start(m.masks[:, 0:P], a["causal"]).then_inc(s.par, 16)
            sp_units(sp, m, s, lambda i: a["mix"][l, i], L_MIX, MIX1_PROJ + OUT_UNITS, UNIT)
            sp_units(sp, m, s, w_in(1), ffn2.u0, IN_A, UNIT)
            sp_units(sp, m, s, w_a(1), ffn2.ua, OUT_UNITS, UNIT_A)
            sp_units(sp, m, s, lambda i: w_in(1)(IN_A + i), ffn2.ub, IN_B, UNIT)
            sp_units(sp, m, s, w_b(1), ffn2.uc, OUT_UNITS, UNIT_B)

        @block.gpsimd
        def _(pool):
            pool.sem_inc(s.low, 2)
            runs = lambda x: ((x.u0, IN_A, UNIT), (x.ua, OUT_UNITS, UNIT_A), (x.ub, IN_B, UNIT), (x.uc, OUT_UNITS, UNIT_B))
            for run in runs(ffn1):
                pool_low(pool, nc, m, s, *run)
            pool.wait_ge(s.par, 80)
            nc.gpsimd.affine_select(out=m.sguT[:], in_=m.sguT[:], pattern=[[0, 4], [1, P]], compare_op=ALU.is_ge, fill=0.0,
                                    base=0, channel_multiplier=-1).then_inc(s.sgw, 1)
            pool_low(pool, nc, m, s, L_MIX, MIX1_PROJ + OUT_UNITS, UNIT)
            for run in runs(ffn2):
                pool_low(pool, nc, m, s, *run)

        @block.scalar
        def _(act):
            act.sem_inc(s.silu, 2)
            for d in range(KD):
                norms[0].act_square(act, nc, m, s, d)
            act_high(act, nc, m, s, 0, 0, 0, UNIT)
            act_high(act, nc, m, s, 1, 1, 0, UNIT)
            norms[0].act_sqrt(act, nc, m, s)
            norms[0].act_apply(act, nc, m, s, hH, scale, shift(0))
            ffn1.act(act, nc, m, s)
            norms[1].act_sqrt(act, nc, m, s)
            norms[1].act_apply(act, nc, m, s, hH, scale, shift(3))
            mix.act(act, nc, m, s)
            norms[2].act_sqrt(act, nc, m, s)
            norms[2].act_apply(act, nc, m, s, hH, scale, shift(6))
            ffn2.act(act, nc, m, s)

        @block.vector
        def _(dve):
            dve.sem_inc(s.ufree, 2)
            dve.sem_inc(s.y, 4)
            dve.sem_inc(s.mod_used, MOD_SLOTS)
            for d in range(KD):
                norms[0].dve_add(dve, nc, m, s, d)
            dve.wait_ge(s.par, 32)
            mods.dve_big(dve, nc, m, s)
            dve_scale_of(dve, 0)
            norms[0].dve_rsqrt(dve, nc, m, s)
            norms[0].dve_apply(dve, nc, m, s, hH, hL)
            ffn1.dve(dve, nc, m, s, lambda d: m.gate[:, d:d + 1], mods)
            dve_scale_of(dve, 1)
            norms[1].dve_rsqrt(dve, nc, m, s)
            norms[1].dve_apply(dve, nc, m, s, hH, hL)
            mix.dve(dve, nc, m, s, lambda d: m.mod[:, 5 * KD + d:5 * KD + d + 1])
            dve_scale_of(dve, 2)
            dve_half_gate(dve, nc, m, 8)
            norms[2].dve_rsqrt(dve, nc, m, s)
            norms[2].dve_apply(dve, nc, m, s, hH, hL)
            ffn2.dve(dve, nc, m, s, lambda d: m.gate[:, d:d + 1])

        @block.tensor
        def _(pe):
            pe.sem_inc(s.mm, 4)
            norms[0].pe_sum(pe, nc, m, s)
            mods.pe_reduce(pe, nc, m, s, 0)
            mods.pe_reduce(pe, nc, m, s, 1)
            norms[0].pe_spread(pe, nc, m, s)
            ffn1.pe(pe, nc, m, s, mods)
            norms[1].pe_sum(pe, nc, m, s)
            norms[1].pe_spread(pe, nc, m, s)
            mix.pe(pe, nc, m, s)
            norms[2].pe_sum(pe, nc, m, s)
            norms[2].pe_spread(pe, nc, m, s)
            ffn2.pe(pe, nc, m, s)

    with nc.Block() as block:
        @block.gpsimd
        def _(pool):
            for x in s.all:
                pool.sem_clear(x)


def second_block(nc, m, s, a):
    norms = [Norm(0, None), Norm(1, 0, tokens=256, src=lambda m: m.mem), Norm(2, 1, y0=0), Norm(3, 2, y0=2 * KD),
             Norm(4, 3, y0=3 * KD)]
    ffn1 = Ffn(0, S_FFN1, KD, norms[2], norms[3], UNIT)
    mix = Mix2(S_MIX, 3 * KD, norms[3], norms[4])
    ffn2 = Ffn(1, S_FFN2, 4 * KD, norms[4], None, 0)
    hH, hL = (lambda k: m.hH[:, k]), (lambda k: m.hL[:, k])
    halves = lambda t: t.rearrange("p a (b n) -> p (a b) n", b=2)
    memH, memL = halves(m.guH[:, 0:4]), halves(m.guL[:, 4:8])
    gain = lambda at: (lambda k: m.vec[:, at + k:at + k + 1])
    no_shift = lambda k: m.zero[:]
    half = lambda d: 0.5

    with nc.Block() as block:
        @block.sync
        def _(sp):
            w_in = lambda g: (lambda i: a["ffn_in"][(2 * LAYERS + g) * IN_UNITS + i])
            w_a = lambda g: (lambda i: a["ffn_out_a"][(2 * LAYERS + g) * OUT_UNITS + i])
            w_b = lambda g: (lambda i: a["ffn_out_b"][(2 * LAYERS + g) * OUT_UNITS + i])
            sp.dma_start(m.vec[:], a["vec"]).then_inc(s.vec, 16)
            sp_unit(sp, m, s, a["mem_kv"][0], 0, UNIT)
            sp_unit(sp, m, s, a["mem_kv"][1], 1, UNIT)
            sp.dma_start(m.mem[:], a["mem"]).then_inc(s.mem, 16)
            sp.dma_start(m.masks[:], a["alibi"]).then_inc(s.dist, 16)

            def ffn(x, g):
                sp_units(sp, m, s, w_in(g), x.u0, IN_A, UNIT)
                sp_units(sp, m, s, w_a(g), x.ua, OUT_UNITS, UNIT_A)
                sp_units(sp, m, s, lambda i: w_in(g)(IN_A + i), x.ub, IN_B, UNIT)
                sp_units(sp, m, s, w_b(g), x.uc, OUT_UNITS, UNIT_B)
            ffn(ffn1, 0)
            sp_units(sp, m, s, lambda i: a["mix_2"][i], S_MIX, 2, UNIT)
            sp.wait_ge(s.y, 4 + 3 * KD)
            sp.dma_start(m.gatew[:], a["gate_w"]).then_inc(s.gw, 16)
            sp_units(sp, m, s, lambda i: a["mix_2"][2 + i], S_MIX + 2, MIX2_PROJ + OUT_UNITS - 2, UNIT)
            ffn(ffn2, 1)
            for d in range(0, KD, 2):
                sp.wait_ge(s.y, 4 + 5 * KD + d + 2)
                sp.dma_start(a["out"][:, d:d + 2], m.x[:, d:d + 2]).then_inc(s.st, 16)
            sp.wait_ge(s.st, 16 * KD // 2)

        @block.gpsimd
        def _(pool):
            pool.sem_inc(s.low, 2)
            nc.gpsimd.memset(m.none[:], 0.0).then_inc(s.none, 1)
            runs = lambda x: ((x.u0, IN_A, UNIT), (x.ua, OUT_UNITS, UNIT_A), (x.ub, IN_B, UNIT), (x.uc, OUT_UNITS, UNIT_B))
            pool_low(pool, nc, m, s, 0, MEM_UNITS, UNIT)
            for run in runs(ffn1):
                pool_low(pool, nc, m, s, *run)
            pool_low(pool, nc, m, s, S_MIX, MIX2_PROJ + 2, UNIT)
            pool.wait_ge(s.dist, 16)
            mix.pool_masks(pool, nc, m, s)
            pool_low(pool, nc, m, s, S_MIX + MIX2_PROJ + 2, OUT_UNITS - 2, UNIT)
            for run in runs(ffn2):
                pool_low(pool, nc, m, s, *run)

        @block.scalar
        def _(act):
            act.sem_inc(s.silu, 2)
            act.wait_ge(s.vec, 16)
            for d in range(KD):
                norms[0].act_square(act, nc, m, s, d)
            act_high(act, nc, m, s, 0, 0, 0, UNIT)
            act_high(act, nc, m, s, 1, 1, 0, UNIT)
            act.wait_ge(s.lam, 1)
            nc.scalar.activation(m.sp[:, 1], m.sp[:, 0], ACT.Exp, scale=-1.0).then_inc(s.elam, 1)
            norms[0].act_sqrt(act, nc, m, s)
            act.wait_ge(s.mem, 16)
            for d in range(KD):
                norms[1].act_square(act, nc, m, s, d)
            norms[1].act_sqrt(act, nc, m, s)
            norms[1].act_apply(act, nc, m, s, lambda k: memH[:, k], gain(V_MEM), no_shift)
            for d in range(KD):
                norms[2].act_square(act, nc, m, s, d)
            for n, t in enumerate((m.memk, m.memv)):
                act_next(act, nc, m, s, n, UNIT)
                for j in range(2):
                    act.wait_ge(s.mm, 4 + 2 * n + j + 1)
                    nc.scalar.activation(t[:, j], m.bank[2 * n + j][:, 0:256], ACT.Copy).then_inc(s.ev, 1)
            norms[2].act_sqrt(act, nc, m, s)
            norms[2].act_apply(act, nc, m, s, hH, gain(V_FFN1), no_shift)
            ffn1.act(act, nc, m, s)
            norms[3].act_sqrt(act, nc, m, s)
            norms[3].act_apply(act, nc, m, s, hH, gain(V_MIX), no_shift)
            mix.act(act, nc, m, s)
            norms[4].act_sqrt(act, nc, m, s)
            norms[4].act_apply(act, nc, m, s, hH, gain(V_FFN2), no_shift)
            ffn2.act(act, nc, m, s)

        @block.vector
        def _(dve):
            dve.sem_inc(s.ufree, 2)
            dve.sem_inc(s.y, 4)
            for d in range(KD):
                norms[0].dve_add(dve, nc, m, s, d)
            dve.wait_ge(s.vec, 16)
            dve_decay_rates(dve, nc, m, s)
            norms[0].dve_rsqrt(dve, nc, m, s)
            dve.wait_ge(s.spread, 1)
            for d in range(KD):
                nc.vector.scalar_tensor_tensor(out=m.x[:, d], in0=m.x[:, d], scalar=m.vec[:, V_FINAL + d:V_FINAL + d + 1],
                                               in1=m.bank[7][:], op0=ALU.mult, op1=ALU.mult).then_inc(s.y, 1)
            for d in range(KD):
                norms[1].dve_add(dve, nc, m, s, d)
            norms[1].dve_rsqrt(dve, nc, m, s)
            norms[1].dve_apply(dve, nc, m, s, lambda k: memH[:, k], lambda k: memL[:, k])
            for n in (2, 3, 4):
                if n == 2:
                    for d in range(KD):
                        norms[n].dve_add(dve, nc, m, s, d)
                norms[n].dve_rsqrt(dve, nc, m, s)
                norms[n].dve_apply(dve, nc, m, s, hH, hL)
                if n == 2:
                    ffn1.dve(dve, nc, m, s, half)
                elif n == 3:
                    mix.dve(dve, nc, m, s)
                else:
                    ffn2.dve(dve, nc, m, s, half)

        @block.tensor
        def _(pe):
            pe.sem_inc(s.mm, 4)
            for n in range(2):
                norms[n].pe_sum(pe, nc, m, s)
                norms[n].pe_spread(pe, nc, m, s)
            mem = lambda k: (memH[:, k], memL[:, k])
            pe_tiles(pe, nc, m, s, 0, 0, [m.bank[0][:, 0:256], m.bank[1][:, 0:256]], mem, KD,
                     lambda k: pe.wait_ge(s.hl, k + 1))
            pe_rows(pe, nc, m, s, 1, mem, [m.bank[2][:, 0:256], m.bank[3][:, 0:256]])
            norms[2].pe_sum(pe, nc, m, s)
            norms[2].pe_spread(pe, nc, m, s)
            pe.wait_ge(s.ev, 4)
            ffn1.pe(pe, nc, m, s)
            norms[3].pe_sum(pe, nc, m, s)
            norms[3].pe_spread(pe, nc, m, s)
            mix.pe(pe, nc, m, s)
            norms[4].pe_sum(pe, nc, m, s)
            norms[4].pe_spread(pe, nc, m, s)
            ffn2.pe(pe, nc, m, s)


def program(nc, a, layers=LAYERS, second=True, debug=None):
    m = memory(nc)
    setup_block(nc, m, a)
    s = signals(nc, "l", True)
    with nc.Fori(0, layers) as l:
        layer_block(nc, m, s, a, l)
    if second:
        second_block(nc, m, signals(nc, "s", False), a)
    if debug:
        st = nc.alloc_semaphore("dbg")
        with nc.Block() as block:
            @block.sync
            def _(sp):
                sp.dma_start(a["out"], m.x[:]).then_inc(st, 16)
                sp.wait_ge(st, 16)

def tiles_of(x):
    return np.ascontiguousarray(x.reshape(-1, P, x.shape[-1]).transpose(1, 0, 2))


def column(v, n):
    return np.ascontiguousarray(np.asarray(v).reshape(n, P).T)


def units(w):
    rows, cols = w.shape
    w = w.reshape(rows // P, P, cols // COLS, COLS).transpose(2, 1, 0, 3)
    return w.reshape(cols // COLS, P, -1)


def ffn_units(w_in, w_out):
    pairs = [units(w_in[:, :DFF]), units(w_in[:, DFF:])]
    both = np.stack(pairs, axis=1).reshape(IN_UNITS, P, UNIT)
    return both, units(w_out[:FT_A * P]), units(w_out[FT_A * P:])


def mix1_units(w_in, w_out):
    sgu = D // 2
    u, v_a, q, k, v = (w_in[:, i * sgu:(i + 1) * sgu] for i in range(5))
    at = 5 * sgu
    iq, ik, iw = w_in[:, at:at + 256], w_in[:, at + 256:at + 320], w_in[:, at + 320:at + 324]
    first = np.concatenate([ik, ik, iw, np.zeros((D, COLS - 132), w_in.dtype)], axis=1)
    return units(np.concatenate([first, iq, v_a, u, v, q, k, w_out], axis=1))


def mix2_units(w_in, w_out):
    x, g, q, k, v, cq = np.split(w_in, [512, 1024, 1280, 1536, 1792], axis=1)
    return units(np.concatenate([x, g, q, k, cq, v, w_out], axis=1))


def block_diagonal(w):
    out = np.zeros((P, 4, P), w.dtype)
    for n in range(8):
        lo = 64 * (n % 2)
        out[lo:lo + 64, n // 2, lo:lo + 64] = w[n]
    return out


def constants():
    c = np.zeros((P, C_WIDTH), np.float32)
    c[:, C_IDENT:C_IDENT + P] = np.eye(P)
    half = HD // 8
    for d in range(P):
        e = d % HD
        if e < half:
            c[d + half, C_PERM + d] = -1.0
        elif e < 2 * half:
            c[d - half, C_PERM + d] = 1.0
    q, k = np.arange(P)[:, None], np.arange(P)[None, :]
    c[:, C_TRI:C_TRI + P] = np.where(k <= q, BIG, BELOW)
    c[:HD, C_SEL] = 1.0
    c[HD:, C_SEL + 1] = 1.0
    inv = np.float32(500000.0) ** (-np.arange(0, 2 * half, 2, dtype=np.float32) / np.float32(2 * half))
    for d in range(P):
        if d % HD < 2 * half:
            c[d, C_FREQ] = inv[d % half]
    causal = np.where(k <= q, 0.0, NEG).astype(np.float32)
    alibi = np.zeros((P, MASKS), np.float32)
    for i in range(TT):
        keys = np.arange((i + 1) * P)[None, :]
        away = i * P + q - keys
        alibi[:, ALIBI_AT[i]:ALIBI_AT[i] + (i + 1) * P] = np.where(away >= 0, -8.0 * away, NEG)
    return c, causal, alibi


def lay_out(v):
    ffns = [ffn_units(v[f"ffn{n}_w_in"][l], v[f"ffn{n}_w_out"][l]) for l in range(LAYERS) for n in (1, 2)]
    ffns += [ffn_units(v[f"ffn{n}_w_in_2"][0], v[f"ffn{n}_w_out_2"][0]) for n in (1, 2)]
    cst, causal, alibi = constants()
    vec = [column(v["final_norm"], 8), column(v["mem_norm_2"][0], 8), column(v["ffn1_norm_2"][0], 8),
           column(v["mix_norm_2"][0], 8), column(v["ffn2_norm_2"][0], 8)]
    vec += [column(v["lru_conv_w_2"][0][j], 4) for j in range(4)]
    vec += [column(v["lru_conv_b_2"][0], 4), column(v["lru_a_b_2"][0].reshape(-1), 4),
            column(v["lru_x_b_2"][0].reshape(-1), 4), column(v["lru_lambda_2"][0], 4)]
    vec += [column(np.tile(v[n][0], 2), 1) for n in ("moba_q_norm_2", "moba_k_norm_2", "mem_q_norm_2", "mem_k_norm_2")]
    return {
        "x": tiles_of(v["x"][0].T),
        "c": column(v["c"][0], KD),
        "positions": v["positions"].reshape(1, T),
        "constants": cst, "causal": causal, "alibi": alibi,
        "ada_w": v["ada_w"].reshape(LAYERS, KD, P, N_MOD, D).transpose(0, 3, 1, 2, 4),
        "ada_b": v["ada_b"].reshape(LAYERS, N_MOD * KD, P).transpose(0, 2, 1),
        "gains": np.stack([np.concatenate([column(v[n][l], KD) for n in ("norm_ffn1", "norm_mix", "norm_ffn2")], axis=1)
                           for l in range(LAYERS)]),
        "ffn_in": np.concatenate([x[0] for x in ffns]),
        "ffn_out_a": np.concatenate([x[1] for x in ffns]),
        "ffn_out_b": np.concatenate([x[2] for x in ffns]),
        "mix": np.stack([mix1_units(v["mix_w_in"][l], v["mix_w_out"][l]) for l in range(LAYERS)]),
        "sgu_w": v["sgu_w"].transpose(0, 3, 1, 2),
        "sgu_b": v["sgu_b"].reshape(LAYERS, 1, 4, P),
        "mem": tiles_of(v["mem_2"][0].T),
        "mem_kv": units(v["mem_w_kv_2"][0]),
        "mix_2": mix2_units(v["w_in_2"][0], v["w_out_2"][0]),
        "vec": np.concatenate(vec, axis=1),
        "gate_w": np.stack([block_diagonal(v["lru_a_w_2"][0]), block_diagonal(v["lru_x_w_2"][0])], axis=1),
    }


def kernel(**inputs):
    import concourse.bacc as _bacc
    from concourse.bass_utils import run_bass_kernel_spmd as _run

    nc = _bacc.Bacc("TRN2", target_bir_lowering=False, num_devices=1)
    arrays, aps = {}, {}
    for name, x in lay_out({k: np.asarray(x) for k, x in inputs.items()}).items():
        x = np.ascontiguousarray(x)
        arrays[f"in_{name}"] = x
        aps[name] = nc.dram_tensor(f"in_{name}", x.shape, mybir.dt.from_np(x.dtype), kind="ExternalInput").ap()
    aps["out"] = nc.dram_tensor("out_0", (P, KD, T), F32, kind="ExternalOutput").ap()
    program(nc, aps)
    r = _run(nc, [arrays], core_ids=[0])
    got = r.results[0]["out_0"]
    return np.ascontiguousarray(got.transpose(1, 0, 2).reshape(D, T).T).reshape(1, T, D)
```

```python
import numpy as np

import concourse.bass as bass
from concourse import mybir
from concourse.alu_op_type import AluOpType as ALU

F32 = mybir.dt.float32
F32R = mybir.dt.float32r
I32 = mybir.dt.int32
ACT = mybir.ActivationFunctionType
AX = mybir.AxisListType

P = 128
D = 1024
T = 512
TT = T // P
KD = D // P
DFF = 2816
LAYERS = 2
COLS = 256
FT = DFF // P
FT_A = 12
FT_B = FT - FT_A
UNIT = KD * COLS
UNIT_A = FT_A * COLS
UNIT_B = FT_B * COLS
IN_UNITS = 2 * DFF // COLS
IN_A = 2 * FT_A // 2
IN_B = 2 * FT_B // 2
OUT_UNITS = D // COLS
FFN_UNITS = IN_UNITS + 2 * OUT_UNITS
N_MOD = 9
HD = 64
HEADS = 8
IDX_HEADS = 4
TOPK = T // 4
EPS = 1e-6
MOD_SLOTS = 2

MIX1_PROJ = 12
MIX2_PROJ = 8
MEM_UNITS = 2

L_FFN1 = 0
L_MIX = L_FFN1 + FFN_UNITS
L_FFN2 = L_MIX + MIX1_PROJ + OUT_UNITS
S_MEM = 0
S_FFN1 = S_MEM + MEM_UNITS
S_MIX = S_FFN1 + FFN_UNITS
S_FFN2 = S_MIX + MIX2_PROJ + OUT_UNITS

NEG = -1.0e30
BELOW = -3.0e38
TAKEN = -3.4e38
BIG = 3.0e38
MAGIC = 12582912.0
TWO_PI_PARTS = (6.28125, 0.001934051513671875, 1.2556659e-06)

C_IDENT, C_TRI, C_SEL, C_FREQ = 0, P, 2 * P, 2 * P + 2
C_WIDTH = 2 * P + 3
ALIBI_AT = [0, 128, 384, 768]
MASKS = 1280
V_FINAL, V_MEM, V_FFN1, V_MIX, V_FFN2 = 0, 8, 16, 24, 32
V_CONVW, V_CONVB, V_AB, V_XB, V_LAM, V_GAINS, V_WIDTH = 40, 56, 60, 64, 68, 72, 76


class Memory:
    pass


class Signals:
    pass


def memory(nc):
    m = Memory()
    base = -(-nc.sbuf_base // 32) * 32
    K = 1024

    def at(name, offset, shape, dt=F32):
        return nc.alloc_sbuf_tensor_at("m_" + name, [P] + shape, dt, offset=base + offset)

    m.x = at("x", 0, [KD, T])
    m.hH = at("hH", 16 * K, [KD, T], F32R)
    m.hL = at("hL", 32 * K, [KD, T], F32R)
    m.guH = at("guH", 48 * K, [FT_A, T], F32R)
    m.guL = at("guL", 72 * K, [FT_A, T], F32R)
    m.wraw = at("wraw", 96 * K, [2, UNIT_A])
    m.wH = at("wH", 120 * K, [2, UNIT_A], F32R)
    m.wL = at("wL", 144 * K, [2, UNIT_A], F32R)
    m.mod_big = at("mod_big", 48 * K, [4, 4, D])
    m.u = at("u", 56 * K, [4, T])
    m.va = at("va", 80 * K, [TT, T])
    m.lx = at("lx", 56 * K, [4, T])
    m.gl = at("gl", 80 * K, [4, T])
    m.xb = at("xb", 72 * K, [4, T])
    m.q = at("q", 64 * K, [4, T])
    m.k = at("k", 88 * K, [4, T])
    m.cq = at("cq", 88 * K, [2, T])
    m.gatew = at("gatew", 92 * K, [2, 4, P])
    spare = UNIT * 4
    m.other = [at(f"other{j}", 96 * K + j * UNIT_A * 4 + spare, [2, T]) for j in range(2)]
    m.lowA = [at(f"lowA{j}", 120 * K + j * UNIT_A * 4 + spare, [2, T], F32R) for j in range(2)]
    m.lowB = [at(f"lowB{j}", 144 * K + j * UNIT_A * 4 + spare, [2, T], F32R) for j in range(2)]
    m.memkL = at("memkL", 144 * K + UNIT_A * 4 + spare, [2, 256], F32R)
    m.qH = at("qH", 64 * K, [4, T], F32R)
    m.kH = at("kH", 88 * K, [4, T], F32R)
    m.cqH = at("cqH", 88 * K, [2, T], F32R)
    m.mem = at("mem", 72 * K, [KD, 256])
    m.sm = at("sm", 16 * K, [3, T])
    m.p = at("p", 22 * K, [3, T])
    m.pT = at("pT", 28 * K, [3, T])
    m.bn = at("bn", 34 * K, [2, T])
    m.hs = at("hs", 38 * K, [2, T])
    m.rx = at("rx", 42 * K, [2, T])
    m.mdh = at("mdh", 38 * K, [2, T])
    m.mn = at("mn", 46 * K, [32])
    m.sums = at("sums", 46 * K + 128, [32])
    m.rinv = at("rinv", 46 * K + 256, [32])
    m.hv = at("hv", 46 * K + 384, [56])
    m.hr = at("hr", 46 * K + 640, [56])
    m.ht = at("ht", 46 * K + 896, [56])
    o = 168 * K
    m.masks = at("masks", o, [MASKS]); o += 5 * K
    g = o
    m.sg = at("sg", g, [2, T])
    m.gut = at("gut", g + 4 * K, [2, T])
    m.t = at("t", g, [4, T])
    m.sq = at("sq", g + 8 * K, [2, T])
    m.acc = at("acc", g + 12 * K, [T])
    m.ix = at("ix", g, [3, T])
    m.ixH = at("ixH", g, [3, T], F32R)
    m.rl = at("rl", g + 6 * K, [2, T])
    m.ra = at("ra", g + 10 * K, [T])
    m.rb = at("rb", g + 12 * K, [T])
    m.rg = at("rg", g, [4, T])
    m.ig3 = at("ig3", g + 8 * K, [3, T])
    m.pos = at("pos", g, [T], I32)
    m.ang = at("ang", g + 2 * K, [T])
    m.turn = at("turn", g + 4 * K, [T])
    o += 14 * K
    a = o
    m.mod_w = at("mod_w", a, [MOD_SLOTS, D])
    m.mod_acc = at("mod_acc", a + 8 * K, [D])
    m.v = at("v", a, [TT, T])
    m.sguT = at("sguT", a + 8 * K, [4, P])
    m.sgub = at("sgub", a + 10 * K, [4, P])
    m.memk = at("memk", a, [2, 256])
    m.memkH = at("memkH", a, [2, 256], F32R)
    m.memv = at("memv", a + 2 * K, [2, 256])
    m.mv = at("mv", a + 4 * K, [TT, 256])
    m.la = at("la", a + 8 * K, [T])
    m.lb = at("lb", a + 10 * K, [T])
    o += 12 * K
    m.cos = at("cos", o, [T])
    m.sin = at("sin", o + 2 * K, [T])
    m.none = at("none", o + 2 * K, [256])
    m.ig1 = at("ig1", o, [1, T])
    o += 4 * K
    def small(name, shape, dt=F32):
        nonlocal o
        here, o = o, o + -(-int(np.prod(shape)) * 4 // 32) * 32
        return at(name, here, shape, dt)

    m.vec = at("vec", o, [V_WIDTH])
    m.mod = small("mod", [(N_MOD + 2) * KD])
    m.mod_b = small("mod_b", [N_MOD * KD])
    m.cst = small("cst", [C_WIDTH])
    m.ones = small("ones", [P])
    m.warm = small("warm", [P], F32R)
    m.gains = small("gains", [3 * KD])
    m.A = small("A", [KD])
    m.gate = small("gate", [KD])
    m.csil = small("csil", [KD])
    m.zero = small("zero", [1])
    m.halfpi = small("halfpi", [1])
    m.wi = small("wi", [4 * TT])
    m.m8 = small("m8", [8])
    m.nv = small("nv", [TT])
    m.nr = small("nr", [TT])
    m.nt = small("nt", [TT])
    m.sp = small("sp", [6, 4])
    assert base + o <= nc.sbuf_usable_end, (base + o, nc.sbuf_usable_end)
    m.ident = m.cst[:, C_IDENT:C_IDENT + P]
    m.tri = m.cst[:, C_TRI:C_TRI + P]
    m.sel = m.cst[:, C_SEL:C_SEL + 2]
    m.freq = m.cst[:, C_FREQ:C_FREQ + 1]
    m.one = m.ones[:, 0:1]
    m.bank = [nc.alloc_psum_tensor(f"bank{i}", [P, 512], F32) for i in range(8)]
    return m


def f(ap):
    return ap.bitcast(F32)



def sp_units(sp, m, s, src, u0, n, size):
    with sp.Fori(0, n // 2) as i:
        for j in range(2):
            sp.wait_ge(s.low, u0 + 2 * i + j + 1)
            sp.dma_start(m.wraw[:, j, 0:size], src(2 * i + j)).then_inc(s.full[j], 16)


def sp_unit(sp, m, s, src, u, size):
    sp.wait_ge(s.low, u + 1)
    sp.dma_start(m.wraw[:, u % 2, 0:size], src).then_inc(s.full[u % 2], 16)


def pool_low(pool, nc, m, s, u0, n, size):
    with pool.Fori(0, n // 2) as i:
        for j in range(2):
            pool.wait_ge(s.high, u0 + 2 * i + j + 1)
            nc.gpsimd.tensor_tensor(m.wL[:, j, 0:size], m.wraw[:, j, 0:size], f(m.wH[:, j, 0:size]), ALU.subtract)\
                .then_inc(s.low, 1)


def act_high(act, nc, m, s, u, j, pair, size):
    act.wait_ge(s.full[j], 16 * (pair + 1))
    act.wait_ge(s.mm, 2 * u + 2)
    nc.scalar.activation(m.wH[:, j, 0:size], m.wraw[:, j, 0:size], ACT.Copy).then_inc(s.high, 1)


def act_next(act, nc, m, s, u, size):
    if size:
        act_high(act, nc, m, s, u + 2, u % 2, (u + 2) // 2, size)


def keep_warm(nc, m, bank, n):
    for _ in range(n):
        nc.tensor.matmul(m.bank[bank][:], m.warm[:], m.warm[:].unsqueeze(1).to_broadcast([P, TT, P]), start=True, stop=True)


def pe_3(nc, out, a, b, first, last):
    nc.tensor.matmul(out, a[0], b[0], start=first, stop=False)
    nc.tensor.matmul(out, a[0], b[1], start=False, stop=False)
    return nc.tensor.matmul(out, a[1], b[0], start=False, stop=last)


def pe_tiles(pe, nc, m, s, u, slot, banks, right, rows, waits=None, by_row=False):
    pe.wait_ge(s.low, u + 3)
    order = [(k, j) for k in range(rows) for j in range(2)] if by_row else [(k, j) for j in range(2) for k in range(rows)]
    for n, (k, j) in enumerate(order):
        if waits and j == 0:
            waits(k)
        at = k * COLS + j * P
        w = m.wH[:, slot, at:at + P], m.wL[:, slot, at:at + P]
        mm = pe_3(nc, banks[j], w, right(k), k == 0, k == rows - 1)
        if k == rows - 1:
            mm.then_inc(s.mm, 1)


def pe_rows(pe, nc, m, s, u, left, outs):
    pe.wait_ge(s.low, u + 3)
    for tt, out in enumerate(outs):
        for k in range(KD):
            hi, lo = left(k)
            w = [x[:, u % 2, k * COLS:(k + 1) * COLS] for x in (m.wH, m.wL)]
            mm = pe_3(nc, out, (hi[:, tt * P:(tt + 1) * P], lo[:, tt * P:(tt + 1) * P]), w, k == 0, k == KD - 1)
        if tt % (len(outs) // 2) == len(outs) // 2 - 1:
            mm.then_inc(s.mm, 1)



class Norm:

    def __init__(self, n, a, y0=None, tokens=T, src=None, warm=(0, 8, 9), warm_bank=2):
        self.warm, self.warm_bank = warm, warm_bank
        self.n, self.a, self.y0, self.tokens, self.src = n, a, y0, tokens, src or (lambda m: m.x)

    def act_square(self, act, nc, m, s, d):
        n = self.n
        if self.y0 is not None:
            act.wait_ge(s.y, 4 + self.y0 + d + 1)
        if d >= 3:
            act.wait_ge(s.acc, 7 * n + d - 2)
        x = self.src(m)[:, d]
        out = m.acc[:, 0:self.tokens] if d == 0 else m.sq[:, d % 2, 0:self.tokens]
        nc.scalar.activation(out, x, ACT.Square).then_inc(s.sq, 1)

    def dve_add(self, dve, nc, m, s, d):
        if d == 0:
            return
        dve.wait_ge(s.sq, 8 * self.n + d + 1)
        dve.drain()
        w = self.tokens
        nc.vector.tensor_tensor(m.acc[:, 0:w], m.acc[:, 0:w], m.sq[:, d % 2, 0:w], ALU.add).then_inc(s.acc, 1)

    def pe_sum(self, pe, nc, m, s):
        keep_warm(nc, m, self.warm_bank, self.warm[0])
        pe.wait_ge(s.acc, 7 * self.n + 7)
        for tt in range(self.tokens // P):
            mm = nc.tensor.matmul(m.bank[6][:, tt:tt + 1], m.acc[:, tt * P:(tt + 1) * P], m.one, start=True, stop=True)
        mm.then_inc(s.ss, 1)
        keep_warm(nc, m, self.warm_bank, self.warm[1])

    def dve_rsqrt(self, dve, nc, m, s):
        tt = self.tokens // P
        v, r, t = m.nv[:, 0:tt], m.nr[:, 0:tt], m.nt[:, 0:tt]
        dve.wait_ge(s.ss, self.n + 1)
        dve.drain()
        nc.vector.tensor_scalar(v, m.bank[6][:, 0:tt], 1.0 / D, EPS, ALU.mult, ALU.add).then_inc(s.var, 1)
        newton(dve, nc, s.rt, self.n + 1, v, r, t).then_inc(s.dg, 1)

    def act_sqrt(self, act, nc, m, s):
        tt = self.tokens // P
        act.wait_ge(s.var, self.n + 1)
        nc.scalar.activation(m.nr[:, 0:tt], m.nv[:, 0:tt], ACT.Sqrt).then_inc(s.rt, 1)

    def pe_spread(self, pe, nc, m, s):
        pe.wait_ge(s.dg, self.n + 1)
        for tt in range(self.tokens // P):
            mm = nc.tensor.matmul(m.bank[7][:, tt * P:(tt + 1) * P], m.nr[:, tt:tt + 1].to_broadcast([P, P]), m.ident,
                                  start=True, stop=True)
        mm.then_inc(s.spread, 1)
        keep_warm(nc, m, self.warm_bank, self.warm[2])

    def dve_scale(self, dve, nc, m, s, k, scale):
        if k == 0:
            dve.wait_ge(s.spread, self.n + 1)
        if 8 * self.a + k >= 4:
            dve.wait_ge(s.hl, 8 * self.a + k - 3)
        w = self.tokens
        nc.vector.scalar_tensor_tensor(out=m.t[:, k % 4, 0:w], in0=self.src(m)[:, k], scalar=scale(k), in1=m.bank[7][:, 0:w],
                                       op0=ALU.mult, op1=ALU.mult).then_inc(s.tt, 1)

    def dve_low(self, dve, nc, m, s, k, hL, hH, shift):
        dve.wait_ge(s.hh, 8 * self.a + k + 1)
        t = m.t[:, k % 4, 0:self.tokens]
        if shift:
            nc.vector.scalar_tensor_tensor(out=hL, in0=t, scalar=shift(k), in1=f(hH), op0=ALU.add, op1=ALU.subtract)\
                .then_inc(s.hl, 1)
        else:
            nc.vector.tensor_tensor(hL, t, f(hH), ALU.subtract).then_inc(s.hl, 1)

    def dve_apply(self, dve, nc, m, s, hH, hL, scale, shift=None):
        self.dve_scale(dve, nc, m, s, 0, scale)
        self.dve_scale(dve, nc, m, s, 1, scale)
        for k in range(KD):
            self.dve_low(dve, nc, m, s, k, hL(k), hH(k), shift)
            if k + 2 < KD:
                self.dve_scale(dve, nc, m, s, k + 2, scale)

    def act_apply(self, act, nc, m, s, hH, shift=None):
        for k in range(KD):
            act.wait_ge(s.tt, 8 * self.a + k + 1)
            t = m.t[:, k % 4, 0:self.tokens]
            nc.scalar.activation(hH(k), t, ACT.Identity, bias=shift(k) if shift else m.zero[:]).then_inc(s.hh, 1)


BETWEEN = (18, 8, 9)


def newton(dve, nc, roots, count, v, r, t):
    dve.wait_ge(roots, count)
    nc.vector.reciprocal(r, r)
    dve.drain()
    nc.vector.scalar_tensor_tensor(out=t, in0=r, scalar=-0.5, in1=r, op0=ALU.mult, op1=ALU.mult)
    dve.drain()
    nc.vector.tensor_tensor(t, t, v, ALU.mult)
    dve.drain()
    return nc.vector.scalar_tensor_tensor(out=r, in0=t, scalar=1.5, in1=r, op0=ALU.add, op1=ALU.mult)



class Ffn:

    def __init__(self, n, u0, y0, norm, after, ahead):
        self.n, self.u0, self.y0, self.norm, self.after, self.ahead = n, u0, y0, norm, after, ahead
        self.ua, self.ub = u0 + IN_A, u0 + IN_A + OUT_UNITS
        self.uc = self.ub + IN_B
        self.f0 = FT * n

    def pe_group(self, pe, nc, m, s, u, f, waits=None):
        h = lambda k: (m.hH[:, k], m.hL[:, k])
        pe.wait_ge(s.silu, f + 2)
        pe_tiles(pe, nc, m, s, u, 0, [m.bank[0][:], m.bank[1][:]], h, KD, waits, by_row=waits is not None)
        pe.wait_ge(s.ufree, f + 2)
        pe_tiles(pe, nc, m, s, u + 1, 1, [m.bank[2][:], m.bank[3][:]], h, KD)

    def pe_out(self, pe, nc, m, s, u, rows, g0, y):
        gu = lambda k: (m.guH[:, k], m.guL[:, k])

        def waits(k):
            if k in (0, rows - 2, rows - 1):
                pe.wait_ge(s.gu, g0 + (rows - 2 if k == 0 else k + 1))
        with pe.Fori(0, OUT_UNITS // 2) as i:
            for q in range(2):
                pe.wait_ge(s.y, y + 4 * i + 2 * q + 2)
                pe_tiles(pe, nc, m, s, u + 2 * i + q, q, [m.bank[4 + 2 * q][:], m.bank[5 + 2 * q][:]], gu, rows, waits)

    def pe(self, pe, nc, m, s, mod=None):
        a = self.norm.a
        first = lambda k: pe.wait_ge(s.hl, 8 * a + k + 1)
        if not mod:
            self.pe_group(pe, nc, m, s, self.u0, self.f0, first)
            with pe.Fori(1, IN_A // 2) as i:
                self.pe_group(pe, nc, m, s, self.u0 + 2 * i, self.f0 + 2 * i)
        else:
            for g in range(2):
                self.pe_group(pe, nc, m, s, self.u0 + 2 * g, self.f0 + 2 * g, None if g else first)
            mod.pe_reduce(pe, nc, m, s, mod.in_a, 6)
            with pe.Fori(1, IN_A // 4) as i:
                for g in range(2):
                    self.pe_group(pe, nc, m, s, self.u0 + 4 * i + 2 * g, self.f0 + 4 * i + 2 * g)
                mod.pe_reduce(pe, nc, m, s, mod.in_a + i, 6)
            pe.wait_ge(s.mod_taken, mod.in_a + IN_A // 4)
        self.pe_out(pe, nc, m, s, self.ua, FT_A, self.f0, self.y0)
        if mod and mod.in_b is not None:
            pe.wait_ge(s.y, 4 + self.y0 + KD)
            with pe.Fori(0, IN_B // 4) as i:
                for g in range(2):
                    self.pe_group(pe, nc, m, s, self.ub + 4 * i + 2 * g, self.f0 + FT_A + 4 * i + 2 * g)
                mod.pe_reduce(pe, nc, m, s, mod.in_b + i, 6)
            self.pe_group(pe, nc, m, s, self.uc - 2, self.f0 + FT - 2)
            pe.wait_ge(s.mod_taken, mod.in_b + IN_B // 4)
            self.pe_out(pe, nc, m, s, self.uc, FT_B, self.f0 + FT_A, self.y0 + KD)
            mod.pe_reduce(pe, nc, m, s, mod.in_b + IN_B // 4, 0)
        else:
            with pe.Fori(0, IN_B // 2) as i:
                self.pe_group(pe, nc, m, s, self.ub + 2 * i, self.f0 + FT_A + 2 * i)
            self.pe_out(pe, nc, m, s, self.uc, FT_B, self.f0 + FT_A, self.y0 + KD)

    def act_group(self, act, nc, m, s, u, pair, f, size):
        for j in range(2):
            act.wait_ge(s.mm, 4 + 2 * u + j + 1)
            act.wait_ge(s.ufree, f + j + 1)
            nc.scalar.activation(m.sg[:, j], m.bank[j][:], ACT.Silu).then_inc(s.silu, 1)
        act_high(act, nc, m, s, u + 2, 0, pair + 1, size)
        act_high(act, nc, m, s, u + 3, 1, pair + 1, size)

    def act(self, act, nc, m, s):
        for u, n, f, after in ((self.u0, IN_A, self.f0, UNIT_A), (self.ub, IN_B, self.f0 + FT_A, UNIT_B)):
            with act.Fori(0, n // 2 - 1) as i:
                self.act_group(act, nc, m, s, u + 2 * i, u // 2 + i, f + 2 * i, UNIT)
            last = n - 2
            self.act_group(act, nc, m, s, u + last, (u + last) // 2, f + last, after)
            out = u + n
            for q in range(OUT_UNITS):
                size = after if q < OUT_UNITS - 2 else (UNIT if after == UNIT_A else self.ahead)
                act_next(act, nc, m, s, out + q, size)
                if after == UNIT_B and self.after:
                    self.after.act_square(act, nc, m, s, 2 * q)
                    self.after.act_square(act, nc, m, s, 2 * q + 1)

    def dve_group(self, dve, nc, m, s, u, f0, tile):
        for j in range(2):
            dve.drain()
            dve.wait_ge(s.silu, 2 + f0 + j + 1)
            dve.wait_ge(s.mm, 4 + 2 * u + 2 + j + 1)
            nc.vector.tensor_tensor(m.gut[:, j], m.sg[:, j], m.bank[2 + j][:], ALU.mult).then_inc(s.ufree, 1)
            dve.drain()
            nc.vector.tensor_copy(m.guH[:, tile + j], m.gut[:, j])
            dve.drain()
            nc.vector.tensor_tensor(m.guL[:, tile + j], m.gut[:, j], f(m.guH[:, tile + j]), ALU.subtract).then_inc(s.gu, 1)

    def dve(self, dve, nc, m, s, gate, mod=None, half_gate=None):
        if not mod:
            with dve.Fori(0, IN_A // 2) as i:
                self.dve_group(dve, nc, m, s, self.u0 + 2 * i, self.f0 + 2 * i, 2 * i)
        else:
            with dve.Fori(0, IN_A // 4) as i:
                for g in range(2):
                    mod.dve_half(dve, nc, m, s, mod.in_a, i, g)
                    self.dve_group(dve, nc, m, s, self.u0 + 4 * i + 2 * g, self.f0 + 4 * i + 2 * g, 4 * i + 2 * g)
                mod.dve_take(dve, nc, m, s, mod.in_a + i, 6)
        if half_gate is not None:
            dve_half_gate(dve, nc, m, half_gate)
        dve_update(dve, nc, m, s, self.ua, gate)
        if mod and mod.in_b is not None:
            last = IN_B // 4
            with dve.Fori(0, last) as i:
                for g in range(2):
                    mod.dve_half(dve, nc, m, s, mod.in_b, i, g)
                    self.dve_group(dve, nc, m, s, self.ub + 4 * i + 2 * g, self.f0 + FT_A + 4 * i + 2 * g, 4 * i + 2 * g)
                mod.dve_take(dve, nc, m, s, mod.in_b + i, 6)
            mod.dve_half(dve, nc, m, s, mod.in_b, last, 0)
            self.dve_group(dve, nc, m, s, self.uc - 2, self.f0 + FT - 2, FT_B - 2)
            mod.dve_half(dve, nc, m, s, mod.in_b, last, 1)
        else:
            with dve.Fori(0, IN_B // 2) as i:
                self.dve_group(dve, nc, m, s, self.ub + 2 * i, self.f0 + FT_A + 2 * i, 2 * i)
        dve_update(dve, nc, m, s, self.uc, gate, self.after)

    def sp(self, sp, m, s, w_in, w_a, w_b, mod=None):
        def pairs(u, src, n):
            with sp.Fori(0, n) as i:
                for g in range(2):
                    for j in range(2):
                        sp.wait_ge(s.low, u + 4 * i + 2 * g + j + 1)
                        sp.dma_start(m.wraw[:, j, 0:UNIT], src(4 * i + 2 * g + j)).then_inc(s.full[j], 16)
                    mod.sp_half(sp, m, s, first, i, g)
        if mod:
            first = mod.in_a
            pairs(self.u0, w_in, IN_A // 4)
        else:
            sp_units(sp, m, s, w_in, self.u0, IN_A, UNIT)
        sp_units(sp, m, s, w_a, self.ua, OUT_UNITS, UNIT_A)
        if mod and mod.in_b is not None:
            first = mod.in_b
            pairs(self.ub, lambda i: w_in(IN_A + i), IN_B // 4)
            sp_units(sp, m, s, lambda i: w_in(IN_UNITS - 2 + i), self.uc - 2, 2, UNIT)
            mod.sp_half(sp, m, s, first, IN_B // 4, 0)
            sp_unit(sp, m, s, w_b(0), self.uc, UNIT_B)
            sp_unit(sp, m, s, w_b(1), self.uc + 1, UNIT_B)
            mod.sp_half(sp, m, s, first, IN_B // 4, 1)
            sp_unit(sp, m, s, w_b(2), self.uc + 2, UNIT_B)
            sp_unit(sp, m, s, w_b(3), self.uc + 3, UNIT_B)
        else:
            sp_units(sp, m, s, lambda i: w_in(IN_A + i), self.ub, IN_B, UNIT)
            sp_units(sp, m, s, w_b, self.uc, OUT_UNITS, UNIT_B)


def dve_half_gate(dve, nc, m, chunk):
    dve.drain()
    nc.vector.tensor_scalar(m.gate[:], m.mod[:, chunk * KD:(chunk + 1) * KD], 0.5, None, ALU.mult)
    dve.drain()


def dve_update(dve, nc, m, s, u, gate, after=None):
    dve.drain()
    for d in range(KD):
        dve.wait_ge(s.mm, 4 + 2 * u + d + 1)
        nc.vector.scalar_tensor_tensor(out=m.x[:, d], in0=m.bank[4 + d % 4][:], scalar=gate(d), in1=m.x[:, d],
                                       op0=ALU.mult, op1=ALU.add).then_inc(s.y, 1)
        if after and d % 2:
            after.dve_add(dve, nc, m, s, d - 1)
            after.dve_add(dve, nc, m, s, d)



class Modulation:

    def __init__(self, w, in_a, in_b):
        self.w, self.in_a, self.in_b = w, in_a, in_b

    def sp_half(self, sp, m, s, first, i, g):
        for k in range(4):
            n = KD * first + 4 * g + k
            sp.wait_ge(s.mod_used, KD * i + n + 1)
            sp.dma_start(m.mod_w[:, k % 2], self.w[first + i, 4 * g + k]).then_inc(s.mod_full[k % 2], 16)

    def dve_half(self, dve, nc, m, s, first, i, g):
        for k in range(4):
            dve.drain()
            dve.wait_ge(s.mod_full[k % 2], 16 * (4 * (first + i) + 2 * g + k // 2 + 1))
            mod_add(nc, m, m.mod_w[:, k % 2], 4 * g + k).then_inc(s.mod_used, 1)

    def pe_reduce(self, pe, nc, m, s, c, bank):
        pe.wait_ge(s.mod_used, KD * (c + 1) + 2)
        mod_reduce(nc, m, bank).then_inc(s.mod_mm, 1)

    def dve_take(self, dve, nc, m, s, c, bank):
        dve.wait_ge(s.mod_mm, c + 1)
        at = c * KD
        nc.vector.tensor_tensor(m.mod[:, bass.ds(at + 2 * KD, KD)], m.bank[bank][:, 8:8 + KD], m.mod_b[:, bass.ds(at, KD)],
                                ALU.add).then_inc(s.mod_taken, 1)


def mod_add(nc, m, w, k):
    if k == 0:
        return nc.vector.tensor_scalar(m.mod_acc[:], w, m.csil[:, 0:1], None, ALU.mult)
    return nc.vector.scalar_tensor_tensor(out=m.mod_acc[:], in0=w, scalar=m.csil[:, k:k + 1], in1=m.mod_acc[:],
                                          op0=ALU.mult, op1=ALU.add)


def mod_reduce(nc, m, bank):
    for j in range(KD):
        mm = nc.tensor.matmul(m.bank[bank][:, 8 + j:9 + j], m.mod_acc[:, j * P:(j + 1) * P], m.one, start=True, stop=True)
    return mm



WARM = (2, 2, 1, 1)


class Attention:

    N = TT * HEADS

    def __init__(self, head, value, cadd=None):
        self.head, self.value = head, value

    def steps(self, n, *stages):
        for lag, stage in stages:
            if 0 <= n - lag < self.N:
                stage(n - lag)

    def of(self, n):
        q, k, mask, tiles = self.head(n % HEADS, n // HEADS)
        return q, k, mask, tiles * P, tiles

    def pe(self, pe, nc, m, s):
        def scores(n):
            q, k, _, w, _ = self.of(n)
            if n >= 3:
                pe.wait_ge(s.sm, n - 2)
            keep_warm(nc, m, 2 + n % 3, WARM[n // HEADS])
            pe_3(nc, m.bank[2 + n % 3][:, 0:w], q, k, True, True).then_inc(s.sc, 1)

        def turn(n):
            _, _, _, w, tiles = self.of(n)
            pe.wait_ge(s.ex, n + 1)
            if n >= 3:
                pe.wait_ge(s.pc, n - 2)
            for b in range(tiles):
                mm = nc.tensor.transpose(m.bank[5 + n % 3][:, b * P:(b + 1) * P], m.p[:, n % 3, b * P:(b + 1) * P], m.ident)
            mm.then_inc(s.tr, 1)

        def product(n):
            i, h = n // HEADS, n % HEADS
            _, _, _, w, tiles = self.of(n)
            if h == 0 and i >= 2:
                pe.wait_ge(s.cl, i - 1)
            pe.wait_ge(s.pc, n + 1)
            for b in range(tiles):
                mm = nc.tensor.matmul(m.bank[i % 2][:, h * HD:(h + 1) * HD], m.pT[:, n % 3, b * P:(b + 1) * P],
                                      self.value(h, b), start=(b == 0), stop=(b == tiles - 1))
            mm.then_inc(s.av, 1)

        def out(n):
            if n % HEADS == HEADS - 1:
                i = n // HEADS
                pe.wait_ge(s.on, i + 1)
                for d in range(4):
                    mm = nc.tensor.transpose(m.bank[i % 2][:, d * P:(d + 1) * P], m.bn[:, i % 2, d * P:(d + 1) * P], m.ident)
                mm.then_inc(s.bt, 1)
        for n in range(self.N + 4):
            self.steps(n, (0, scores), (1, turn), (2, product), (4, out))

    def dve(self, dve, nc, m, s, premask=None):
        def mask(n):
            q, k, mask, w, _ = self.of(n)
            dve.wait_ge(s.sc, n + 1)
            if n >= 3:
                dve.wait_ge(s.ex, n - 2)
            if premask:
                premask(n)
            nc.vector.tensor_tensor_reduce(out=m.sm[:, n % 3, 0:w], in0=m.bank[2 + n % 3][:, 0:w], in1=mask,
                                           scale=-(HD ** -0.5), scalar=BIG, op0=ALU.add, op1=ALU.min,
                                           accum_out=m.mn[:, n:n + 1]).then_inc(s.sm, 1)

        def copy(n):
            w = self.of(n)[3]
            dve.wait_ge(s.tr, n + 1)
            if n >= 3:
                dve.wait_ge(s.av, n - 2)
            nc.vector.tensor_copy(m.pT[:, n % 3, 0:w], m.bank[5 + n % 3][:, 0:w]).then_inc(s.pc, 1)

        def normalize(n):
            if n % HEADS == HEADS - 1:
                i = n // HEADS
                r = m.rinv[:, i * HEADS:(i + 1) * HEADS]
                dve.wait_ge(s.av, n + 1)
                nc.vector.reciprocal(r, m.sums[:, i * HEADS:(i + 1) * HEADS])
                dve.drain()
                if i >= 2:
                    dve.wait_ge(s.bt, i - 1)
                nc.vector.tensor_tensor(m.bn[:, i % 2].rearrange("p (h e) -> p h e", h=HEADS),
                                        m.bank[i % 2][:].rearrange("p (h e) -> p h e", h=HEADS),
                                        r.unsqueeze(2).to_broadcast([P, HEADS, HD]), ALU.mult).then_inc(s.on, 1)

        def low(n):
            if n % HEADS == HEADS - 1:
                i = n // HEADS
                dve.wait_ge(s.ch, i + 1)
                nc.vector.tensor_tensor(m.guL[:, 4:8, i * P:(i + 1) * P], m.bank[i % 2][:].rearrange("p (d t) -> p d t", d=4),
                                        f(m.guH[:, 4:8, i * P:(i + 1) * P]), ALU.subtract).then_inc(s.cl, 1)
        for n in range(self.N + 6):
            self.steps(n, (0, mask), (1, copy), (2, normalize), (5, low))

    def act(self, act, nc, m, s):
        def exponential(n):
            w = self.of(n)[3]
            act.wait_ge(s.sm, n + 1)
            if n >= 3:
                act.wait_ge(s.tr, n - 2)
            nc.scalar.activation(m.p[:, n % 3, 0:w], m.sm[:, n % 3, 0:w], ACT.Exp, scale=-1.0, bias=m.mn[:, n:n + 1],
                                 accum_out=m.sums[:, n:n + 1]).then_inc(s.ex, 1)

        def high(n):
            if n % HEADS == HEADS - 1:
                i = n // HEADS
                act.wait_ge(s.bt, i + 1)
                nc.scalar.activation(m.guH[:, 4:8, i * P:(i + 1) * P], m.bank[i % 2][:].rearrange("p (d t) -> p d t", d=4),
                                     ACT.Copy).then_inc(s.ch, 1)
        for n in range(self.N + 5):
            self.steps(n, (0, exponential), (4, high))


def pair(t, h, at, n):
    return t[64 * (h % 2):64 * (h % 2) + 64, h // 2, at:at + n]


def low_pair(t, h, at, n):
    return pair(t[h // 4], h % 4, at, n)


def dve_split(dve, nc, x, high, low):
    dve.drain()
    nc.vector.tensor_copy(high, x)
    dve.drain()
    return nc.vector.tensor_tensor(low, x, f(high), ALU.subtract)


class Projections:

    def __init__(self, m, u0, ev0, a):
        self.m, self.u0, self.ev0, self.a = m, u0, ev0, a

    def h(self, k):
        return self.m.hH[:, k], self.m.hL[:, k]

    def banks(self, pe, s, n):
        if n >= 2:
            pe.wait_ge(s.ev, self.ev0 + 2 * n - 2)
        return [self.m.bank[2 * (n % 2) + j][:] for j in range(2)]

    def pe_first(self, pe, s, k):
        pe.wait_ge(s.hl, 8 * self.a + k + 1)

    def pe_tiles(self, pe, nc, s, n, waits=None):
        pe_tiles(pe, nc, self.m, s, self.u0 + n, n % 2, self.banks(pe, s, n), self.h, KD, waits)

    def pe_rows(self, pe, nc, s, n):
        banks = self.banks(pe, s, n)
        outs = [banks[tt // 2][:, (tt % 2) * COLS:(tt % 2 + 1) * COLS] for tt in range(TT)]
        pe_rows(pe, nc, self.m, s, self.u0 + n, self.h, outs)

    def take(self, act, nc, s, n, outs, func=ACT.Copy):
        act_next(act, nc, self.m, s, self.u0 + n, UNIT)
        for j, (out, bank) in enumerate(outs):
            act.wait_ge(s.mm, 4 + 2 * (self.u0 + n) + j + 1)
            nc.scalar.activation(out, bank, func).then_inc(s.ev, 1)

    def cols(self, act, nc, s, n, t, c, func=ACT.Copy):
        self.take(act, nc, s, n, [(t[:, 2 * c + j], self.m.bank[2 * (n % 2) + j][:]) for j in range(2)], func)

    def rows(self, act, nc, s, n, t, c, func=ACT.Copy):
        self.take(act, nc, s, n, [(t[:, 2 * j:2 * j + 2, c * COLS:(c + 1) * COLS],
                                   self.m.bank[2 * (n % 2) + j][:].rearrange("p (t n) -> p t n", t=2))
                                  for j in range(2)], func)



class Mix1:

    def __init__(self, u0, y0, norm, after):
        self.u0, self.y0, self.norm, self.after = u0, y0, norm, after
        self.index = [(i, h) for i in range(1, TT) for h in range(IDX_HEADS)]

        def head(h, i):
            m = self.m
            return ((pair(m.qH, h, i * P, P), low_pair(m.lowA, h, i * P, P)),
                    (pair(m.kH, h, 0, (i + 1) * P), low_pair(m.lowB, h, 0, (i + 1) * P)),
                    m.masks[:, ALIBI_AT[i]:ALIBI_AT[i] + (i + 1) * P], i + 1)
        self.attention = Attention(head, lambda h, b: self.m.v[:, b, h * HD:(h + 1) * HD])

    def pe(self, pe, nc, m, s):
        self.m = m
        u0 = self.u0
        proj = Projections(m, u0, 0, self.norm.a)
        h, tiles, rows = proj.h, (lambda n: proj.pe_tiles(pe, nc, s, n)), (lambda n: proj.pe_rows(pe, nc, s, n))

        pe.wait_ge(s.mod_taken, 6)
        proj.pe_tiles(pe, nc, s, 0, lambda k: proj.pe_first(pe, s, k))
        tiles(1)
        pe.wait_ge(s.ev, 2)
        for tt in range(TT):
            mm = nc.tensor.transpose(m.bank[7][:, tt * IDX_HEADS:(tt + 1) * IDX_HEADS], m.rl[0:IDX_HEADS, 0, tt * P:(tt + 1) * P],
                                     m.ident[0:IDX_HEADS, 0:IDX_HEADS])
        mm.then_inc(s.wt, 1)
        rows(2)
        rows(3)
        pe.wait_ge(s.rope, 3)
        for n, (i, hh) in enumerate(self.index):
            if n == 3:
                pe.wait_ge(s.wtd, 1)
            if n >= 4:
                pe.wait_ge(s.relu, n - 3)
            lo, w = 64 * (hh % 2), (i + 1) * P
            pe_3(nc, m.bank[4 + n % 4][:, 0:w], (pair(m.ixH, hh, i * P, P), pair(m.lowB[0], hh, i * P, P)),
                 (m.ixH[lo:lo + 64, 2, 0:w], m.lowB[1][lo:lo + 64, 0, 0:w]), True, True).then_inc(s.lg, 1)
        tiles(4)
        tiles(5)
        pe.wait_ge(s.sgw, 1)
        pe.wait_ge(s.relu, len(self.index))
        for g in range(4):
            for c in range(TT):
                nc.tensor.matmul(m.bank[4 + g][:, c * P:(c + 1) * P], m.ones[0:1, :], m.sgub[0:1, g], start=True, stop=False)
                mm = nc.tensor.matmul(m.bank[4 + g][:, c * P:(c + 1) * P], m.va[:, c, g * P:(g + 1) * P], m.sguT[:, g],
                                      start=False, stop=True)
            mm.then_inc(s.sgu, 1)
        for n in range(6, 10):
            tiles(n)
        rows(10)
        rows(11)
        pe.wait_ge(s.ev, 24)
        pe.wait_ge(s.ao, 4)
        pe.wait_ge(s.rope, 11)
        self.attention.pe(pe, nc, m, s)
        pe_mixed_out(pe, nc, m, s, u0 + MIX1_PROJ, self.y0)

    def act(self, act, nc, m, s):
        self.m = m
        u0 = self.u0
        proj = Projections(m, u0, 0, self.norm.a)
        cols = lambda n, t, c, func=ACT.Copy: proj.cols(act, nc, s, n, t, c, func)
        rows = lambda n, t, c, func=ACT.Copy: proj.rows(act, nc, s, n, t, c, func)
        proj.take(act, nc, s, 0, [(m.ix[:, 2], m.bank[0][:]), (m.rl[:, 0], m.bank[1][:])])
        cols(1, m.ix, 0)
        rows(2, m.va, 0, ACT.Gelu)
        rows(3, m.va, 1, ACT.Gelu)
        act.wait_ge(s.wtd, 1)
        for n, (i, hh) in enumerate(self.index):
            act.wait_ge(s.lg, n + 1)
            if n >= 2:
                act.wait_ge(s.lacc, n - 1)
            w = (i + 1) * P
            nc.scalar.activation(m.rl[:, n % 2, 0:w], m.bank[4 + n % 4][:, 0:w], ACT.Relu).then_inc(s.relu, 1)
        cols(4, m.u, 0, ACT.Gelu)
        cols(5, m.u, 1, ACT.Gelu)
        cols(6, m.q, 0)
        cols(7, m.q, 1)
        cols(8, m.k, 0)
        cols(9, m.k, 1)
        rows(10, m.v, 0)
        rows(11, m.v, 1)
        self.attention.act(act, nc, m, s)
        act_mixed_out(act, nc, m, s, u0 + MIX1_PROJ, self.after)

    def dve(self, dve, nc, m, s, gate):
        self.m = m

        def rotate(x, other, high, low):
            dve.drain()
            nc.vector.tensor_tensor(m.ra[:], x, m.cos[:], ALU.mult)
            nc.vector.tensor_tensor(m.rb[:], other, m.sin[:], ALU.mult)
            dve.drain()
            nc.vector.tensor_tensor(m.ra[:], m.ra[:], m.rb[:], ALU.add)
            dve_split(dve, nc, m.ra[:], high, low).then_inc(s.rope, 1)
        dve.wait_ge(s.swap[0], 16 * 8)
        for j in (2, 0, 1):
            rotate(m.ix[:, j], m.other[j // 2][:, j % 2], m.ixH[:, j], m.lowB[j // 2][:, j % 2])
        dve.wait_ge(s.wt, 1)
        nc.vector.tensor_copy(m.wi[:], m.bank[7][:, 0:IDX_HEADS * TT]).then_inc(s.wtd, 1)
        score = [m.masks[:, ALIBI_AT[i]:ALIBI_AT[i] + (i + 1) * P] for i in range(TT)]
        for n, (i, hh) in enumerate(self.index):
            dve.wait_ge(s.relu, n + 1)
            w = m.wi[:, 4 * i + hh:4 * i + hh + 1]
            dve.drain()
            if hh == 0:
                nc.vector.tensor_scalar(score[i], m.rl[:, n % 2, 0:(i + 1) * P], w, None, ALU.mult).then_inc(s.lacc, 1)
            else:
                nc.vector.scalar_tensor_tensor(out=score[i], in0=m.rl[:, n % 2, 0:(i + 1) * P], scalar=w, in1=score[i],
                                               op0=ALU.mult, op1=ALU.add).then_inc(s.lacc, 1)
            if hh == IDX_HEADS - 1:
                dve.drain()
                diagonal = score[i][:, i * P:(i + 1) * P]
                nc.vector.tensor_tensor(diagonal, diagonal, m.tri, ALU.min)
        for i in range(1, TT):
            for _ in range(TOPK // 8):
                dve.drain()
                nc.vector.max(m.m8[:], score[i])
                dve.drain()
                nc.vector.match_replace(score[i], m.m8[:], score[i], TAKEN)
            dve.drain()
            nc.vector.tensor_scalar(score[i], score[i], (BELOW + TAKEN) / 2, NEG, ALU.is_gt, ALU.mult)
        dve.wait_ge(s.ev, 12)
        for g in range(4):
            dve.wait_ge(s.sgu, g + 1)
            dve.drain()
            nc.vector.tensor_tensor(m.ra[:], m.u[:, g], m.bank[4 + g][:], ALU.mult).then_inc(s.ao, 1)
            dve_split(dve, nc, m.ra[:], m.guH[:, g], m.guL[:, g])
        for n, (x, high, low) in enumerate(((m.q, m.qH, m.lowA), (m.k, m.kH, m.lowB))):
            dve.wait_ge(s.swap[1 + n], 16 * 8)
            for j in range(4):
                rotate(x[:, j], m.other[j // 2][:, j % 2], high[:, j], low[j // 2][:, j % 2])
        self.attention.dve(dve, nc, m, s)
        dve_update(dve, nc, m, s, self.u0 + MIX1_PROJ, gate, self.after)



class Mix2:

    CHAIN = 8

    def __init__(self, u0, y0, norm, after):
        self.u0, self.y0, self.norm, self.after = u0, y0, norm, after

        def head(h, i):
            m = self.m
            if h < 4:
                return ((pair(m.qH, h, i * P, P), low_pair(m.lowA, h, i * P, P)),
                        (pair(m.qH, h + 4, 0, (i + 1) * P), low_pair(m.lowA, h + 4, 0, (i + 1) * P)),
                        m.mdh[:, h % 2, 0:(i + 1) * P], i + 1)
            return ((pair(m.cqH, h - 4, i * P, P), pair(m.lowB[0], h - 4, i * P, P)),
                    (pair(m.memkH, h - 4, 0, 256), pair(m.memkL, h - 4, 0, 256)), m.none[:], 2)

        def value(h, b):
            return self.m.mv[:, b, h * HD:(h + 1) * HD] if h < 4 else self.m.memv[:, b, (h - 4) * HD:(h - 3) * HD]
        self.attention = Attention(head, value)

    def chain(self, r):
        m = self.m
        x = m.q[:, r] if r < 4 else (m.cq[:, r - 4] if r < 6 else m.memk[:, r - 6])
        return x, (4 if r < 6 else 2), (8 * r if r < 7 else 52)

    def parts(self, r):
        m = self.m
        if r < 4:
            return m.qH[:, r], m.lowA[r // 2][:, r % 2]
        return (m.cqH[:, r - 4], m.lowB[0][:, r - 4]) if r < 6 else (m.memkH[:, r - 6], m.memkL[:, r - 6])

    def pe(self, pe, nc, m, s):
        self.m = m
        proj = Projections(m, self.u0, 4, self.norm.a)
        proj.pe_tiles(pe, nc, s, 0, lambda k: proj.pe_first(pe, s, k))
        for n in range(1, 5):
            proj.pe_tiles(pe, nc, s, n)
        pe.wait_ge(s.gw, 16)
        for g in range(2):
            for c in range(4):
                pe.wait_ge(s.xb, c + 1)
                if g:
                    pe.wait_ge(s.sgm, c + 1)
                nc.tensor.matmul(m.bank[4 + c][:], m.gatew[:, g, c], m.xb[:, c], start=True, stop=True).then_inc(s.ga, 1)
        for n in range(5, 7):
            proj.pe_tiles(pe, nc, s, n)
        proj.pe_rows(pe, nc, s, 7)
        pe.wait_ge(s.sgm, 8)
        for r in range(self.CHAIN):
            _, tiles, at = self.chain(r)
            pe.wait_ge(s.hsq, r + 1)
            for tt in range(tiles):
                mm = nc.tensor.matmul(m.bank[4][:, at + 2 * tt:at + 2 * tt + 2], m.hs[:, r % 2, tt * P:(tt + 1) * P], m.sel,
                                      start=True, stop=True)
            mm.then_inc(s.hss, 1)
        for r in range(self.CHAIN):
            pe.wait_ge(s.rxd, r + 1)
            if r >= 2:
                pe.wait_ge(s.hq, r - 1)
            for tt in range(self.chain(r)[1]):
                mm = nc.tensor.transpose(m.bank[5 + r % 2][:, tt * P:(tt + 1) * P], m.rx[:, r % 2, tt * P:(tt + 1) * P],
                                         m.ident)
            mm.then_inc(s.hx, 1)
        pe.wait_ge(s.hq, self.CHAIN)
        pe.wait_ge(s.ev, 20)
        self.attention.pe(pe, nc, m, s)
        pe_mixed_out(pe, nc, m, s, self.u0 + MIX2_PROJ, self.y0)

    def act(self, act, nc, m, s):
        self.m = m
        proj = Projections(m, self.u0, 4, self.norm.a)
        ig = self.input_gate
        proj.cols(act, nc, s, 0, m.lx, 0)
        proj.cols(act, nc, s, 1, m.lx, 1)
        proj.cols(act, nc, s, 2, m.gl, 0, ACT.Gelu_apprx_tanh)
        proj.cols(act, nc, s, 3, m.gl, 1, ACT.Gelu_apprx_tanh)
        proj.cols(act, nc, s, 4, m.q, 0)
        for c in range(4):
            act.wait_ge(s.ga, c + 1)
            nc.scalar.activation(m.rg[:, c], m.bank[4 + c][:], ACT.Sigmoid, bias=m.vec[:, V_AB + c:V_AB + c + 1])\
                .then_inc(s.sgm, 1)
        for c in range(4):
            act.wait_ge(s.ga, 4 + c + 1)
            nc.scalar.activation(ig(c), m.bank[4 + c][:], ACT.Sigmoid, bias=m.vec[:, V_XB + c:V_XB + c + 1])\
                .then_inc(s.sgm, 1)
        proj.cols(act, nc, s, 5, m.q, 1)
        act.wait_ge(s.c8, 1)
        for c in range(4):
            nc.scalar.activation(m.lx[:, c], m.rg[:, c], ACT.Exp, scale=m.sp[:, 4, c:c + 1]).then_inc(s.et, 1)
        for c in range(4):
            act.wait_ge(s.et, c + 1)
            nc.scalar.activation(m.rg[:, c], m.rg[:, c], ACT.Tanh, scale=m.sp[:, 5, c:c + 1]).then_inc(s.et, 1)
        proj.cols(act, nc, s, 6, m.cq, 0)
        for c in range(4):
            act.wait_ge(s.m2, c + 1)
            nc.scalar.activation(m.rg[:, c], m.rg[:, c], ACT.Sqrt).then_inc(s.mult, 1)
        proj.rows(act, nc, s, 7, m.mv, 0)
        for r in range(self.CHAIN):
            x, tiles, _ = self.chain(r)
            if r >= 2:
                act.wait_ge(s.hss, r - 1)
            act.wait_ge(s.ev, 20)
            nc.scalar.activation(m.hs[:, r % 2, 0:tiles * P], x, ACT.Square).then_inc(s.hsq, 1)
        act.wait_ge(s.hvar, 1)
        nc.scalar.activation(m.hr[:], m.hv[:], ACT.Sqrt).then_inc(s.hrt, 1)
        self.attention.act(act, nc, m, s)
        act_mixed_out(act, nc, m, s, self.u0 + MIX2_PROJ, self.after)

    def input_gate(self, c):
        return self.m.ig3[:, c] if c < 3 else self.m.ig1[:, 0]

    def dve(self, dve, nc, m, s):
        self.m = m
        vec = lambda at: m.vec[:, at:at + 1]
        for c in range(4):
            dve.wait_ge(s.ev, 4 + c + 1)
            nc.vector.tensor_scalar(m.xb[:, c], m.lx[:, c], vec(V_CONVW + 12 + c), vec(V_CONVB + c), ALU.mult, ALU.add)
            for back in range(1, 4):
                dve.drain()
                mm = nc.vector.scalar_tensor_tensor(out=m.xb[:, c, back:], in0=m.lx[:, c, 0:T - back],
                                                    scalar=vec(V_CONVW + 4 * (3 - back) + c), in1=m.xb[:, c, back:],
                                                    op0=ALU.mult, op1=ALU.add)
            mm.then_inc(s.xb, 1)
        for c in range(4):
            dve.drain()
            dve.wait_ge(s.et, 4 + c + 1)
            nc.vector.tensor_tensor(m.la[:], m.lx[:, c], m.lx[:, c], ALU.mult)
            dve.drain()
            nc.vector.scalar_tensor_tensor(out=m.rg[:, c], in0=m.la[:], scalar=1.0, in1=m.rg[:, c], op0=ALU.add,
                                           op1=ALU.mult).then_inc(s.m2, 1)
        dve.wait_ge(s.sgm, 8)
        for c in range(4):
            dve.drain()
            nc.vector.tensor_tensor(m.la[:], m.xb[:, c], self.input_gate(c), ALU.mult)
            dve.wait_ge(s.mult, c + 1)
            nc.vector.memset(m.rg[:, c, 0:1], 1.0)
            dve.drain()
            nc.vector.tensor_tensor(m.la[:], m.la[:], m.rg[:, c], ALU.mult)
            dve.drain()
            nc.vector.tensor_tensor_scan(m.lb[:], m.lx[:, c], m.la[:], 0.0, ALU.mult, ALU.add)
            dve.drain()
            dve.wait_ge(s.ev, 8 + c + 1)
            nc.vector.tensor_tensor(m.la[:], m.lb[:], m.gl[:, c], ALU.mult)
            dve.drain()
            nc.vector.tensor_copy(m.guH[:, c], m.la[:])
            dve.drain()
            nc.vector.tensor_tensor(m.guL[:, c], m.la[:], f(m.guH[:, c]), ALU.subtract)
        dve.wait_ge(s.hss, self.CHAIN)
        nc.vector.tensor_scalar(m.hv[:], m.bank[4][:, 0:56], 1.0 / HD, EPS, ALU.mult, ALU.add).then_inc(s.hvar, 1)
        newton(dve, nc, s.hrt, 1, m.hv[:], m.hr[:], m.ht[:])
        dve.drain()

        def spread(r):
            _, tiles, at = self.chain(r)
            if r >= 2:
                dve.wait_ge(s.hx, r - 1)
            nc.vector.tensor_copy(m.rx[:, r % 2, 0:tiles * P].rearrange("p (t e) -> p t e", e=HD),
                                  m.hr[:, at:at + 2 * tiles].unsqueeze(2).to_broadcast([P, 2 * tiles, HD])).then_inc(s.rxd, 1)
        spread(0)
        spread(1)
        for r in range(self.CHAIN):
            x, tiles, _ = self.chain(r)
            dve.wait_ge(s.hx, r + 1)
            dve.drain()
            full = m.la[:, 0:tiles * P]
            nc.vector.scalar_tensor_tensor(out=full, in0=x, scalar=vec(V_GAINS + r // 2), in1=m.bank[5 + r % 2][:, 0:tiles * P],
                                           op0=ALU.mult, op1=ALU.mult)
            dve_split(dve, nc, full, *self.parts(r)).then_inc(s.hq, 1)
            if r + 2 < self.CHAIN:
                spread(r + 2)

        def mask_ready(n):
            if n % HEADS < 4:
                dve.wait_ge(s.mkd, n // HEADS * 4 + n % HEADS + 1)
        self.attention.dve(dve, nc, m, s, mask_ready)
        dve_update(dve, nc, m, s, self.u0 + MIX2_PROJ, lambda d: 1.0, self.after)

    def pool_masks(self, pool, nc, m, s):
        for i in range(TT):
            for h in range(4):
                before = HEADS * i + h - 2 if h >= 2 else HEADS * (i - 1) + h + 2
                if h >= 2 or i:
                    pool.wait_ge(s.sm, before + 1)
                else:
                    pool.wait_ge(s.hvar, 1)
                w = (i + 1) * P
                nc.gpsimd.tensor_scalar(m.mdh[:, h % 2, 0:w], m.masks[:, ALIBI_AT[i]:ALIBI_AT[i] + w], 4.0 ** -(h + 1), None,
                                        ALU.mult).then_inc(s.mkd, 1)


def dve_decay_rates(dve, nc, m, s):
    lam, (size, e, z, z2, minus, rate) = m.vec[:, V_LAM:V_LAM + 4], [m.sp[:, j] for j in range(6)]
    nc.vector.scalar_tensor_tensor(out=size, in0=lam, scalar=-1.0, in1=lam, op0=ALU.mult, op1=ALU.max).then_inc(s.lam, 1)
    dve.wait_ge(s.elam, 1)
    nc.vector.tensor_scalar(z, e, 2.0, None, ALU.add)
    dve.drain()
    nc.vector.reciprocal(z, z)
    dve.drain()
    nc.vector.tensor_tensor(z, z, e, ALU.mult)
    dve.drain()
    nc.vector.tensor_tensor(z2, z, z, ALU.mult)
    nc.vector.memset(rate, 1.0 / 17)
    for n in range(15, 0, -2):
        dve.drain()
        nc.vector.tensor_tensor(rate, rate, z2, ALU.mult)
        dve.drain()
        nc.vector.tensor_scalar(rate, rate, 1.0 / n, None, ALU.add)
    nc.vector.tensor_scalar(size, lam, -1.0, 0.0, ALU.mult, ALU.max)
    dve.drain()
    nc.vector.scalar_tensor_tensor(out=rate, in0=rate, scalar=2.0, in1=z, op0=ALU.mult, op1=ALU.mult)
    dve.drain()
    nc.vector.tensor_tensor(rate, rate, size, ALU.add)
    dve.drain()
    nc.vector.tensor_scalar(minus, rate, -8.0, None, ALU.mult)
    nc.vector.tensor_scalar(rate, rate, 8.0, None, ALU.mult).then_inc(s.c8, 1)


def sp_swap(sp, m, x, tiles, sem):
    half = HD // 8
    for lo in (0, HD):
        for e in range(2):
            to, of = lo + half * e, lo + half * (1 - e)
            for j in range(2):
                n = min(tiles - 2 * j, 2)
                sp.dma_start(m.other[j][to:to + half, 0:n], x[of:of + half, 2 * j:2 * j + n]).then_inc(sem, 16)


def pe_mixed_out(pe, nc, m, s, u, y0):
    pe.wait_ge(s.cl, TT)
    cat = lambda k: (m.guH[:, k], m.guL[:, k])
    for q in range(OUT_UNITS):
        pe.wait_ge(s.y, y0 + 2 * q + 2)
        pe_tiles(pe, nc, m, s, u + q, q % 2, [m.bank[4 + 2 * (q % 2)][:], m.bank[5 + 2 * (q % 2)][:]], cat, KD)


def act_mixed_out(act, nc, m, s, u, after):
    for q in range(OUT_UNITS):
        act_next(act, nc, m, s, u + q, UNIT)
        after.act_square(act, nc, m, s, 2 * q)
        after.act_square(act, nc, m, s, 2 * q + 1)



def signals(nc, tag, first):
    s = Signals()
    s.all = []

    def new(name):
        s.all.append(nc.alloc_semaphore(f"{tag}_{name}"))
        return s.all[-1]
    s.full = [new("full0"), new("full1")]
    s.high = new("high")
    s.low = new("low")
    s.mm = new("mm")
    s.silu = new("silu")
    s.ufree = new("ufree")
    s.gu = new("gu")
    s.y = new("y")
    s.sq = new("sq")
    s.acc = new("acc")
    s.ss = new("ss")
    s.var = new("var")
    s.rt = new("rt")
    s.dg = new("dg")
    s.spread = new("spread")
    s.tt = new("tt")
    s.hh = new("hh")
    s.hl = new("hl")
    s.ev = new("ev")
    s.sm = new("sm")
    s.sc = new("sc")
    s.ex = new("ex")
    s.pc = new("pc")
    s.tr = new("tr")
    s.av = new("av")
    s.on = new("on")
    s.bt = new("bt")
    s.cl = new("cl")
    s.ch = new("ch")
    if first:
        s.swap = [new("swap0"), new("swap1"), new("swap2")]
        s.clear = new("clear")
        s.mod_full = [new("mod_full0"), new("mod_full1")]
        s.mod_used = new("mod_used")
        s.mod_mm = new("mod_mm")
        s.mod_taken = new("mod_taken")
        s.par = new("par")
        s.rope = new("rope")
        s.lg = new("lg")
        s.relu = new("relu")
        s.wt = new("wt")
        s.wtd = new("wtd")
        s.lacc = new("lacc")
        s.sgw = new("sgw")
        s.sgu = new("sgu")
        s.ao = new("ao")
    else:
        s.vec = new("vec")
        s.dist = new("dist")
        s.gw = new("gw")
        s.mem = new("mem")
        s.lam = new("lam")
        s.elam = new("elam")
        s.c8 = new("c8")
        s.none = new("none")
        s.xb = new("xb")
        s.ga = new("ga")
        s.sgm = new("sgm")
        s.et = new("et")
        s.m2 = new("m2")
        s.mult = new("mult")
        s.hsq = new("hsq")
        s.hss = new("hss")
        s.hvar = new("hvar")
        s.hrt = new("hrt")
        s.rxd = new("rxd")
        s.hx = new("hx")
        s.hq = new("hq")
        s.mkd = new("mkd")
        s.st = new("st")
    return s


def setup_block(nc, m, a):
    s = Signals()
    s.ld = nc.alloc_semaphore("i_loaded")
    s.c = nc.alloc_semaphore("i_c")
    s.cx = nc.alloc_semaphore("i_x")
    s.ms = nc.alloc_semaphore("i_set")
    s.big = [nc.alloc_semaphore(f"i_big{q}") for q in range(4)]
    s.bias = nc.alloc_semaphore("i_bias")
    s.sil = nc.alloc_semaphore("i_silu")
    s.sum = nc.alloc_semaphore("i_sum")
    s.red = nc.alloc_semaphore("i_reduced")
    s.ang = nc.alloc_semaphore("i_angles")
    with nc.Block() as block:
        @block.sync
        def _(sp):
            sp.dma_start(m.pos[:], a["positions"].partition_broadcast(P)).then_inc(s.ld, 16)
            sp.dma_start(m.cst[:], a["constants"]).then_inc(s.ld, 16)
            sp.dma_start(m.csil[:], a["c"]).then_inc(s.c, 16)
            sp.dma_start(m.mod_b[:], a["ada_b"][LAYERS - 1]).then_inc(s.bias, 16)
            for q in range(4):
                piece = a["ada_w"][LAYERS - 1, N_MOD - 2 + q // 2, 4 * (q % 2):4 * (q % 2) + 4]
                sp.dma_start(m.mod_big[:, q], piece.rearrange("k p n -> p k n")).then_inc(s.big[q], 16)
            sp.dma_start(m.x[:], a["x"]).then_inc(s.cx, 16)
            sp.wait_ge(s.cx, 16)

        @block.vector
        def _(dve):
            nc.vector.memset(m.ones[:], 1.0)
            nc.vector.memset(m.zero[:], 0.0)
            nc.vector.memset(m.halfpi[:], float(np.pi / 2)).then_inc(s.ms, 1)
            dve.wait_ge(s.ld, 32)
            nc.vector.tensor_copy(m.warm[:], m.ident)
            nc.vector.tensor_copy(m.ang[:], m.pos[:])
            dve.drain()
            nc.vector.tensor_scalar(m.ang[:], m.ang[:], m.freq, None, ALU.mult)
            dve.drain()
            nc.vector.tensor_scalar(m.turn[:], m.ang[:], float(1 / (2 * np.pi)), MAGIC, ALU.mult, ALU.add)
            dve.drain()
            nc.vector.tensor_scalar(m.turn[:], m.turn[:], -MAGIC, None, ALU.add)
            for part in TWO_PI_PARTS:
                dve.drain()
                nc.vector.scalar_tensor_tensor(out=m.ang[:], in0=m.turn[:], scalar=-part, in1=m.ang[:], op0=ALU.mult, op1=ALU.add)
            dve.drain()
            nc.vector.tensor_scalar(m.ang[:], m.ang[:], 3.1415925, -3.1415925, ALU.min, ALU.max)
            dve.drain()
            nc.vector.scalar_tensor_tensor(out=m.turn[:], in0=m.ang[:], scalar=-1.0, in1=m.ang[:], op0=ALU.mult, op1=ALU.max)\
                .then_inc(s.ang, 1)
            dve.wait_ge(s.sil, 1)
            dve.wait_ge(s.bias, 16)
            for c in range(2):
                for k in range(KD):
                    dve.drain()
                    if k % 4 == 0:
                        dve.wait_ge(s.big[2 * c + k // 4], 16)
                    last = mod_add(nc, m, m.mod_big[:, 2 * c + k // 4, k % 4], k)
                last.then_inc(s.sum, 1)
                dve.wait_ge(s.red, c + 1)
                at = (N_MOD - 2 + c) * KD
                nc.vector.tensor_tensor(m.mod[:, at + 2 * KD:at + 3 * KD], m.bank[6][:, 8:8 + KD], m.mod_b[:, at:at + KD], ALU.add)

        @block.tensor
        def _(pe):
            for c in range(2):
                pe.wait_ge(s.sum, c + 1)
                mod_reduce(nc, m, 6).then_inc(s.red, 1)

        @block.scalar
        def _(act):
            act.wait_ge(s.c, 16)
            nc.scalar.activation(m.csil[:], m.csil[:], ACT.Silu).then_inc(s.sil, 1)
            act.wait_ge(s.ms, 1)
            act.wait_ge(s.ang, 1)
            nc.scalar.activation(m.sin[:], m.ang[:], ACT.Sin)
            nc.scalar.activation(m.cos[:], m.turn[:], ACT.Sin, scale=-1.0, bias=m.halfpi[:])


def layer_block(nc, m, s, a, l):
    norms = [Norm(0, 0), Norm(1, 1, y0=KD, warm=BETWEEN), Norm(2, 2, y0=2 * KD, warm=BETWEEN)]
    ffn1 = Ffn(0, L_FFN1, 0, norms[0], norms[1], UNIT)
    mix = Mix1(L_MIX, 2 * KD, norms[1], norms[2])
    ffn2 = Ffn(1, L_FFN2, 3 * KD, norms[2], None, 0)
    mod1, mod2 = Modulation(a["ada_w"][l], 0, 3), Modulation(a["ada_w"][l], 6, None)
    hH, hL = (lambda k: m.hH[:, k]), (lambda k: m.hL[:, k])
    shift = lambda chunk: (lambda k: m.mod[:, chunk * KD + k:chunk * KD + k + 1])
    scale = lambda k: m.A[:, k:k + 1]
    gate = lambda d: m.gate[:, d:d + 1]

    def dve_scale_of(dve, n):
        dve.drain()
        at = (3 * n + 1) * KD
        nc.vector.scalar_tensor_tensor(out=m.A[:], in0=m.mod[:, at:at + KD], scalar=1.0, in1=m.gains[:, n * KD:(n + 1) * KD],
                                       op0=ALU.add, op1=ALU.mult)
        dve.drain()

    with nc.Block() as block:
        @block.sync
        def _(sp):
            w_in = lambda g: (lambda i: a["ffn_in"][(2 * l + g) * IN_UNITS + i])
            w_a = lambda g: (lambda i: a["ffn_out_a"][(2 * l + g) * OUT_UNITS + i])
            w_b = lambda g: (lambda i: a["ffn_out_b"][(2 * l + g) * OUT_UNITS + i])
            sp.dma_start(m.mod_b[:], a["ada_b"][l]).then_inc(s.par, 16)
            sp.dma_start(m.gains[:], a["gains"][l]).then_inc(s.par, 16)
            ffn1.sp(sp, m, s, w_in(0), w_a(0), w_b(0), mod1)
            sp_units(sp, m, s, lambda i: a["mix"][l, i], L_MIX, 2, UNIT)
            sp.wait_ge(s.mod_mm, 6)
            sp.dma_start(m.sguT[:], a["sgu_w"][l]).then_inc(s.par, 16)
            sp.dma_start(m.sgub[0:1], a["sgu_b"][l]).then_inc(s.par, 16)
            sp.dma_start(m.masks[:, 0:P], a["causal"]).then_inc(s.par, 16)
            unit = lambda n: sp_unit(sp, m, s, a["mix"][l, n], L_MIX + n, UNIT)
            unit(2)
            unit(3)
            sp.wait_ge(s.ev, 4)
            sp.wait_ge(s.clear, 1)
            sp_swap(sp, m, m.ix, 3, s.swap[0])
            sp_units(sp, m, s, lambda i: a["mix"][l, 4 + i], L_MIX + 4, 6, UNIT)
            sp.wait_ge(s.ev, 16)
            sp.wait_ge(s.rope, 3)
            sp_swap(sp, m, m.q, 4, s.swap[1])
            unit(10)
            unit(11)
            sp.wait_ge(s.ev, 20)
            sp.wait_ge(s.rope, 7)
            sp_swap(sp, m, m.k, 4, s.swap[2])
            sp_units(sp, m, s, lambda i: a["mix"][l, MIX1_PROJ + i], L_MIX + MIX1_PROJ, OUT_UNITS, UNIT)
            ffn2.sp(sp, m, s, w_in(1), w_a(1), w_b(1), mod2)

        @block.gpsimd
        def _(pool):
            pool.sem_inc(s.low, 2)
            runs = lambda x: ((x.u0, IN_A, UNIT), (x.ua, OUT_UNITS, UNIT_A), (x.ub, IN_B, UNIT), (x.uc, OUT_UNITS, UNIT_B))
            for run in runs(ffn1):
                pool_low(pool, nc, m, s, *run)
            pool.wait_ge(s.low, L_MIX + 2)
            nc.gpsimd.memset(m.other[0][:], 0.0)
            nc.gpsimd.memset(m.other[1][:], 0.0).then_inc(s.clear, 1)
            pool_low(pool, nc, m, s, L_MIX, 4, UNIT)
            pool.wait_ge(s.par, 80)
            nc.gpsimd.affine_select(out=m.sguT[:], in_=m.sguT[:], pattern=[[0, 4], [1, P]], compare_op=ALU.is_ge, fill=0.0,
                                    base=0, channel_multiplier=-1).then_inc(s.sgw, 1)
            pool_low(pool, nc, m, s, L_MIX + 4, MIX1_PROJ + OUT_UNITS - 4, UNIT)
            for run in runs(ffn2):
                pool_low(pool, nc, m, s, *run)

        @block.scalar
        def _(act):
            act.sem_inc(s.silu, 2)
            for d in range(KD):
                norms[0].act_square(act, nc, m, s, d)
            act_high(act, nc, m, s, 0, 0, 0, UNIT)
            act_high(act, nc, m, s, 1, 1, 0, UNIT)
            norms[0].act_sqrt(act, nc, m, s)
            norms[0].act_apply(act, nc, m, s, hH, shift(0))
            ffn1.act(act, nc, m, s)
            norms[1].act_sqrt(act, nc, m, s)
            norms[1].act_apply(act, nc, m, s, hH, shift(3))
            mix.act(act, nc, m, s)
            norms[2].act_sqrt(act, nc, m, s)
            norms[2].act_apply(act, nc, m, s, hH, shift(6))
            ffn2.act(act, nc, m, s)

        @block.vector
        def _(dve):
            dve.sem_inc(s.ufree, 2)
            dve.sem_inc(s.y, 4)
            dve.sem_inc(s.mod_used, MOD_SLOTS)
            nc.vector.tensor_copy(m.mod[:, 0:2 * KD], m.mod[:, N_MOD * KD:(N_MOD + 2) * KD])
            for d in range(KD):
                norms[0].dve_add(dve, nc, m, s, d)
            dve.wait_ge(s.par, 32)
            dve_scale_of(dve, 0)
            norms[0].dve_rsqrt(dve, nc, m, s)
            norms[0].dve_apply(dve, nc, m, s, hH, hL, scale, shift(0))
            ffn1.dve(dve, nc, m, s, gate, mod1, half_gate=2)
            dve_scale_of(dve, 1)
            norms[1].dve_rsqrt(dve, nc, m, s)
            mod1.dve_take(dve, nc, m, s, 5, 0)
            norms[1].dve_apply(dve, nc, m, s, hH, hL, scale, shift(3))
            mix.dve(dve, nc, m, s, lambda d: m.mod[:, 5 * KD + d:5 * KD + d + 1])
            dve_scale_of(dve, 2)
            norms[2].dve_rsqrt(dve, nc, m, s)
            norms[2].dve_apply(dve, nc, m, s, hH, hL, scale, shift(6))
            ffn2.dve(dve, nc, m, s, gate, mod2, half_gate=8)

        @block.tensor
        def _(pe):
            pe.sem_inc(s.mm, 4)
            norms[0].pe_sum(pe, nc, m, s)
            norms[0].pe_spread(pe, nc, m, s)
            ffn1.pe(pe, nc, m, s, mod1)
            norms[1].pe_sum(pe, nc, m, s)
            norms[1].pe_spread(pe, nc, m, s)
            mix.pe(pe, nc, m, s)
            norms[2].pe_sum(pe, nc, m, s)
            norms[2].pe_spread(pe, nc, m, s)
            ffn2.pe(pe, nc, m, s, mod2)

    with nc.Block() as block:
        @block.gpsimd
        def _(pool):
            for x in s.all:
                pool.sem_clear(x)


def second_block(nc, m, s, a):
    norms = [Norm(0, None), Norm(1, 0, tokens=256, src=lambda m: m.mem), Norm(2, 1, y0=0, warm_bank=5),
             Norm(3, 2, y0=2 * KD, warm=BETWEEN),
             Norm(4, 3, y0=3 * KD, warm=BETWEEN)]
    ffn1 = Ffn(0, S_FFN1, KD, norms[2], norms[3], UNIT)
    mix = Mix2(S_MIX, 3 * KD, norms[3], norms[4])
    ffn2 = Ffn(1, S_FFN2, 4 * KD, norms[4], None, 0)
    hH, hL = (lambda k: m.hH[:, k]), (lambda k: m.hL[:, k])
    halves = lambda t: t.rearrange("p a (b n) -> p (a b) n", b=2)
    memH, memL = halves(m.guH[:, 0:4]), halves(m.guL[:, 4:8])
    gain = lambda at: (lambda k: m.vec[:, at + k:at + k + 1])
    half = lambda d: 0.5

    with nc.Block() as block:
        @block.sync
        def _(sp):
            w_in = lambda g: (lambda i: a["ffn_in"][(2 * LAYERS + g) * IN_UNITS + i])
            w_a = lambda g: (lambda i: a["ffn_out_a"][(2 * LAYERS + g) * OUT_UNITS + i])
            w_b = lambda g: (lambda i: a["ffn_out_b"][(2 * LAYERS + g) * OUT_UNITS + i])
            sp.dma_start(m.vec[:], a["vec"]).then_inc(s.vec, 16)
            sp_unit(sp, m, s, a["mem_kv"][0], 0, UNIT)
            sp_unit(sp, m, s, a["mem_kv"][1], 1, UNIT)
            sp.dma_start(m.mem[:], a["mem"]).then_inc(s.mem, 16)
            sp.dma_start(m.masks[:], a["alibi"]).then_inc(s.dist, 16)

            ffn1.sp(sp, m, s, w_in(0), w_a(0), w_b(0))
            sp_units(sp, m, s, lambda i: a["mix_2"][i], S_MIX, 2, UNIT)
            sp.wait_ge(s.y, 4 + 3 * KD)
            sp.dma_start(m.gatew[:], a["gate_w"]).then_inc(s.gw, 16)
            sp_units(sp, m, s, lambda i: a["mix_2"][2 + i], S_MIX + 2, MIX2_PROJ + OUT_UNITS - 2, UNIT)
            ffn2.sp(sp, m, s, w_in(1), w_a(1), w_b(1))
            for d in range(0, KD, 2):
                sp.wait_ge(s.y, 4 + 5 * KD + d + 2)
                sp.dma_start(a["out"][:, d:d + 2], m.x[:, d:d + 2]).then_inc(s.st, 16)
            sp.wait_ge(s.st, 16 * KD // 2)

        @block.gpsimd
        def _(pool):
            pool.sem_inc(s.low, 2)
            nc.gpsimd.memset(m.none[:], 0.0).then_inc(s.none, 1)
            runs = lambda x: ((x.u0, IN_A, UNIT), (x.ua, OUT_UNITS, UNIT_A), (x.ub, IN_B, UNIT), (x.uc, OUT_UNITS, UNIT_B))
            pool_low(pool, nc, m, s, 0, MEM_UNITS, UNIT)
            for run in runs(ffn1):
                pool_low(pool, nc, m, s, *run)
            pool_low(pool, nc, m, s, S_MIX, MIX2_PROJ + 2, UNIT)
            pool.wait_ge(s.dist, 16)
            mix.pool_masks(pool, nc, m, s)
            pool_low(pool, nc, m, s, S_MIX + MIX2_PROJ + 2, OUT_UNITS - 2, UNIT)
            for run in runs(ffn2):
                pool_low(pool, nc, m, s, *run)

        @block.scalar
        def _(act):
            act.sem_inc(s.silu, 2)
            act.wait_ge(s.vec, 16)
            for d in range(KD):
                norms[0].act_square(act, nc, m, s, d)
            act_high(act, nc, m, s, 0, 0, 0, UNIT)
            act_high(act, nc, m, s, 1, 1, 0, UNIT)
            act.wait_ge(s.lam, 1)
            nc.scalar.activation(m.sp[:, 1], m.sp[:, 0], ACT.Exp, scale=-1.0).then_inc(s.elam, 1)
            norms[0].act_sqrt(act, nc, m, s)
            act.wait_ge(s.mem, 16)
            for d in range(KD):
                norms[1].act_square(act, nc, m, s, d)
            norms[1].act_sqrt(act, nc, m, s)
            norms[1].act_apply(act, nc, m, s, lambda k: memH[:, k])
            for d in range(KD):
                norms[2].act_square(act, nc, m, s, d)
            for n, t in enumerate((m.memk, m.memv)):
                act_next(act, nc, m, s, n, UNIT)
                for j in range(2):
                    act.wait_ge(s.mm, 4 + 2 * n + j + 1)
                    nc.scalar.activation(t[:, j], m.bank[2 * n + j][:, 0:256], ACT.Copy).then_inc(s.ev, 1)
            norms[2].act_sqrt(act, nc, m, s)
            norms[2].act_apply(act, nc, m, s, hH)
            ffn1.act(act, nc, m, s)
            norms[3].act_sqrt(act, nc, m, s)
            norms[3].act_apply(act, nc, m, s, hH)
            mix.act(act, nc, m, s)
            norms[4].act_sqrt(act, nc, m, s)
            norms[4].act_apply(act, nc, m, s, hH)
            ffn2.act(act, nc, m, s)

        @block.vector
        def _(dve):
            dve.sem_inc(s.ufree, 2)
            dve.sem_inc(s.y, 4)
            for d in range(KD):
                norms[0].dve_add(dve, nc, m, s, d)
            dve.wait_ge(s.vec, 16)
            dve_decay_rates(dve, nc, m, s)
            norms[0].dve_rsqrt(dve, nc, m, s)
            dve.wait_ge(s.spread, 1)
            for d in range(KD):
                nc.vector.scalar_tensor_tensor(out=m.x[:, d], in0=m.x[:, d], scalar=m.vec[:, V_FINAL + d:V_FINAL + d + 1],
                                               in1=m.bank[7][:], op0=ALU.mult, op1=ALU.mult).then_inc(s.y, 1)
            for d in range(KD):
                norms[1].dve_add(dve, nc, m, s, d)
            norms[1].dve_rsqrt(dve, nc, m, s)
            norms[1].dve_apply(dve, nc, m, s, lambda k: memH[:, k], lambda k: memL[:, k], gain(V_MEM))
            for n in (2, 3, 4):
                if n == 2:
                    for d in range(KD):
                        norms[n].dve_add(dve, nc, m, s, d)
                norms[n].dve_rsqrt(dve, nc, m, s)
                norms[n].dve_apply(dve, nc, m, s, hH, hL, gain({2: V_FFN1, 3: V_MIX, 4: V_FFN2}[n]))
                if n == 2:
                    ffn1.dve(dve, nc, m, s, half)
                elif n == 3:
                    mix.dve(dve, nc, m, s)
                else:
                    ffn2.dve(dve, nc, m, s, half)

        @block.tensor
        def _(pe):
            pe.sem_inc(s.mm, 4)
            for n in range(2):
                norms[n].pe_sum(pe, nc, m, s)
                norms[n].pe_spread(pe, nc, m, s)
            mem = lambda k: (memH[:, k], memL[:, k])
            pe_tiles(pe, nc, m, s, 0, 0, [m.bank[0][:, 0:256], m.bank[1][:, 0:256]], mem, KD,
                     lambda k: pe.wait_ge(s.hl, k + 1))
            pe_rows(pe, nc, m, s, 1, mem, [m.bank[2][:, 0:256], m.bank[3][:, 0:256]])
            norms[2].pe_sum(pe, nc, m, s)
            norms[2].pe_spread(pe, nc, m, s)
            pe.wait_ge(s.ev, 4)
            ffn1.pe(pe, nc, m, s)
            norms[3].pe_sum(pe, nc, m, s)
            norms[3].pe_spread(pe, nc, m, s)
            mix.pe(pe, nc, m, s)
            norms[4].pe_sum(pe, nc, m, s)
            norms[4].pe_spread(pe, nc, m, s)
            ffn2.pe(pe, nc, m, s)


def program(nc, a, layers=LAYERS, second=True, debug=None):
    m = memory(nc)
    setup_block(nc, m, a)
    s = signals(nc, "l", True)
    with nc.Fori(0, layers) as l:
        layer_block(nc, m, s, a, l)
    if second:
        second_block(nc, m, signals(nc, "s", False), a)
    if debug:
        st = nc.alloc_semaphore("dbg")
        with nc.Block() as block:
            @block.sync
            def _(sp):
                sp.dma_start(a["out"], m.x[:]).then_inc(st, 16)
                sp.wait_ge(st, 16)

def tiles_of(x):
    return np.ascontiguousarray(x.reshape(-1, P, x.shape[-1]).transpose(1, 0, 2))


def column(v, n):
    return np.ascontiguousarray(np.asarray(v).reshape(n, P).T)


def units(w):
    rows, cols = w.shape
    w = w.reshape(rows // P, P, cols // COLS, COLS).transpose(2, 1, 0, 3)
    return w.reshape(cols // COLS, P, -1)


def ffn_units(w_in, w_out):
    pairs = [units(w_in[:, :DFF]), units(w_in[:, DFF:])]
    both = np.stack(pairs, axis=1).reshape(IN_UNITS, P, UNIT)
    return both, units(w_out[:FT_A * P]), units(w_out[FT_A * P:])


def mix1_units(w_in, w_out):
    sgu = D // 2
    u, v_a, q, k, v = (w_in[:, i * sgu:(i + 1) * sgu] for i in range(5))
    at = 5 * sgu
    iq, ik, iw = w_in[:, at:at + 256], w_in[:, at + 256:at + 320], w_in[:, at + 320:at + 324]
    first = np.concatenate([ik, ik, iw, np.zeros((D, COLS - 132), w_in.dtype)], axis=1)
    return units(np.concatenate([first, iq, v_a, u, q, k, v, w_out], axis=1))


def mix2_units(w_in, w_out):
    x, g, q, k, v, cq = np.split(w_in, [512, 1024, 1280, 1536, 1792], axis=1)
    return units(np.concatenate([x, g, q, k, cq, v, w_out], axis=1))


def block_diagonal(w):
    out = np.zeros((P, 4, P), w.dtype)
    for n in range(8):
        lo = 64 * (n % 2)
        out[lo:lo + 64, n // 2, lo:lo + 64] = w[n]
    return out


def constants():
    c = np.zeros((P, C_WIDTH), np.float32)
    c[:, C_IDENT:C_IDENT + P] = np.eye(P)
    half = HD // 8
    q, k = np.arange(P)[:, None], np.arange(P)[None, :]
    c[:, C_TRI:C_TRI + P] = np.where(k <= q, BIG, BELOW)
    c[:HD, C_SEL] = 1.0
    c[HD:, C_SEL + 1] = 1.0
    inv = np.float32(500000.0) ** (-np.arange(0, 2 * half, 2, dtype=np.float32) / np.float32(2 * half))
    for d in range(P):
        if d % HD < 2 * half:
            c[d, C_FREQ] = inv[d % half] * (-1 if d % HD < half else 1)
    causal = np.where(k <= q, 0.0, NEG).astype(np.float32)
    alibi = np.zeros((P, MASKS), np.float32)
    for i in range(TT):
        keys = np.arange((i + 1) * P)[None, :]
        away = i * P + q - keys
        alibi[:, ALIBI_AT[i]:ALIBI_AT[i] + (i + 1) * P] = np.where(away >= 0, -8.0 * away, NEG)
    return c, causal, alibi


def in_order_of_use(chunks):
    return np.concatenate([chunks[:, 2:], np.roll(chunks[:, :2], -1, axis=0)], axis=1)


def lay_out(v):
    ffns = [ffn_units(v[f"ffn{n}_w_in"][l], v[f"ffn{n}_w_out"][l]) for l in range(LAYERS) for n in (1, 2)]
    ffns += [ffn_units(v[f"ffn{n}_w_in_2"][0], v[f"ffn{n}_w_out_2"][0]) for n in (1, 2)]
    cst, causal, alibi = constants()
    vec = [column(v["final_norm"], 8), column(v["mem_norm_2"][0], 8), column(v["ffn1_norm_2"][0], 8),
           column(v["mix_norm_2"][0], 8), column(v["ffn2_norm_2"][0], 8)]
    vec += [column(v["lru_conv_w_2"][0][j], 4) for j in range(4)]
    vec += [column(v["lru_conv_b_2"][0], 4), column(v["lru_a_b_2"][0].reshape(-1), 4),
            column(v["lru_x_b_2"][0].reshape(-1), 4), column(v["lru_lambda_2"][0], 4)]
    vec += [column(np.tile(v[n][0], 2), 1) for n in ("moba_q_norm_2", "moba_k_norm_2", "mem_q_norm_2", "mem_k_norm_2")]
    return {
        "x": tiles_of(v["x"][0].T),
        "c": column(v["c"][0], KD),
        "positions": v["positions"].reshape(1, T),
        "constants": cst, "causal": causal, "alibi": alibi,
        "ada_w": in_order_of_use(v["ada_w"].reshape(LAYERS, KD, P, N_MOD, D).transpose(0, 3, 1, 2, 4)),
        "ada_b": in_order_of_use(v["ada_b"].reshape(LAYERS, N_MOD, KD, P)).reshape(LAYERS, N_MOD * KD, P).transpose(0, 2, 1),
        "gains": np.stack([np.concatenate([column(v[n][l], KD) for n in ("norm_ffn1", "norm_mix", "norm_ffn2")], axis=1)
                           for l in range(LAYERS)]),
        "ffn_in": np.concatenate([x[0] for x in ffns]),
        "ffn_out_a": np.concatenate([x[1] for x in ffns]),
        "ffn_out_b": np.concatenate([x[2] for x in ffns]),
        "mix": np.stack([mix1_units(v["mix_w_in"][l], v["mix_w_out"][l]) for l in range(LAYERS)]),
        "sgu_w": v["sgu_w"].transpose(0, 3, 1, 2),
        "sgu_b": v["sgu_b"].reshape(LAYERS, 1, 4, P),
        "mem": tiles_of(v["mem_2"][0].T),
        "mem_kv": units(v["mem_w_kv_2"][0]),
        "mix_2": mix2_units(v["w_in_2"][0], v["w_out_2"][0]),
        "vec": np.concatenate(vec, axis=1),
        "gate_w": np.stack([block_diagonal(v["lru_a_w_2"][0]), block_diagonal(v["lru_x_w_2"][0])], axis=1),
    }


def kernel(**inputs):
    import concourse.bacc as _bacc
    from concourse.bass_utils import run_bass_kernel_spmd as _run

    nc = _bacc.Bacc("TRN2", target_bir_lowering=False, num_devices=1)
    arrays, aps = {}, {}
    for name, x in lay_out({k: np.asarray(x) for k, x in inputs.items()}).items():
        x = np.ascontiguousarray(x)
        arrays[f"in_{name}"] = x
        aps[name] = nc.dram_tensor(f"in_{name}", x.shape, mybir.dt.from_np(x.dtype), kind="ExternalInput").ap()
    aps["out"] = nc.dram_tensor("out_0", (P, KD, T), F32, kind="ExternalOutput").ap()
    program(nc, aps)
    r = _run(nc, [arrays], core_ids=[0])
    got = r.results[0]["out_0"]
    return np.ascontiguousarray(got.transpose(1, 0, 2).reshape(D, T).T).reshape(1, T, D)
```

```python
import numpy as np

import concourse.bass as bass
from concourse import mybir
from concourse.alu_op_type import AluOpType as ALU

F32 = mybir.dt.float32
F32R = mybir.dt.float32r
I32 = mybir.dt.int32
ACT = mybir.ActivationFunctionType
AX = mybir.AxisListType

P = 128
D = 1024
T = 512
TT = T // P
KD = D // P
DFF = 2816
LAYERS = 2
COLS = 256
FT = DFF // P
FT_A = 12
FT_B = FT - FT_A
UNIT = KD * COLS
UNIT_A = FT_A * COLS
UNIT_B = FT_B * COLS
IN_UNITS = 2 * DFF // COLS
IN_A = 2 * FT_A // 2
IN_B = 2 * FT_B // 2
OUT_UNITS = D // COLS
FFN_UNITS = IN_UNITS + 2 * OUT_UNITS
N_MOD = 9
HD = 64
HEADS = 8
IDX_HEADS = 4
TOPK = T // 4
EPS = 1e-6
MOD_SLOTS = 2

MIX1_PROJ = 12
MIX2_PROJ = 8
MEM_UNITS = 2

L_FFN1 = 0
L_MIX = L_FFN1 + FFN_UNITS
L_FFN2 = L_MIX + MIX1_PROJ + OUT_UNITS
S_MEM = 0
S_FFN1 = S_MEM + MEM_UNITS
S_MIX = S_FFN1 + FFN_UNITS
S_FFN2 = S_MIX + MIX2_PROJ + OUT_UNITS

NEG = -1.0e30
BELOW = -3.0e38
TAKEN = -3.4e38
BIG = 3.0e38
MAGIC = 12582912.0
TWO_PI_PARTS = (6.28125, 0.001934051513671875, 1.2556659e-06)

C_IDENT, C_TRI, C_SEL, C_FREQ = 0, P, 2 * P, 2 * P + 2
C_WIDTH = 2 * P + 3
ALIBI_AT = [0, 128, 384, 768]
MASKS = 1280
V_FINAL, V_MEM, V_FFN1, V_MIX, V_FFN2 = 0, 8, 16, 24, 32
V_CONVW, V_CONVB, V_AB, V_XB, V_LAM, V_GAINS, V_WIDTH = 40, 56, 60, 64, 68, 72, 76


class Memory:
    pass


class Signals:
    pass


def memory(nc):
    m = Memory()
    base = -(-nc.sbuf_base // 32) * 32
    K = 1024

    def at(name, offset, shape, dt=F32):
        return nc.alloc_sbuf_tensor_at("m_" + name, [P] + shape, dt, offset=base + offset)

    m.x = at("x", 0, [KD, T])
    m.hH = at("hH", 16 * K, [KD, T], F32R)
    m.hL = at("hL", 32 * K, [KD, T], F32R)
    m.guH = at("guH", 48 * K, [FT_A, T], F32R)
    m.guL = at("guL", 72 * K, [FT_A, T], F32R)
    m.wraw = at("wraw", 96 * K, [2, UNIT_A])
    m.wH = at("wH", 120 * K, [2, UNIT_A], F32R)
    m.wL = at("wL", 144 * K, [2, UNIT_A], F32R)
    m.mod_big = at("mod_big", 48 * K, [4, 4, D])
    m.u = at("u", 56 * K, [4, T])
    m.va = at("va", 80 * K, [TT, T])
    m.lx = at("lx", 56 * K, [4, T])
    m.gl = at("gl", 80 * K, [4, T])
    m.xb = at("xb", 72 * K, [4, T])
    m.q = at("q", 64 * K, [4, T])
    m.k = at("k", 88 * K, [4, T])
    m.cq = at("cq", 88 * K, [2, T])
    m.gatew = at("gatew", 92 * K, [2, 4, P])
    spare = UNIT * 4
    m.other = [at(f"other{j}", 96 * K + j * UNIT_A * 4 + spare, [2, T]) for j in range(2)]
    m.lowA = [at(f"lowA{j}", 120 * K + j * UNIT_A * 4 + spare, [2, T], F32R) for j in range(2)]
    m.lowB = [at(f"lowB{j}", 144 * K + j * UNIT_A * 4 + spare, [2, T], F32R) for j in range(2)]
    m.hs = m.other[0]
    m.rx = m.other[0]
    m.nf = m.other[1]
    m.memkL = at("memkL", 144 * K + UNIT_A * 4 + spare, [2, 256], F32R)
    m.qH = at("qH", 64 * K, [4, T], F32R)
    m.kH = at("kH", 88 * K, [4, T], F32R)
    m.cqH = at("cqH", 88 * K, [2, T], F32R)
    m.mem = at("mem", 72 * K, [KD, 256])
    m.sm = at("sm", 16 * K, [3, T])
    m.p = at("p", 22 * K, [3, T])
    m.pT = at("pT", 28 * K, [3, T])
    m.bn = at("bn", 34 * K, [2, T])
    m.mdh = at("mdh", 38 * K, [2, T])
    m.mn = at("mn", 46 * K, [32])
    m.sums = at("sums", 46 * K + 128, [32])
    m.rinv = at("rinv", 46 * K + 256, [32])
    o = 168 * K
    m.masks = at("masks", o, [MASKS]); o += 5 * K
    g = o
    m.sg = at("sg", g, [2, T])
    m.gut = at("gut", g + 4 * K, [2, T])
    m.t = at("t", g, [4, T])
    m.sq = at("sq", g + 8 * K, [2, T])
    m.acc = at("acc", g + 12 * K, [T])
    m.ix = at("ix", g, [3, T])
    m.ixH = at("ixH", g, [3, T], F32R)
    m.rl = at("rl", g + 6 * K, [2, T])
    m.full = at("full", 80 * K, [4, T])
    m.ra = at("ra", g + 10 * K, [T])
    m.rb = at("rb", g + 12 * K, [T])
    m.rg = at("rg", g, [4, T])
    m.ig3 = at("ig3", g + 8 * K, [3, T])
    m.pos = at("pos", g, [T], I32)
    m.ang = at("ang", g + 2 * K, [T])
    m.turn = at("turn", g + 4 * K, [T])
    o += 14 * K
    a = o
    m.mod_w = at("mod_w", a, [MOD_SLOTS, D])
    m.c = at("c", a + 8 * K, [D])
    m.v = at("v", a, [TT, T])
    m.sguT = at("sguT", a + 8 * K, [4, P])
    m.sgub = at("sgub", a + 10 * K, [4, P])
    m.memk = at("memk", a, [2, 256])
    m.memkH = at("memkH", a, [2, 256], F32R)
    m.memv = at("memv", a + 2 * K, [2, 256])
    m.mv = at("mv", a + 4 * K, [TT, 256])
    m.la = at("la", a + 8 * K, [T])
    m.lb = at("lb", a + 10 * K, [T])
    o += 12 * K
    m.cos = at("cos", o, [T])
    m.sin = at("sin", o + 2 * K, [T])
    m.none = at("none", o + 2 * K, [256])
    m.hv = at("hv", o + 3 * K, [56])
    m.hr = at("hr", o + 3 * K + 256, [56])
    m.ht = at("ht", o + 3 * K + 512, [56])
    m.ig1 = at("ig1", o, [1, T])
    o += 4 * K
    def small(name, shape, dt=F32):
        nonlocal o
        here, o = o, o + -(-int(np.prod(shape)) * 4 // 32) * 32
        return at(name, here, shape, dt)

    m.vec = at("vec", o, [V_WIDTH])
    m.mod = small("mod", [(N_MOD + 2) * KD])
    m.mod_b = small("mod_b", [N_MOD * KD])
    m.cst = small("cst", [C_WIDTH])
    m.ones = small("ones", [P])
    m.warm = small("warm", [P], F32R)
    m.gains = small("gains", [3 * KD])
    m.A = small("A", [KD])
    m.gate = small("gate", [KD])
    m.red = small("red", [KD])
    m.zero = small("zero", [1])
    m.halfpi = small("halfpi", [1])
    m.wi = small("wi", [4 * TT])
    m.m8 = small("m8", [8])
    m.nv = small("nv", [TT])
    m.nr = small("nr", [TT])
    m.nt = small("nt", [TT])
    m.sp = small("sp", [6, 4])
    assert base + o <= nc.sbuf_usable_end, (base + o, nc.sbuf_usable_end)
    m.ident = m.cst[:, C_IDENT:C_IDENT + P]
    m.tri = m.cst[:, C_TRI:C_TRI + P]
    m.sel = m.cst[:, C_SEL:C_SEL + 2]
    m.freq = m.cst[:, C_FREQ:C_FREQ + 1]
    m.one = m.ones[:, 0:1]
    m.bank = [nc.alloc_psum_tensor(f"bank{i}", [P, 512], F32) for i in range(8)]
    return m


def f(ap):
    return ap.bitcast(F32)



def sp_units(sp, m, s, src, u0, n, size):
    with sp.Fori(0, n // 2) as i:
        for j in range(2):
            sp.wait_ge(s.low, u0 + 2 * i + j + 1)
            sp.dma_start(m.wraw[:, j, 0:size], src(2 * i + j)).then_inc(s.full[j], 16)


def sp_unit(sp, m, s, src, u, size):
    sp.wait_ge(s.low, u + 1)
    sp.dma_start(m.wraw[:, u % 2, 0:size], src).then_inc(s.full[u % 2], 16)


def pool_low(pool, nc, m, s, u0, n, size):
    with pool.Fori(0, n // 2) as i:
        for j in range(2):
            pool.wait_ge(s.high, u0 + 2 * i + j + 1)
            nc.gpsimd.tensor_tensor(m.wL[:, j, 0:size], m.wraw[:, j, 0:size], f(m.wH[:, j, 0:size]), ALU.subtract)\
                .then_inc(s.low, 1)


def pool_unit(pool, nc, m, s, j):
    return nc.gpsimd.tensor_tensor(m.wL[:, j, 0:UNIT], m.wraw[:, j, 0:UNIT], f(m.wH[:, j, 0:UNIT]), ALU.subtract)


def act_high(act, nc, m, s, u, j, pair, size):
    act.wait_ge(s.full[j], 16 * (pair + 1))
    act.wait_ge(s.mm, 2 * u + 2)
    nc.scalar.activation(m.wH[:, j, 0:size], m.wraw[:, j, 0:size], ACT.Copy).then_inc(s.high, 1)


def act_next(act, nc, m, s, u, size):
    if size:
        act_high(act, nc, m, s, u + 2, u % 2, (u + 2) // 2, size)


def keep_warm(nc, m, bank, n):
    for _ in range(n):
        nc.tensor.matmul(m.bank[bank][:], m.warm[:], m.warm[:].unsqueeze(1).to_broadcast([P, TT, P]), start=True, stop=True)


def pe_3(nc, out, a, b, first, last):
    nc.tensor.matmul(out, a[0], b[0], start=first, stop=False)
    nc.tensor.matmul(out, a[0], b[1], start=False, stop=False)
    return nc.tensor.matmul(out, a[1], b[0], start=False, stop=last)


def pe_tiles(pe, nc, m, s, u, slot, banks, right, rows, waits=None, by_row=False):
    pe.wait_ge(s.low, u + 3)
    order = [(k, j) for k in range(rows) for j in range(2)] if by_row else [(k, j) for j in range(2) for k in range(rows)]
    for n, (k, j) in enumerate(order):
        if waits and j == 0:
            waits(k)
        at = k * COLS + j * P
        w = m.wH[:, slot, at:at + P], m.wL[:, slot, at:at + P]
        mm = pe_3(nc, banks[j], w, right(k), k == 0, k == rows - 1)
        if k == rows - 1:
            mm.then_inc(s.mm, 1)


def pe_rows(pe, nc, m, s, u, left, outs):
    pe.wait_ge(s.low, u + 3)
    for tt, out in enumerate(outs):
        for k in range(KD):
            hi, lo = left(k)
            w = [x[:, u % 2, k * COLS:(k + 1) * COLS] for x in (m.wH, m.wL)]
            mm = pe_3(nc, out, (hi[:, tt * P:(tt + 1) * P], lo[:, tt * P:(tt + 1) * P]), w, k == 0, k == KD - 1)
        if tt % (len(outs) // 2) == len(outs) // 2 - 1:
            mm.then_inc(s.mm, 1)



class Norm:

    def __init__(self, n, q, a, y0=None, tokens=T, src=None, warm=(0, 8, 9), warm_bank=2):
        self.warm, self.warm_bank = warm, warm_bank
        self.n, self.q, self.a, self.y0, self.tokens, self.src = n, q, a, y0, tokens, src or (lambda m: m.x)

    def act_square(self, act, nc, m, s, d):
        if self.y0 is not None:
            act.wait_ge(s.y, 4 + self.y0 + d + 1)
        if d >= 3:
            act.wait_ge(s.acc, 7 * self.q + d - 2)
        x = self.src(m)[:, d]
        out = m.acc[:, 0:self.tokens] if d == 0 else m.sq[:, d % 2, 0:self.tokens]
        nc.scalar.activation(out, x, ACT.Square).then_inc(s.sq, 1)

    def dve_add(self, dve, nc, m, s, d):
        if d == 0:
            return
        dve.wait_ge(s.sq, 8 * self.q + d + 1)
        dve.drain()
        w = self.tokens
        nc.vector.tensor_tensor(m.acc[:, 0:w], m.acc[:, 0:w], m.sq[:, d % 2, 0:w], ALU.add).then_inc(s.acc, 1)

    def pe_sum(self, pe, nc, m, s):
        keep_warm(nc, m, self.warm_bank, self.warm[0])
        if self.q is not None:
            pe.wait_ge(s.acc, 7 * self.q + 7)
        for tt in range(self.tokens // P):
            mm = nc.tensor.matmul(m.bank[6][:, tt:tt + 1], m.acc[:, tt * P:(tt + 1) * P], m.one, start=True, stop=True)
        mm.then_inc(s.ss, 1)
        keep_warm(nc, m, self.warm_bank, self.warm[1])

    def dve_rsqrt(self, dve, nc, m, s):
        tt = self.tokens // P
        v, r, t = m.nv[:, 0:tt], m.nr[:, 0:tt], m.nt[:, 0:tt]
        dve.wait_ge(s.ss, self.n + 1)
        dve.drain()
        nc.vector.tensor_scalar(v, m.bank[6][:, 0:tt], 1.0 / D, EPS, ALU.mult, ALU.add).then_inc(s.var, 1)
        newton(dve, nc, s.rt, self.n + 1, v, r, t).then_inc(s.dg, 1)

    def act_sqrt(self, act, nc, m, s):
        tt = self.tokens // P
        act.wait_ge(s.var, self.n + 1)
        nc.scalar.activation(m.nr[:, 0:tt], m.nv[:, 0:tt], ACT.Sqrt).then_inc(s.rt, 1)

    def pe_spread(self, pe, nc, m, s):
        pe.wait_ge(s.dg, self.n + 1)
        for tt in range(self.tokens // P):
            mm = nc.tensor.matmul(m.bank[7][:, tt * P:(tt + 1) * P], m.nr[:, tt:tt + 1].to_broadcast([P, P]), m.ident,
                                  start=True, stop=True)
        mm.then_inc(s.spread, 1)
        keep_warm(nc, m, self.warm_bank, self.warm[2])

    def dve_scale(self, dve, nc, m, s, k, scale):
        if k == 0:
            dve.wait_ge(s.spread, self.n + 1)
        if 8 * self.a + k >= 4:
            dve.wait_ge(s.hl, 8 * self.a + k - 3)
        w = self.tokens
        nc.vector.scalar_tensor_tensor(out=m.t[:, k % 4, 0:w], in0=self.src(m)[:, k], scalar=scale(k), in1=m.bank[7][:, 0:w],
                                       op0=ALU.mult, op1=ALU.mult).then_inc(s.tt, 1)

    def dve_low(self, dve, nc, m, s, k, hL, hH, shift):
        dve.wait_ge(s.hh, 8 * self.a + k + 1)
        t = m.t[:, k % 4, 0:self.tokens]
        if shift:
            nc.vector.scalar_tensor_tensor(out=hL, in0=t, scalar=shift(k), in1=f(hH), op0=ALU.add, op1=ALU.subtract)\
                .then_inc(s.hl, 1)
        else:
            nc.vector.tensor_tensor(hL, t, f(hH), ALU.subtract).then_inc(s.hl, 1)

    def dve_apply(self, dve, nc, m, s, hH, hL, scale, shift=None):
        self.dve_scale(dve, nc, m, s, 0, scale)
        self.dve_scale(dve, nc, m, s, 1, scale)
        for k in range(KD):
            self.dve_low(dve, nc, m, s, k, hL(k), hH(k), shift)
            if k + 2 < KD:
                self.dve_scale(dve, nc, m, s, k + 2, scale)

    def act_apply(self, act, nc, m, s, hH, shift=None):
        for k in range(KD):
            act.wait_ge(s.tt, 8 * self.a + k + 1)
            t = m.t[:, k % 4, 0:self.tokens]
            nc.scalar.activation(hH(k), t, ACT.Identity, bias=shift(k) if shift else m.zero[:]).then_inc(s.hh, 1)


BETWEEN = (22, 9, 12)


def newton(dve, nc, roots, count, v, r, t):
    dve.wait_ge(roots, count)
    nc.vector.reciprocal(r, r)
    dve.drain()
    nc.vector.scalar_tensor_tensor(out=t, in0=r, scalar=-0.5, in1=r, op0=ALU.mult, op1=ALU.mult)
    dve.drain()
    nc.vector.tensor_tensor(t, t, v, ALU.mult)
    dve.drain()
    return nc.vector.scalar_tensor_tensor(out=r, in0=t, scalar=1.5, in1=r, op0=ALU.add, op1=ALU.mult)



class Ffn:

    def __init__(self, n, u0, y0, norm, after, ahead):
        self.n, self.u0, self.y0, self.norm, self.after, self.ahead = n, u0, y0, norm, after, ahead
        self.ua, self.ub = u0 + IN_A, u0 + IN_A + OUT_UNITS
        self.uc = self.ub + IN_B
        self.f0 = FT * n

    def pe_group(self, pe, nc, m, s, u, f, waits=None):
        h = lambda k: (m.hH[:, k], m.hL[:, k])
        pe.wait_ge(s.silu, f + 2)
        pe_tiles(pe, nc, m, s, u, 0, [m.bank[0][:], m.bank[1][:]], h, KD, waits, by_row=waits is not None)
        pe.wait_ge(s.ufree, f + 2)
        pe_tiles(pe, nc, m, s, u + 1, 1, [m.bank[2][:], m.bank[3][:]], h, KD)

    def pe_out(self, pe, nc, m, s, u, rows, g0, y):
        gu = lambda k: (m.guH[:, k], m.guL[:, k])

        def waits(k):
            if k in (0, rows - 2, rows - 1):
                pe.wait_ge(s.gu, g0 + (rows - 2 if k == 0 else k + 1))
        with pe.Fori(0, OUT_UNITS // 2) as i:
            for q in range(2):
                pe.wait_ge(s.y, y + 4 * i + 2 * q + 2)
                pe_tiles(pe, nc, m, s, u + 2 * i + q, q, [m.bank[4 + 2 * q][:], m.bank[5 + 2 * q][:]], gu, rows, waits)

    def pe(self, pe, nc, m, s):
        a = self.norm.a
        first = lambda k: pe.wait_ge(s.hl, 8 * a + k + 1)
        self.pe_group(pe, nc, m, s, self.u0, self.f0, first)
        with pe.Fori(1, IN_A // 2) as i:
            self.pe_group(pe, nc, m, s, self.u0 + 2 * i, self.f0 + 2 * i)
        self.pe_out(pe, nc, m, s, self.ua, FT_A, self.f0, self.y0)
        with pe.Fori(0, IN_B // 2) as i:
            self.pe_group(pe, nc, m, s, self.ub + 2 * i, self.f0 + FT_A + 2 * i)
        self.pe_out(pe, nc, m, s, self.uc, FT_B, self.f0 + FT_A, self.y0 + KD)

    def act_group(self, act, nc, m, s, u, pair, f, size):
        for j in range(2):
            act.wait_ge(s.mm, 4 + 2 * u + j + 1)
            act.wait_ge(s.ufree, f + j + 1)
            nc.scalar.activation(m.sg[:, j], m.bank[j][:], ACT.Silu).then_inc(s.silu, 1)
        act_high(act, nc, m, s, u + 2, 0, pair + 1, size)
        act_high(act, nc, m, s, u + 3, 1, pair + 1, size)

    def act(self, act, nc, m, s):
        for u, n, f, after in ((self.u0, IN_A, self.f0, UNIT_A), (self.ub, IN_B, self.f0 + FT_A, UNIT_B)):
            with act.Fori(0, n // 2 - 1) as i:
                self.act_group(act, nc, m, s, u + 2 * i, u // 2 + i, f + 2 * i, UNIT)
            last = n - 2
            self.act_group(act, nc, m, s, u + last, (u + last) // 2, f + last, after)
            out = u + n
            for q in range(OUT_UNITS):
                size = after if q < OUT_UNITS - 2 else (UNIT if after == UNIT_A else self.ahead)
                act_next(act, nc, m, s, out + q, size)
                if after == UNIT_B and self.after:
                    self.after.act_square(act, nc, m, s, 2 * q)
                    self.after.act_square(act, nc, m, s, 2 * q + 1)

    def dve_group(self, dve, nc, m, s, u, f0, tile):
        for j in range(2):
            dve.drain()
            dve.wait_ge(s.silu, 2 + f0 + j + 1)
            dve.wait_ge(s.mm, 4 + 2 * u + 2 + j + 1)
            nc.vector.tensor_tensor(m.gut[:, j], m.sg[:, j], m.bank[2 + j][:], ALU.mult).then_inc(s.ufree, 1)
            dve.drain()
            nc.vector.tensor_copy(m.guH[:, tile + j], m.gut[:, j])
            dve.drain()
            nc.vector.tensor_tensor(m.guL[:, tile + j], m.gut[:, j], f(m.guH[:, tile + j]), ALU.subtract).then_inc(s.gu, 1)

    def dve(self, dve, nc, m, s, gate, mod=None, half_gate=None):
        if not mod:
            with dve.Fori(0, IN_A // 2) as i:
                self.dve_group(dve, nc, m, s, self.u0 + 2 * i, self.f0 + 2 * i, 2 * i)
        else:
            with dve.Fori(0, IN_A // 4) as i:
                for g in range(2):
                    mod.dve_half(dve, nc, m, s, mod.in_a, i, g)
                    self.dve_group(dve, nc, m, s, self.u0 + 4 * i + 2 * g, self.f0 + 4 * i + 2 * g, 4 * i + 2 * g)
                mod.dve_take(dve, nc, m, mod.in_a + i)
        if half_gate is not None:
            dve_half_gate(dve, nc, m, half_gate)
        dve_update(dve, nc, m, s, self.ua, gate)
        if mod and mod.in_b is not None:
            last = IN_B // 4
            with dve.Fori(0, last) as i:
                for g in range(2):
                    mod.dve_half(dve, nc, m, s, mod.in_b, i, g)
                    self.dve_group(dve, nc, m, s, self.ub + 4 * i + 2 * g, self.f0 + FT_A + 4 * i + 2 * g, 4 * i + 2 * g)
                mod.dve_take(dve, nc, m, mod.in_b + i)
            mod.dve_half(dve, nc, m, s, mod.in_b, last, 0)
            self.dve_group(dve, nc, m, s, self.uc - 2, self.f0 + FT - 2, FT_B - 2)
            mod.dve_half(dve, nc, m, s, mod.in_b, last, 1)
            mod.dve_take(dve, nc, m, mod.in_b + last)
        else:
            with dve.Fori(0, IN_B // 2) as i:
                self.dve_group(dve, nc, m, s, self.ub + 2 * i, self.f0 + FT_A + 2 * i, 2 * i)
        dve_update(dve, nc, m, s, self.uc, gate, self.after)

    def sp(self, sp, m, s, w_in, w_a, w_b, mod=None):
        def two(u, src, at):
            for j in range(2):
                sp.wait_ge(s.low, u + at + j + 1)
                sp.dma_start(m.wraw[:, j, 0:UNIT], src(at + j)).then_inc(s.full[j], 16)

        def chunks(u, src, n, first, then):
            two(u, src, 0)
            with sp.Fori(0, n - 1) as i:
                two(u, src, 4 * i + 2)
                mod.sp_half(sp, m, s, first, i, 0)
                two(u, src, 4 * i + 4)
                mod.sp_half(sp, m, s, first, i, 1)
            two(u, src, 4 * n - 2)
            mod.sp_half(sp, m, s, first, n - 1, 0)
            then()
            mod.sp_half(sp, m, s, first, n - 1, 1)
        if mod:
            chunks(self.u0, w_in, IN_A // 4, mod.in_a, lambda: sp_units(sp, m, s, w_a, self.ua, 2, UNIT_A))
            sp_units(sp, m, s, lambda i: w_a(2 + i), self.ua + 2, OUT_UNITS - 2, UNIT_A)
        else:
            sp_units(sp, m, s, w_in, self.u0, IN_A, UNIT)
            sp_units(sp, m, s, w_a, self.ua, OUT_UNITS, UNIT_A)
        if mod and mod.in_b is not None:
            last = lambda: sp_units(sp, m, s, lambda i: w_in(IN_UNITS - 2 + i), self.uc - 2, 2, UNIT)
            chunks(self.ub, lambda i: w_in(IN_A + i), IN_B // 4, mod.in_b, last)
            sp_units(sp, m, s, w_b, self.uc, 2, UNIT_B)
            mod.sp_half(sp, m, s, mod.in_b, IN_B // 4, 0)
            mod.sp_half(sp, m, s, mod.in_b, IN_B // 4, 1)
            sp_units(sp, m, s, lambda i: w_b(2 + i), self.uc + 2, OUT_UNITS - 2, UNIT_B)
        else:
            sp_units(sp, m, s, lambda i: w_in(IN_A + i), self.ub, IN_B, UNIT)
            sp_units(sp, m, s, w_b, self.uc, OUT_UNITS, UNIT_B)


def dve_half_gate(dve, nc, m, chunk):
    dve.drain()
    nc.vector.tensor_scalar(m.gate[:], m.mod[:, chunk * KD:(chunk + 1) * KD], 0.5, None, ALU.mult)
    dve.drain()


def dve_update(dve, nc, m, s, u, gate, after=None):
    dve.drain()
    for d in range(KD):
        dve.wait_ge(s.mm, 4 + 2 * u + d + 1)
        nc.vector.scalar_tensor_tensor(out=m.x[:, d], in0=m.bank[4 + d % 4][:], scalar=gate(d), in1=m.x[:, d],
                                       op0=ALU.mult, op1=ALU.add).then_inc(s.y, 1)
        if after and d % 2:
            after.dve_add(dve, nc, m, s, d - 1)
            after.dve_add(dve, nc, m, s, d)



class Modulation:

    def __init__(self, w, in_a, in_b):
        self.w, self.in_a, self.in_b = w, in_a, in_b

    def sp_half(self, sp, m, s, first, i, g):
        for k in range(4):
            n = KD * first + 4 * g + k
            sp.wait_ge(s.mod_used, KD * i + n + 1)
            sp.dma_start(m.mod_w[:, k % 2], self.w[first + i, 4 * g + k]).then_inc(s.mod_full[k % 2], 16)

    def dve_half(self, dve, nc, m, s, first, i, g):
        dve.drain()
        for k in range(4):
            dve.wait_ge(s.mod_full[k % 2], 16 * (4 * (first + i) + 2 * g + k // 2 + 1))
            mod_sum(nc, m, m.mod_w[:, k % 2], 4 * g + k).then_inc(s.mod_used, 1)

    def dve_take(self, dve, nc, m, c):
        at = c * KD
        dve.drain()
        nc.vector.tensor_tensor(m.mod[:, bass.ds(at + 2 * KD, KD)], m.red[:], m.mod_b[:, bass.ds(at, KD)], ALU.add)
        dve.drain()


def mod_sum(nc, m, w, k):
    return nc.vector.tensor_tensor_reduce(out=w, in0=w, in1=m.c[:], scale=1.0, scalar=0.0, op0=ALU.mult, op1=ALU.add,
                                          accum_out=m.red[:, k:k + 1])



WARM = (2, 1, 1, 0)


class Attention:

    N = TT * HEADS

    def __init__(self, head, value, parts):
        self.head, self.value, self.parts = head, value, parts

    def steps(self, n, *stages):
        for lag, stage in stages:
            if 0 <= n - lag < self.N:
                stage(n - lag)

    def of(self, n):
        q, k, mask, tiles = self.head(n % HEADS, n // HEADS)
        return q, k, mask, tiles * P, tiles

    def pe(self, pe, nc, m, s):
        def scores(n):
            q, k, _, w, _ = self.of(n)
            if n >= 3:
                pe.wait_ge(s.sm, n - 2)
            if n < HEADS:
                pe.wait_ge(s.parts, self.parts(n))
            keep_warm(nc, m, 2 + n % 3, WARM[n // HEADS])
            pe_3(nc, m.bank[2 + n % 3][:, 0:w], q, k, True, True).then_inc(s.sc, 1)

        def turn(n):
            _, _, _, w, tiles = self.of(n)
            pe.wait_ge(s.ex, n + 1)
            if n >= 3:
                pe.wait_ge(s.pc, n - 2)
            for b in range(tiles):
                mm = nc.tensor.transpose(m.bank[5 + n % 3][:, b * P:(b + 1) * P], m.p[:, n % 3, b * P:(b + 1) * P], m.ident)
            mm.then_inc(s.tr, 1)

        def product(n):
            i, h = n // HEADS, n % HEADS
            _, _, _, w, tiles = self.of(n)
            if h == 0 and i >= 2:
                pe.wait_ge(s.cl, i - 1)
            pe.wait_ge(s.pc, n + 1)
            for b in range(tiles):
                mm = nc.tensor.matmul(m.bank[i % 2][:, h * HD:(h + 1) * HD], m.pT[:, n % 3, b * P:(b + 1) * P],
                                      self.value(h, b), start=(b == 0), stop=(b == tiles - 1))
            mm.then_inc(s.av, 1)

        def out(n):
            if n % HEADS == HEADS - 1:
                i = n // HEADS
                pe.wait_ge(s.on, i + 1)
                for d in range(4):
                    mm = nc.tensor.transpose(m.bank[i % 2][:, d * P:(d + 1) * P], m.bn[:, i % 2, d * P:(d + 1) * P], m.ident)
                mm.then_inc(s.bt, 1)
        for n in range(self.N + 4):
            self.steps(n, (0, scores), (1, turn), (2, product), (4, out))

    def dve(self, dve, nc, m, s, premask=None):
        def mask(n):
            q, k, mask, w, _ = self.of(n)
            dve.wait_ge(s.sc, n + 1)
            if n >= 3:
                dve.wait_ge(s.ex, n - 2)
            if premask:
                premask(n)
            nc.vector.tensor_tensor_reduce(out=m.sm[:, n % 3, 0:w], in0=m.bank[2 + n % 3][:, 0:w], in1=mask,
                                           scale=-(HD ** -0.5), scalar=BIG, op0=ALU.add, op1=ALU.min,
                                           accum_out=m.mn[:, n:n + 1]).then_inc(s.sm, 1)

        def copy(n):
            w = self.of(n)[3]
            dve.wait_ge(s.tr, n + 1)
            if n >= 3:
                dve.wait_ge(s.av, n - 2)
            nc.vector.tensor_copy(m.pT[:, n % 3, 0:w], m.bank[5 + n % 3][:, 0:w]).then_inc(s.pc, 1)

        def normalize(n):
            if n % HEADS == HEADS - 1:
                i = n // HEADS
                r = m.rinv[:, i * HEADS:(i + 1) * HEADS]
                dve.wait_ge(s.av, n + 1)
                nc.vector.reciprocal(r, m.sums[:, i * HEADS:(i + 1) * HEADS])
                dve.drain()
                if i >= 2:
                    dve.wait_ge(s.bt, i - 1)
                nc.vector.tensor_tensor(m.bn[:, i % 2].rearrange("p (h e) -> p h e", h=HEADS),
                                        m.bank[i % 2][:].rearrange("p (h e) -> p h e", h=HEADS),
                                        r.unsqueeze(2).to_broadcast([P, HEADS, HD]), ALU.mult).then_inc(s.on, 1)

        def low(n):
            if n % HEADS == HEADS - 1:
                i = n // HEADS
                dve.wait_ge(s.ch, i + 1)
                nc.vector.tensor_tensor(m.guL[:, 4:8, i * P:(i + 1) * P], m.bank[i % 2][:].rearrange("p (d t) -> p d t", d=4),
                                        f(m.guH[:, 4:8, i * P:(i + 1) * P]), ALU.subtract).then_inc(s.cl, 1)
        for n in range(self.N + 6):
            self.steps(n, (0, mask), (1, copy), (2, normalize), (5, low))

    def act(self, act, nc, m, s):
        def exponential(n):
            w = self.of(n)[3]
            act.wait_ge(s.sm, n + 1)
            if n >= 3:
                act.wait_ge(s.tr, n - 2)
            nc.scalar.activation(m.p[:, n % 3, 0:w], m.sm[:, n % 3, 0:w], ACT.Exp, scale=-1.0, bias=m.mn[:, n:n + 1],
                                 accum_out=m.sums[:, n:n + 1]).then_inc(s.ex, 1)

        def high(n):
            if n % HEADS == HEADS - 1:
                i = n // HEADS
                act.wait_ge(s.bt, i + 1)
                nc.scalar.activation(m.guH[:, 4:8, i * P:(i + 1) * P], m.bank[i % 2][:].rearrange("p (d t) -> p d t", d=4),
                                     ACT.Copy).then_inc(s.ch, 1)
        for n in range(self.N + 5):
            self.steps(n, (0, exponential), (4, high))


def pair(t, h, at, n):
    return t[64 * (h % 2):64 * (h % 2) + 64, h // 2, at:at + n]


def low_pair(t, h, at, n):
    return pair(t[h // 4], h % 4, at, n)


def dve_split(dve, nc, x, high, low):
    dve.drain()
    nc.vector.tensor_copy(high, x)
    dve.drain()
    return nc.vector.tensor_tensor(low, x, f(high), ALU.subtract)


class Projections:

    def __init__(self, m, u0, ev0, a):
        self.m, self.u0, self.ev0, self.a = m, u0, ev0, a

    def h(self, k):
        return self.m.hH[:, k], self.m.hL[:, k]

    def banks(self, pe, s, n):
        if n >= 2:
            pe.wait_ge(s.ev, self.ev0 + 2 * n - 2)
        return [self.m.bank[2 * (n % 2) + j][:] for j in range(2)]

    def pe_first(self, pe, s, k):
        pe.wait_ge(s.hl, 8 * self.a + k + 1)

    def pe_tiles(self, pe, nc, s, n, waits=None):
        pe_tiles(pe, nc, self.m, s, self.u0 + n, n % 2, self.banks(pe, s, n), self.h, KD, waits,
                 by_row=waits is not None)

    def pe_rows(self, pe, nc, s, n):
        banks = self.banks(pe, s, n)
        outs = [banks[tt // 2][:, (tt % 2) * COLS:(tt % 2 + 1) * COLS] for tt in range(TT)]
        pe_rows(pe, nc, self.m, s, self.u0 + n, self.h, outs)

    def take(self, act, nc, s, n, outs, func=ACT.Copy):
        act_next(act, nc, self.m, s, self.u0 + n, UNIT)
        for j, (out, bank) in enumerate(outs):
            act.wait_ge(s.mm, 4 + 2 * (self.u0 + n) + j + 1)
            nc.scalar.activation(out, bank, func).then_inc(s.ev, 1)

    def cols(self, act, nc, s, n, t, c, func=ACT.Copy):
        self.take(act, nc, s, n, [(t[:, 2 * c + j], self.m.bank[2 * (n % 2) + j][:]) for j in range(2)], func)

    def rows(self, act, nc, s, n, t, c, func=ACT.Copy):
        self.take(act, nc, s, n, [(t[:, 2 * j:2 * j + 2, c * COLS:(c + 1) * COLS],
                                   self.m.bank[2 * (n % 2) + j][:].rearrange("p (t n) -> p t n", t=2))
                                  for j in range(2)], func)



class Mix1:

    def __init__(self, m, u0, y0, norm, after):
        self.m, self.u0, self.y0, self.norm, self.after = m, u0, y0, norm, after
        self.index = [(i, h) for i in range(1, TT) for h in range(IDX_HEADS)]

        def head(h, i):
            m = self.m
            return ((pair(m.qH, h, i * P, P), low_pair(m.lowA, h, i * P, P)),
                    (pair(m.kH, h, 0, (i + 1) * P), low_pair(m.lowB, h, 0, (i + 1) * P)),
                    m.masks[:, ALIBI_AT[i]:ALIBI_AT[i] + (i + 1) * P], i + 1)
        self.attention = Attention(head, lambda h, b: self.m.v[:, b, h * HD:(h + 1) * HD],
                                   lambda h: 4 + h // 2 + 1)

    def pe(self, pe, nc, m, s):
        u0 = self.u0
        proj = Projections(m, u0, 0, self.norm.a)
        h, tiles, rows = proj.h, (lambda n: proj.pe_tiles(pe, nc, s, n)), (lambda n: proj.pe_rows(pe, nc, s, n))

        proj.pe_tiles(pe, nc, s, 0, lambda k: proj.pe_first(pe, s, k))
        tiles(1)
        pe.wait_ge(s.ev, 2)
        for tt in range(TT):
            mm = nc.tensor.transpose(m.bank[7][:, tt * IDX_HEADS:(tt + 1) * IDX_HEADS], m.rl[0:IDX_HEADS, 0, tt * P:(tt + 1) * P],
                                     m.ident[0:IDX_HEADS, 0:IDX_HEADS])
        mm.then_inc(s.wt, 1)
        rows(2)
        rows(3)
        pe.wait_ge(s.rope, 3)
        for n, (i, hh) in enumerate(self.index):
            if n == 3:
                pe.wait_ge(s.wtd, 1)
            if n >= 4:
                pe.wait_ge(s.relu, n - 3)
            lo, w = 64 * (hh % 2), (i + 1) * P
            pe_3(nc, m.bank[4 + n % 4][:, 0:w], (pair(m.ixH, hh, i * P, P), pair(m.lowB[0], hh, i * P, P)),
                 (m.ixH[lo:lo + 64, 2, 0:w], m.lowB[1][lo:lo + 64, 0, 0:w]), True, True).then_inc(s.lg, 1)
        tiles(4)
        tiles(5)
        pe.wait_ge(s.sgw, 1)
        pe.wait_ge(s.relu, len(self.index))
        for g in range(4):
            for c in range(TT):
                nc.tensor.matmul(m.bank[4 + g][:, c * P:(c + 1) * P], m.ones[0:1, :], m.sgub[0:1, g], start=True, stop=False)
                mm = nc.tensor.matmul(m.bank[4 + g][:, c * P:(c + 1) * P], m.va[:, c, g * P:(g + 1) * P], m.sguT[:, g],
                                      start=False, stop=True)
            mm.then_inc(s.sgu, 1)
        for n in range(6, 10):
            tiles(n)
        rows(10)
        rows(11)
        pe.wait_ge(s.ev, 24)
        pe.wait_ge(s.ao, 4)
        self.attention.pe(pe, nc, m, s)
        pe_mixed_out(pe, nc, m, s, u0 + MIX1_PROJ, self.y0)

    def act_parts(self, act, nc, m, s, n):
        for j in range(4):
            act.wait_ge(s.rope, 3 + 4 * n + j + 1)
            nc.scalar.activation((m.qH, m.kH)[n][:, j], m.full[:, j], ACT.Copy).then_inc(s.hparts, 1)

    def pool_parts(self, pool, nc, m, s):
        for n, (high, low) in enumerate(((m.qH, m.lowA), (m.kH, m.lowB))):
            for j in range(4):
                pool.wait_ge(s.hparts, 4 * n + j + 1)
                nc.gpsimd.tensor_tensor(low[j // 2][:, j % 2], m.full[:, j], f(high[:, j]), ALU.subtract).then_inc(s.parts, 1)

    def act(self, act, nc, m, s):
        u0 = self.u0
        proj = Projections(m, u0, 0, self.norm.a)
        cols = lambda n, t, c, func=ACT.Copy: proj.cols(act, nc, s, n, t, c, func)
        rows = lambda n, t, c, func=ACT.Copy: proj.rows(act, nc, s, n, t, c, func)
        proj.take(act, nc, s, 0, [(m.ix[:, 2], m.bank[0][:]), (m.rl[:, 0], m.bank[1][:])])
        cols(1, m.ix, 0)
        rows(2, m.va, 0, ACT.Gelu)
        rows(3, m.va, 1, ACT.Gelu)
        act.wait_ge(s.wtd, 1)
        for n, (i, hh) in enumerate(self.index):
            act.wait_ge(s.lg, n + 1)
            if n >= 2:
                act.wait_ge(s.lacc, n - 1)
            w = (i + 1) * P
            nc.scalar.activation(m.rl[:, n % 2, 0:w], m.bank[4 + n % 4][:, 0:w], ACT.Relu).then_inc(s.relu, 1)
        cols(4, m.u, 0, ACT.Gelu)
        cols(5, m.u, 1, ACT.Gelu)
        cols(6, m.q, 0)
        cols(7, m.q, 1)
        cols(8, m.k, 0)
        cols(9, m.k, 1)
        rows(10, m.v, 0)
        self.act_parts(act, nc, m, s, 0)
        rows(11, m.v, 1)
        self.act_parts(act, nc, m, s, 1)
        self.attention.act(act, nc, m, s)
        act_mixed_out(act, nc, m, s, u0 + MIX1_PROJ, self.after)

    def dve(self, dve, nc, m, s, gate):

        def rotate(x, other, out):
            dve.drain()
            nc.vector.tensor_tensor(m.ra[:], x, m.cos[:], ALU.mult)
            nc.vector.tensor_tensor(m.rb[:], other, m.sin[:], ALU.mult)
            dve.drain()
            return nc.vector.tensor_tensor(out, m.ra[:], m.rb[:], ALU.add)
        dve.wait_ge(s.swap[0], 16 * 8)
        for j in (2, 0, 1):
            rotate(m.ix[:, j], m.other[j // 2][:, j % 2], m.ra[:])
            dve_split(dve, nc, m.ra[:], m.ixH[:, j], m.lowB[j // 2][:, j % 2]).then_inc(s.rope, 1)
        dve.wait_ge(s.wt, 1)
        nc.vector.tensor_copy(m.wi[:], m.bank[7][:, 0:IDX_HEADS * TT]).then_inc(s.wtd, 1)
        score = [m.masks[:, ALIBI_AT[i]:ALIBI_AT[i] + (i + 1) * P] for i in range(TT)]
        for n, (i, hh) in enumerate(self.index):
            dve.wait_ge(s.relu, n + 1)
            w = m.wi[:, 4 * i + hh:4 * i + hh + 1]
            dve.drain()
            if hh == 0:
                nc.vector.tensor_scalar(score[i], m.rl[:, n % 2, 0:(i + 1) * P], w, None, ALU.mult).then_inc(s.lacc, 1)
            else:
                nc.vector.scalar_tensor_tensor(out=score[i], in0=m.rl[:, n % 2, 0:(i + 1) * P], scalar=w, in1=score[i],
                                               op0=ALU.mult, op1=ALU.add).then_inc(s.lacc, 1)
            if hh == IDX_HEADS - 1:
                dve.drain()
                diagonal = score[i][:, i * P:(i + 1) * P]
                nc.vector.tensor_tensor(diagonal, diagonal, m.tri, ALU.min)
        for i in range(1, TT):
            for _ in range(TOPK // 8):
                dve.drain()
                nc.vector.max(m.m8[:], score[i])
                dve.drain()
                nc.vector.match_replace(score[i], m.m8[:], score[i], TAKEN)
            dve.drain()
            nc.vector.tensor_scalar(score[i], score[i], (BELOW + TAKEN) / 2, NEG, ALU.is_gt, ALU.mult)
        dve.wait_ge(s.ev, 12)
        for g in range(4):
            dve.wait_ge(s.sgu, g + 1)
            dve.drain()
            nc.vector.tensor_tensor(m.ra[:], m.u[:, g], m.bank[4 + g][:], ALU.mult).then_inc(s.ao, 1)
            dve_split(dve, nc, m.ra[:], m.guH[:, g], m.guL[:, g])
        for n, x in enumerate((m.q, m.k)):
            dve.wait_ge(s.swap[1 + n], 16 * (4 if n else 8))
            for j in range(4):
                if n:
                    dve.wait_ge(s.parts, j + 1)
                rotate(x[:, j], m.u[:, j] if n else m.other[j // 2][:, j % 2], m.full[:, j]).then_inc(s.rope, 1)
        self.attention.dve(dve, nc, m, s)
        dve_update(dve, nc, m, s, self.u0 + MIX1_PROJ, gate, self.after)



class Mix2:

    SUMS = (6, 7, 0, 1, 2, 3, 4, 5)
    CHAIN = 8

    def __init__(self, m, u0, y0, norm, after):
        self.m, self.u0, self.y0, self.norm, self.after = m, u0, y0, norm, after

        def head(h, i):
            m = self.m
            if h < 4:
                return ((pair(m.qH, h, i * P, P), low_pair(m.lowA, h, i * P, P)),
                        (pair(m.qH, h + 4, 0, (i + 1) * P), low_pair(m.lowA, h + 4, 0, (i + 1) * P)),
                        m.mdh[:, h % 2, 0:(i + 1) * P], i + 1)
            return ((pair(m.cqH, h - 4, i * P, P), pair(m.lowB[0], h - 4, i * P, P)),
                    (pair(m.memkH, h - 4, 0, 256), pair(m.memkL, h - 4, 0, 256)), m.none[:], 2)

        def value(h, b):
            return self.m.mv[:, b, h * HD:(h + 1) * HD] if h < 4 else self.m.memv[:, b, (h - 4) * HD:(h - 3) * HD]
        self.attention = Attention(head, value, lambda h: 3 + h // 2 if h < 4 else 7 + (h - 4) // 2)

    def chain(self, r):
        m = self.m
        x = m.q[:, r] if r < 4 else (m.cq[:, r - 4] if r < 6 else m.memk[:, r - 6])
        return x, (4 if r < 6 else 2), (8 * r if r < 7 else 52)

    def normalized(self, r):
        return self.m.nf[:, r % 2, 0:self.chain(r)[1] * P]

    def act_spread(self, act, nc, m, s, r):
        _, tiles, at = self.chain(r)
        if r == 0:
            act.wait_ge(s.hn, 1)
        if r >= 2:
            act.wait_ge(s.hx, r - 1)
        nc.scalar.activation(m.rx[:, r % 2, 0:tiles * P].rearrange("p (t e) -> p t e", e=HD),
                             m.hr[:, at:at + 2 * tiles].unsqueeze(2).to_broadcast([P, 2 * tiles, HD]), ACT.Copy)\
            .then_inc(s.rxd, 1)

    def act_high(self, act, nc, m, s, r):
        act.wait_ge(s.hq, r + 1)
        nc.scalar.activation(self.parts(r)[0], self.normalized(r), ACT.Copy).then_inc(s.hparts, 1)

    def pool_parts(self, pool, nc, m, s):
        for r in range(self.CHAIN):
            high, low = self.parts(r)
            pool.wait_ge(s.hparts, r + 1)
            nc.gpsimd.tensor_tensor(low, self.normalized(r), f(high), ALU.subtract).then_inc(s.parts, 1)

    def parts(self, r):
        m = self.m
        if r < 4:
            return m.qH[:, r], m.lowA[r // 2][:, r % 2]
        return (m.cqH[:, r - 4], m.lowB[0][:, r - 4]) if r < 6 else (m.memkH[:, r - 6], m.memkL[:, r - 6])

    def pe(self, pe, nc, m, s):
        proj = Projections(m, self.u0, 4, self.norm.a)
        proj.pe_tiles(pe, nc, s, 0, lambda k: proj.pe_first(pe, s, k))

        def head_sums(at):
            for n in (at, at + 1):
                _, tiles, col = self.chain(self.SUMS[n])
                pe.wait_ge(s.hsq, n + 1)
                for tt in range(tiles):
                    mm = nc.tensor.matmul(m.bank[4][:, col + 2 * tt:col + 2 * tt + 2], m.hs[:, n % 2, tt * P:(tt + 1) * P],
                                          m.sel, start=True, stop=True)
                mm.then_inc(s.hss, 1)

        def spread(r):
            pe.wait_ge(s.rxd, r + 1)
            if r >= 3:
                pe.wait_ge(s.hq, r - 2)
            for tt in range(self.chain(r)[1]):
                mm = nc.tensor.transpose(m.bank[5 + r % 3][:, tt * P:(tt + 1) * P], m.rx[:, r % 2, tt * P:(tt + 1) * P],
                                         m.ident)
            mm.then_inc(s.hx, 1)
        proj.pe_tiles(pe, nc, s, 1)
        head_sums(0)
        proj.pe_tiles(pe, nc, s, 2)
        proj.pe_tiles(pe, nc, s, 3)
        head_sums(2)
        proj.pe_tiles(pe, nc, s, 4)
        head_sums(4)
        pe.wait_ge(s.gw, 16)
        for n in range(8):
            pe.wait_ge(s.xb, n % 4 + 1)
            if n >= 3:
                pe.wait_ge(s.sgm, n - 2)
            nc.tensor.matmul(m.bank[5 + n % 3][:], m.gatew[:, n // 4, n % 4], m.xb[:, n % 4], start=True, stop=True)\
                .then_inc(s.ga, 1)
        proj.pe_tiles(pe, nc, s, 5)
        head_sums(6)
        proj.pe_tiles(pe, nc, s, 6)
        pe.wait_ge(s.sgm, 8)
        for r in range(4):
            spread(r)
        proj.pe_rows(pe, nc, s, 7)
        for r in range(4, self.CHAIN):
            spread(r)
        pe.wait_ge(s.hq, self.CHAIN)
        pe.wait_ge(s.ev, 20)
        self.attention.pe(pe, nc, m, s)
        pe_mixed_out(pe, nc, m, s, self.u0 + MIX2_PROJ, self.y0)

    def act(self, act, nc, m, s):
        proj = Projections(m, self.u0, 4, self.norm.a)
        ig = self.input_gate

        def squares(at):
            for n in (at, at + 1):
                x, tiles, _ = self.chain(self.SUMS[n])
                if n >= 2:
                    act.wait_ge(s.hss, n - 1)
                nc.scalar.activation(m.hs[:, n % 2, 0:tiles * P], x, ACT.Square).then_inc(s.hsq, 1)
        proj.cols(act, nc, s, 0, m.lx, 0)
        squares(0)
        proj.cols(act, nc, s, 1, m.lx, 1)
        proj.cols(act, nc, s, 2, m.q, 0)
        act.wait_ge(s.ev, 10)
        squares(2)
        proj.cols(act, nc, s, 3, m.q, 1)
        act.wait_ge(s.ev, 12)
        squares(4)
        proj.cols(act, nc, s, 4, m.cq, 0)
        for n in range(8):
            at = (V_AB, V_XB)[n // 4] + n % 4
            act.wait_ge(s.ga, n + 1)
            nc.scalar.activation(ig(n - 4) if n >= 4 else m.rg[:, n], m.bank[5 + n % 3][:], ACT.Sigmoid,
                                 bias=m.vec[:, at:at + 1]).then_inc(s.sgm, 1)
        act.wait_ge(s.ev, 14)
        squares(6)
        proj.cols(act, nc, s, 5, m.gl, 0, ACT.Gelu_apprx_tanh)
        act.wait_ge(s.c8, 1)
        for c in range(4):
            nc.scalar.activation(m.lx[:, c], m.rg[:, c], ACT.Exp, scale=m.sp[:, 4, c:c + 1]).then_inc(s.et, 1)
        for c in range(4):
            act.wait_ge(s.et, c + 1)
            nc.scalar.activation(m.rg[:, c], m.rg[:, c], ACT.Tanh, scale=m.sp[:, 5, c:c + 1]).then_inc(s.et, 1)
        act.wait_ge(s.hvar, 1)
        nc.scalar.activation(m.hr[:], m.hv[:], ACT.Sqrt).then_inc(s.hrt, 1)
        for c in range(4):
            act.wait_ge(s.m2, c + 1)
            nc.scalar.activation(m.rg[:, c], m.rg[:, c], ACT.Sqrt).then_inc(s.mult, 1)
        spread = lambda r: self.act_spread(act, nc, m, s, r)
        high = lambda r: self.act_high(act, nc, m, s, r)
        spread(0)
        spread(1)
        proj.cols(act, nc, s, 6, m.gl, 1, ACT.Gelu_apprx_tanh)
        spread(2)
        spread(3)
        for r in range(4):
            high(r)
        spread(4)
        spread(5)
        proj.rows(act, nc, s, 7, m.mv, 0)
        for r in range(4, self.CHAIN):
            high(r)
            if r + 2 < self.CHAIN:
                spread(r + 2)
        self.attention.act(act, nc, m, s)
        act_mixed_out(act, nc, m, s, self.u0 + MIX2_PROJ, self.after)

    def input_gate(self, c):
        return self.m.ig3[:, c] if c < 3 else self.m.ig1[:, 0]

    def dve(self, dve, nc, m, s):
        vec = lambda at: m.vec[:, at:at + 1]
        for c in range(4):
            dve.wait_ge(s.ev, 4 + c + 1)
            nc.vector.tensor_scalar(m.xb[:, c], m.lx[:, c], vec(V_CONVW + 12 + c), vec(V_CONVB + c), ALU.mult, ALU.add)
            for back in range(1, 4):
                dve.drain()
                mm = nc.vector.scalar_tensor_tensor(out=m.xb[:, c, back:], in0=m.lx[:, c, 0:T - back],
                                                    scalar=vec(V_CONVW + 4 * (3 - back) + c), in1=m.xb[:, c, back:],
                                                    op0=ALU.mult, op1=ALU.add)
            mm.then_inc(s.xb, 1)
        for c in range(4):
            dve.drain()
            dve.wait_ge(s.et, 4 + c + 1)
            nc.vector.tensor_tensor(m.la[:], m.lx[:, c], m.lx[:, c], ALU.mult)
            dve.drain()
            nc.vector.scalar_tensor_tensor(out=m.rg[:, c], in0=m.la[:], scalar=1.0, in1=m.rg[:, c], op0=ALU.add,
                                           op1=ALU.mult).then_inc(s.m2, 1)
            if c == 0:
                dve.wait_ge(s.hss, self.CHAIN)
                nc.vector.tensor_scalar(m.hv[:], m.bank[4][:, 0:56], 1.0 / HD, EPS, ALU.mult, ALU.add).then_inc(s.hvar, 1)
        newton(dve, nc, s.hrt, 1, m.hv[:], m.hr[:], m.ht[:]).then_inc(s.hn, 1)

        def normalize(r):
            x, tiles, _ = self.chain(r)
            if r >= 2:
                dve.wait_ge(s.parts, r - 1)
            dve.wait_ge(s.hx, r + 1)
            nc.vector.scalar_tensor_tensor(out=self.normalized(r), in0=x, scalar=vec(V_GAINS + r // 2),
                                           in1=m.bank[5 + r % 3][:, 0:tiles * P], op0=ALU.mult, op1=ALU.mult)\
                .then_inc(s.hq, 1)

        def recur(c):
            dve.drain()
            nc.vector.tensor_tensor(m.la[:], m.xb[:, c], self.input_gate(c), ALU.mult)
            dve.wait_ge(s.mult, c + 1)
            nc.vector.memset(m.rg[:, c, 0:1], 1.0)
            dve.drain()
            nc.vector.tensor_tensor(m.la[:], m.la[:], m.rg[:, c], ALU.mult)
            dve.drain()
            nc.vector.tensor_tensor_scan(m.lb[:], m.lx[:, c], m.la[:], 0.0, ALU.mult, ALU.add)
            dve.drain()
            dve.wait_ge(s.ev, 14 + c + 1)
            nc.vector.tensor_tensor(m.la[:], m.lb[:], m.gl[:, c], ALU.mult)
            dve_split(dve, nc, m.la[:], m.guH[:, c], m.guL[:, c])
        dve.wait_ge(s.sgm, 8)
        recur(0)
        normalize(0)
        normalize(1)
        recur(1)
        normalize(2)
        normalize(3)
        recur(2)
        recur(3)
        for r in range(4, self.CHAIN):
            normalize(r)

        def mask_ready(n):
            if n % HEADS < 4:
                dve.wait_ge(s.mkd, n // HEADS * 4 + n % HEADS + 1)
        self.attention.dve(dve, nc, m, s, mask_ready)
        dve_update(dve, nc, m, s, self.u0 + MIX2_PROJ, lambda d: 1.0, self.after)

    def pool_masks(self, pool, nc, m, s, tiles):
        for i in tiles:
            for h in range(4):
                before = HEADS * i + h - 2 if h >= 2 else HEADS * (i - 1) + h + 2
                if h >= 2 or i:
                    pool.wait_ge(s.sm, before + 1)
                else:
                    pool.wait_ge(s.ev, 20)
                w = (i + 1) * P
                nc.gpsimd.tensor_scalar(m.mdh[:, h % 2, 0:w], m.masks[:, ALIBI_AT[i]:ALIBI_AT[i] + w], 4.0 ** -(h + 1), None,
                                        ALU.mult).then_inc(s.mkd, 1)


def dve_decay_rates(dve, nc, m, s):
    lam, (size, e, z, z2, minus, rate) = m.vec[:, V_LAM:V_LAM + 4], [m.sp[:, j] for j in range(6)]
    nc.vector.scalar_tensor_tensor(out=size, in0=lam, scalar=-1.0, in1=lam, op0=ALU.mult, op1=ALU.max).then_inc(s.lam, 1)
    dve.wait_ge(s.elam, 1)
    nc.vector.tensor_scalar(z, e, 2.0, None, ALU.add)
    dve.drain()
    nc.vector.reciprocal(z, z)
    dve.drain()
    nc.vector.tensor_tensor(z, z, e, ALU.mult)
    dve.drain()
    nc.vector.tensor_tensor(z2, z, z, ALU.mult)
    nc.vector.memset(rate, 1.0 / 17)
    for n in range(15, 0, -2):
        dve.drain()
        nc.vector.tensor_tensor(rate, rate, z2, ALU.mult)
        dve.drain()
        nc.vector.tensor_scalar(rate, rate, 1.0 / n, None, ALU.add)
    nc.vector.tensor_scalar(size, lam, -1.0, 0.0, ALU.mult, ALU.max)
    dve.drain()
    nc.vector.scalar_tensor_tensor(out=rate, in0=rate, scalar=2.0, in1=z, op0=ALU.mult, op1=ALU.mult)
    dve.drain()
    nc.vector.tensor_tensor(rate, rate, size, ALU.add)
    dve.drain()
    nc.vector.tensor_scalar(minus, rate, -8.0, None, ALU.mult)
    nc.vector.tensor_scalar(rate, rate, 8.0, None, ALU.mult).then_inc(s.c8, 1)


def sp_swap(sp, others, x, tiles, sem):
    half = HD // 8
    for lo in (0, HD):
        for e in range(2):
            to, of = lo + half * e, lo + half * (1 - e)
            for j, other in enumerate(others):
                n = min(tiles - 2 * j, tiles // len(others) + tiles % 2)
                sp.dma_start(other[to:to + half, 0:n], x[of:of + half, 2 * j:2 * j + n]).then_inc(sem, 16)


def pe_mixed_out(pe, nc, m, s, u, y0):
    pe.wait_ge(s.cl, TT)
    cat = lambda k: (m.guH[:, k], m.guL[:, k])
    for q in range(OUT_UNITS):
        pe.wait_ge(s.y, y0 + 2 * q + 2)
        pe_tiles(pe, nc, m, s, u + q, q % 2, [m.bank[4 + 2 * (q % 2)][:], m.bank[5 + 2 * (q % 2)][:]], cat, KD)


def act_mixed_out(act, nc, m, s, u, after):
    for q in range(OUT_UNITS):
        act_next(act, nc, m, s, u + q, UNIT)
        after.act_square(act, nc, m, s, 2 * q)
        after.act_square(act, nc, m, s, 2 * q + 1)



def signals(nc, tag, first):
    s = Signals()
    s.all = []

    def new(name):
        s.all.append(nc.alloc_semaphore(f"{tag}_{name}"))
        return s.all[-1]
    s.full = [new("full0"), new("full1")]
    s.high = new("high")
    s.low = new("low")
    s.mm = new("mm")
    s.silu = new("silu")
    s.ufree = new("ufree")
    s.gu = new("gu")
    s.y = new("y")
    s.sq = new("sq")
    s.acc = new("acc")
    s.ss = new("ss")
    s.var = new("var")
    s.rt = new("rt")
    s.dg = new("dg")
    s.spread = new("spread")
    s.tt = new("tt")
    s.hh = new("hh")
    s.hl = new("hl")
    s.ev = new("ev")
    s.sm = new("sm")
    s.sc = new("sc")
    s.ex = new("ex")
    s.pc = new("pc")
    s.tr = new("tr")
    s.av = new("av")
    s.on = new("on")
    s.bt = new("bt")
    s.cl = new("cl")
    s.hparts = new("hparts")
    s.parts = new("parts")
    s.ch = new("ch")
    if first:
        s.swap = [new("swap0"), new("swap1"), new("swap2")]
        s.clear = new("clear")
        s.mod_full = [new("mod_full0"), new("mod_full1")]
        s.mod_used = new("mod_used")
        s.crow = new("crow")
        s.csil = new("csil")
        s.par = new("par")
        s.rope = new("rope")
        s.lg = new("lg")
        s.relu = new("relu")
        s.wt = new("wt")
        s.wtd = new("wtd")
        s.lacc = new("lacc")
        s.sgw = new("sgw")
        s.sgu = new("sgu")
        s.ao = new("ao")
    else:
        s.vec = new("vec")
        s.dist = new("dist")
        s.gw = new("gw")
        s.mem = new("mem")
        s.lam = new("lam")
        s.elam = new("elam")
        s.c8 = new("c8")
        s.xb = new("xb")
        s.ga = new("ga")
        s.sgm = new("sgm")
        s.et = new("et")
        s.m2 = new("m2")
        s.mult = new("mult")
        s.hsq = new("hsq")
        s.hss = new("hss")
        s.hvar = new("hvar")
        s.hrt = new("hrt")
        s.hn = new("hn")
        s.rxd = new("rxd")
        s.hx = new("hx")
        s.hq = new("hq")
        s.mkd = new("mkd")
        s.st = new("st")
    return s


def setup_block(nc, m, a):
    s = Signals()
    s.ld = nc.alloc_semaphore("i_loaded")
    s.c = nc.alloc_semaphore("i_c")
    s.cx = nc.alloc_semaphore("i_x")
    s.ms = nc.alloc_semaphore("i_set")
    s.sq = nc.alloc_semaphore("i_sq")
    s.acc = nc.alloc_semaphore("i_acc")
    first = Norm(None, 0, None)
    s.big = [nc.alloc_semaphore(f"i_big{q}") for q in range(4)]
    s.bias = nc.alloc_semaphore("i_bias")
    s.sil = nc.alloc_semaphore("i_silu")
    s.ang = nc.alloc_semaphore("i_angles")
    with nc.Block() as block:
        @block.sync
        def _(sp):
            sp.dma_start(m.pos[:], a["positions"].partition_broadcast(P)).then_inc(s.ld, 16)
            sp.dma_start(m.cst[:], a["constants"]).then_inc(s.ld, 16)
            sp.dma_start(m.c[:], a["c"].partition_broadcast(P)).then_inc(s.c, 16)
            sp.dma_start(m.x[:], a["x"]).then_inc(s.cx, 16)
            sp.dma_start(m.mod_b[:], a["ada_b"][LAYERS - 1]).then_inc(s.bias, 16)
            for q in range(4):
                piece = a["ada_w"][LAYERS - 1, N_MOD - 2 + q // 2, 4 * (q % 2):4 * (q % 2) + 4]
                sp.dma_start(m.mod_big[:, q], piece.rearrange("t p k -> p t k")).then_inc(s.big[q], 16)

        @block.vector
        def _(dve):
            nc.vector.memset(m.ones[:], 1.0)
            nc.vector.memset(m.zero[:], 0.0)
            nc.vector.memset(m.halfpi[:], float(np.pi / 2)).then_inc(s.ms, 1)
            dve.wait_ge(s.ld, 32)
            nc.vector.tensor_copy(m.warm[:], m.ident)
            nc.vector.tensor_copy(m.ang[:], m.pos[:])
            dve.drain()
            nc.vector.tensor_scalar(m.ang[:], m.ang[:], m.freq, None, ALU.mult)
            dve.drain()
            nc.vector.tensor_scalar(m.turn[:], m.ang[:], float(1 / (2 * np.pi)), MAGIC, ALU.mult, ALU.add)
            dve.drain()
            nc.vector.tensor_scalar(m.turn[:], m.turn[:], -MAGIC, None, ALU.add)
            for part in TWO_PI_PARTS:
                dve.drain()
                nc.vector.scalar_tensor_tensor(out=m.ang[:], in0=m.turn[:], scalar=-part, in1=m.ang[:], op0=ALU.mult, op1=ALU.add)
            dve.drain()
            nc.vector.tensor_scalar(m.ang[:], m.ang[:], 3.1415925, -3.1415925, ALU.min, ALU.max)
            dve.drain()
            nc.vector.scalar_tensor_tensor(out=m.turn[:], in0=m.ang[:], scalar=-1.0, in1=m.ang[:], op0=ALU.mult, op1=ALU.max)\
                .then_inc(s.ang, 1)
            for d in range(KD):
                first.dve_add(dve, nc, m, s, d)
            dve.wait_ge(s.sil, 1)
            dve.wait_ge(s.bias, 16)
            for c in range(2):
                dve.drain()
                for k in range(KD):
                    if k % 4 == 0:
                        dve.wait_ge(s.big[2 * c + k // 4], 16)
                    mod_sum(nc, m, m.mod_big[:, 2 * c + k // 4, k % 4], k)
                dve.drain()
                at = (N_MOD - 2 + c) * KD
                nc.vector.tensor_tensor(m.mod[:, at + 2 * KD:at + 3 * KD], m.red[:], m.mod_b[:, at:at + KD], ALU.add)

        @block.scalar
        def _(act):
            act.wait_ge(s.c, 16)
            nc.scalar.activation(m.c[:], m.c[:], ACT.Silu).then_inc(s.sil, 1)
            act.wait_ge(s.ms, 1)
            act.wait_ge(s.ang, 1)
            nc.scalar.activation(m.sin[:], m.ang[:], ACT.Sin)
            nc.scalar.activation(m.cos[:], m.turn[:], ACT.Sin, scale=-1.0, bias=m.halfpi[:])
            act.wait_ge(s.cx, 16)
            for d in range(KD):
                first.act_square(act, nc, m, s, d)


def layer_block(nc, m, s, a, l):
    norms = [Norm(0, None, 0), Norm(1, 0, 1, y0=KD, warm=BETWEEN), Norm(2, 1, 2, y0=2 * KD, warm=BETWEEN),
             Norm(None, 2, None, y0=4 * KD)]
    ffn1 = Ffn(0, L_FFN1, 0, norms[0], norms[1], UNIT)
    mix = Mix1(m, L_MIX, 2 * KD, norms[1], norms[2])
    ffn2 = Ffn(1, L_FFN2, 3 * KD, norms[2], norms[3], 0)
    mod1, mod2 = Modulation(a["ada_w"][l], 0, 3), Modulation(a["ada_w"][l], 6, None)
    hH, hL = (lambda k: m.hH[:, k]), (lambda k: m.hL[:, k])
    shift = lambda chunk: (lambda k: m.mod[:, chunk * KD + k:chunk * KD + k + 1])
    scale = lambda k: m.A[:, k:k + 1]
    gate = lambda d: m.gate[:, d:d + 1]

    def dve_scale_of(dve, n):
        dve.drain()
        at = (3 * n + 1) * KD
        nc.vector.scalar_tensor_tensor(out=m.A[:], in0=m.mod[:, at:at + KD], scalar=1.0, in1=m.gains[:, n * KD:(n + 1) * KD],
                                       op0=ALU.add, op1=ALU.mult)
        dve.drain()

    with nc.Block() as block:
        @block.sync
        def _(sp):
            w_in = lambda g: (lambda i: a["ffn_in"][(2 * l + g) * IN_UNITS + i])
            w_a = lambda g: (lambda i: a["ffn_out_a"][(2 * l + g) * OUT_UNITS + i])
            w_b = lambda g: (lambda i: a["ffn_out_b"][(2 * l + g) * OUT_UNITS + i])
            sp.dma_start(m.mod_b[:], a["ada_b"][l]).then_inc(s.par, 16)
            sp.dma_start(m.gains[:], a["gains"][l]).then_inc(s.par, 16)
            ffn1.sp(sp, m, s, w_in(0), w_a(0), w_b(0), mod1)
            sp_units(sp, m, s, lambda i: a["mix"][l, i], L_MIX, 2, UNIT)
            sp.wait_ge(s.mod_used, 6 * KD + MOD_SLOTS)
            sp.dma_start(m.sguT[:], a["sgu_w"][l]).then_inc(s.par, 16)
            sp.dma_start(m.sgub[0:1], a["sgu_b"][l]).then_inc(s.par, 16)
            sp.dma_start(m.masks[:, 0:P], a["causal"]).then_inc(s.par, 16)
            unit = lambda n: sp_unit(sp, m, s, a["mix"][l, n], L_MIX + n, UNIT)
            unit(2)
            unit(3)
            sp.wait_ge(s.ev, 4)
            sp.wait_ge(s.clear, 1)
            sp_swap(sp, m.other, m.ix, 3, s.swap[0])
            sp_units(sp, m, s, lambda i: a["mix"][l, 4 + i], L_MIX + 4, 6, UNIT)
            sp.wait_ge(s.ev, 16)
            sp.wait_ge(s.rope, 3)
            sp_swap(sp, m.other, m.q, 4, s.swap[1])
            unit(10)
            unit(11)
            sp.wait_ge(s.ev, 20)
            sp.wait_ge(s.ao, 4)
            sp_swap(sp, [m.u], m.k, 4, s.swap[2])
            sp.dma_start(m.c[:], a["c"].partition_broadcast(P)).then_inc(s.crow, 16)
            sp_units(sp, m, s, lambda i: a["mix"][l, MIX1_PROJ + i], L_MIX + MIX1_PROJ, OUT_UNITS, UNIT)
            ffn2.sp(sp, m, s, w_in(1), w_a(1), w_b(1), mod2)

        @block.gpsimd
        def _(pool):
            pool.sem_inc(s.low, 2)
            runs = lambda x: ((x.u0, IN_A, UNIT), (x.ua, OUT_UNITS, UNIT_A), (x.ub, IN_B, UNIT), (x.uc, OUT_UNITS, UNIT_B))
            for run in runs(ffn1):
                pool_low(pool, nc, m, s, *run)
            pool.wait_ge(s.low, L_MIX + 2)
            nc.gpsimd.memset(m.other[0][:], 0.0)
            nc.gpsimd.memset(m.other[1][:], 0.0).then_inc(s.clear, 1)
            pool_low(pool, nc, m, s, L_MIX, 4, UNIT)
            pool.wait_ge(s.par, 80)
            nc.gpsimd.affine_select(out=m.sguT[:], in_=m.sguT[:], pattern=[[0, 4], [1, P]], compare_op=ALU.is_ge, fill=0.0,
                                    base=0, channel_multiplier=-1).then_inc(s.sgw, 1)
            pool_low(pool, nc, m, s, L_MIX + 4, MIX1_PROJ - 4, UNIT)
            mix.pool_parts(pool, nc, m, s)
            pool_low(pool, nc, m, s, L_MIX + MIX1_PROJ, OUT_UNITS, UNIT)
            for run in runs(ffn2):
                pool_low(pool, nc, m, s, *run)

        @block.scalar
        def _(act):
            act.sem_inc(s.silu, 2)
            norms[0].act_sqrt(act, nc, m, s)
            act_high(act, nc, m, s, 0, 0, 0, UNIT)
            act_high(act, nc, m, s, 1, 1, 0, UNIT)
            norms[0].act_apply(act, nc, m, s, hH, shift(0))
            ffn1.act(act, nc, m, s)
            norms[1].act_sqrt(act, nc, m, s)
            norms[1].act_apply(act, nc, m, s, hH, shift(3))
            mix.act(act, nc, m, s)
            norms[2].act_sqrt(act, nc, m, s)
            norms[2].act_apply(act, nc, m, s, hH, shift(6))
            act.wait_ge(s.crow, 16)
            nc.scalar.activation(m.c[:], m.c[:], ACT.Silu).then_inc(s.csil, 1)
            ffn2.act(act, nc, m, s)

        @block.vector
        def _(dve):
            dve.sem_inc(s.ufree, 2)
            dve.sem_inc(s.y, 4)
            dve.sem_inc(s.mod_used, MOD_SLOTS)
            nc.vector.tensor_copy(m.mod[:, 0:2 * KD], m.mod[:, N_MOD * KD:(N_MOD + 2) * KD])
            dve.wait_ge(s.par, 32)
            dve_scale_of(dve, 0)
            norms[0].dve_rsqrt(dve, nc, m, s)
            norms[0].dve_apply(dve, nc, m, s, hH, hL, scale, shift(0))
            ffn1.dve(dve, nc, m, s, gate, mod1, half_gate=2)
            dve_scale_of(dve, 1)
            norms[1].dve_rsqrt(dve, nc, m, s)
            norms[1].dve_apply(dve, nc, m, s, hH, hL, scale, shift(3))
            mix.dve(dve, nc, m, s, lambda d: m.mod[:, 5 * KD + d:5 * KD + d + 1])
            dve_scale_of(dve, 2)
            norms[2].dve_rsqrt(dve, nc, m, s)
            norms[2].dve_apply(dve, nc, m, s, hH, hL, scale, shift(6))
            dve.wait_ge(s.csil, 1)
            ffn2.dve(dve, nc, m, s, gate, mod2, half_gate=8)

        @block.tensor
        def _(pe):
            pe.sem_inc(s.mm, 4)
            norms[0].pe_sum(pe, nc, m, s)
            norms[0].pe_spread(pe, nc, m, s)
            ffn1.pe(pe, nc, m, s)
            norms[1].pe_sum(pe, nc, m, s)
            norms[1].pe_spread(pe, nc, m, s)
            mix.pe(pe, nc, m, s)
            norms[2].pe_sum(pe, nc, m, s)
            norms[2].pe_spread(pe, nc, m, s)
            ffn2.pe(pe, nc, m, s)

    with nc.Block() as block:
        @block.gpsimd
        def _(pool):
            for x in s.all:
                pool.sem_clear(x)


def second_block(nc, m, s, a):
    norms = [Norm(0, None, None), Norm(1, 0, 0, tokens=256, src=lambda m: m.mem), Norm(2, 1, 1, y0=0, warm_bank=5),
             Norm(3, 2, 2, y0=2 * KD, warm=BETWEEN), Norm(4, 3, 3, y0=3 * KD, warm=BETWEEN)]
    ffn1 = Ffn(0, S_FFN1, KD, norms[2], norms[3], UNIT)
    mix = Mix2(m, S_MIX, 3 * KD, norms[3], norms[4])
    ffn2 = Ffn(1, S_FFN2, 4 * KD, norms[4], None, 0)
    hH, hL = (lambda k: m.hH[:, k]), (lambda k: m.hL[:, k])
    halves = lambda t: t.rearrange("p a (b n) -> p (a b) n", b=2)
    memH, memL = halves(m.guH[:, 0:4]), halves(m.guL[:, 4:8])
    gain = lambda at: (lambda k: m.vec[:, at + k:at + k + 1])
    half = lambda d: 0.5

    with nc.Block() as block:
        @block.sync
        def _(sp):
            w_in = lambda g: (lambda i: a["ffn_in"][(2 * LAYERS + g) * IN_UNITS + i])
            w_a = lambda g: (lambda i: a["ffn_out_a"][(2 * LAYERS + g) * OUT_UNITS + i])
            w_b = lambda g: (lambda i: a["ffn_out_b"][(2 * LAYERS + g) * OUT_UNITS + i])
            sp.dma_start(m.vec[:], a["vec"]).then_inc(s.vec, 16)
            sp_unit(sp, m, s, a["mem_kv"][0], 0, UNIT)
            sp_unit(sp, m, s, a["mem_kv"][1], 1, UNIT)
            sp.dma_start(m.mem[:], a["mem"]).then_inc(s.mem, 16)
            sp.dma_start(m.masks[:], a["alibi"]).then_inc(s.dist, 16)

            ffn1.sp(sp, m, s, w_in(0), w_a(0), w_b(0))
            sp_units(sp, m, s, lambda i: a["mix_2"][i], S_MIX, 2, UNIT)
            sp.wait_ge(s.y, 4 + 3 * KD)
            sp.dma_start(m.gatew[:], a["gate_w"]).then_inc(s.gw, 16)
            sp_units(sp, m, s, lambda i: a["mix_2"][2 + i], S_MIX + 2, MIX2_PROJ + OUT_UNITS - 2, UNIT)
            ffn2.sp(sp, m, s, w_in(1), w_a(1), w_b(1))
            for d in range(0, KD, 2):
                sp.wait_ge(s.y, 4 + 5 * KD + d + 2)
                sp.dma_start(a["out"][:, d:d + 2], m.x[:, d:d + 2]).then_inc(s.st, 16)
            sp.wait_ge(s.st, 16 * KD // 2)

        @block.gpsimd
        def _(pool):
            pool.sem_inc(s.low, 2)
            nc.gpsimd.memset(m.none[:], 0.0)
            runs = lambda x: ((x.u0, IN_A, UNIT), (x.ua, OUT_UNITS, UNIT_A), (x.ub, IN_B, UNIT), (x.uc, OUT_UNITS, UNIT_B))
            pool_low(pool, nc, m, s, 0, MEM_UNITS, UNIT)
            for run in runs(ffn1):
                pool_low(pool, nc, m, s, *run)
            pool_low(pool, nc, m, s, S_MIX, MIX2_PROJ, UNIT)
            mix.pool_parts(pool, nc, m, s)
            pool.wait_ge(s.dist, 16)
            for q in range(3):
                mix.pool_masks(pool, nc, m, s, (0,) if q == 0 else ((1,) if q == 1 else (2, 3)))
                if q < 2:
                    pool.wait_ge(s.high, S_MIX + MIX2_PROJ + q + 1)
                    pool_unit(pool, nc, m, s, q).then_inc(s.low, 1)
            pool_low(pool, nc, m, s, S_MIX + MIX2_PROJ + 2, OUT_UNITS - 2, UNIT)
            for run in runs(ffn2):
                pool_low(pool, nc, m, s, *run)

        @block.scalar
        def _(act):
            act.sem_inc(s.silu, 2)
            act.wait_ge(s.vec, 16)
            norms[0].act_sqrt(act, nc, m, s)
            act.wait_ge(s.mem, 16)
            for d in range(KD):
                norms[1].act_square(act, nc, m, s, d)
            act_high(act, nc, m, s, 0, 0, 0, UNIT)
            act_high(act, nc, m, s, 1, 1, 0, UNIT)
            norms[1].act_sqrt(act, nc, m, s)
            norms[1].act_apply(act, nc, m, s, lambda k: memH[:, k])
            for d in range(KD):
                norms[2].act_square(act, nc, m, s, d)
            for n, t in enumerate((m.memk, m.memv)):
                act_next(act, nc, m, s, n, UNIT)
                for j in range(2):
                    act.wait_ge(s.mm, 4 + 2 * n + j + 1)
                    nc.scalar.activation(t[:, j], m.bank[2 * n + j][:, 0:256], ACT.Copy).then_inc(s.ev, 1)
            norms[2].act_sqrt(act, nc, m, s)
            norms[2].act_apply(act, nc, m, s, hH)
            act.wait_ge(s.lam, 1)
            nc.scalar.activation(m.sp[:, 1], m.sp[:, 0], ACT.Exp, scale=-1.0).then_inc(s.elam, 1)
            ffn1.act(act, nc, m, s)
            norms[3].act_sqrt(act, nc, m, s)
            norms[3].act_apply(act, nc, m, s, hH)
            mix.act(act, nc, m, s)
            norms[4].act_sqrt(act, nc, m, s)
            norms[4].act_apply(act, nc, m, s, hH)
            ffn2.act(act, nc, m, s)

        @block.vector
        def _(dve):
            dve.sem_inc(s.ufree, 2)
            dve.sem_inc(s.y, 4)
            norms[0].dve_rsqrt(dve, nc, m, s)
            dve.wait_ge(s.vec, 16)
            dve.wait_ge(s.spread, 1)
            for d in range(KD):
                nc.vector.scalar_tensor_tensor(out=m.x[:, d], in0=m.x[:, d], scalar=m.vec[:, V_FINAL + d:V_FINAL + d + 1],
                                               in1=m.bank[7][:], op0=ALU.mult, op1=ALU.mult).then_inc(s.y, 1)
            for d in range(KD):
                norms[1].dve_add(dve, nc, m, s, d)
            norms[1].dve_rsqrt(dve, nc, m, s)
            norms[1].dve_apply(dve, nc, m, s, lambda k: memH[:, k], lambda k: memL[:, k], gain(V_MEM))
            for n in (2, 3, 4):
                if n == 2:
                    for d in range(KD):
                        norms[n].dve_add(dve, nc, m, s, d)
                norms[n].dve_rsqrt(dve, nc, m, s)
                norms[n].dve_apply(dve, nc, m, s, hH, hL, gain({2: V_FFN1, 3: V_MIX, 4: V_FFN2}[n]))
                if n == 2:
                    dve_decay_rates(dve, nc, m, s)
                    ffn1.dve(dve, nc, m, s, half)
                elif n == 3:
                    mix.dve(dve, nc, m, s)
                else:
                    ffn2.dve(dve, nc, m, s, half)

        @block.tensor
        def _(pe):
            pe.sem_inc(s.mm, 4)
            for n in range(2):
                norms[n].pe_sum(pe, nc, m, s)
                norms[n].pe_spread(pe, nc, m, s)
            mem = lambda k: (memH[:, k], memL[:, k])
            pe_tiles(pe, nc, m, s, 0, 0, [m.bank[0][:, 0:256], m.bank[1][:, 0:256]], mem, KD,
                     lambda k: pe.wait_ge(s.hl, k + 1), by_row=True)
            pe_rows(pe, nc, m, s, 1, mem, [m.bank[2][:, 0:256], m.bank[3][:, 0:256]])
            norms[2].pe_sum(pe, nc, m, s)
            norms[2].pe_spread(pe, nc, m, s)
            pe.wait_ge(s.ev, 4)
            ffn1.pe(pe, nc, m, s)
            norms[3].pe_sum(pe, nc, m, s)
            norms[3].pe_spread(pe, nc, m, s)
            mix.pe(pe, nc, m, s)
            norms[4].pe_sum(pe, nc, m, s)
            norms[4].pe_spread(pe, nc, m, s)
            ffn2.pe(pe, nc, m, s)


def program(nc, a, layers=LAYERS, second=True, debug=None):
    m = memory(nc)
    setup_block(nc, m, a)
    s = signals(nc, "l", True)
    with nc.Fori(0, layers) as l:
        layer_block(nc, m, s, a, l)
    if second:
        second_block(nc, m, signals(nc, "s", False), a)
    if debug:
        st = nc.alloc_semaphore("dbg")
        with nc.Block() as block:
            @block.sync
            def _(sp):
                sp.dma_start(a["out"], m.x[:]).then_inc(st, 16)
                sp.wait_ge(st, 16)

def tiles_of(x):
    return np.ascontiguousarray(x.reshape(-1, P, x.shape[-1]).transpose(1, 0, 2))


def column(v, n):
    return np.ascontiguousarray(np.asarray(v).reshape(n, P).T)


def units(w):
    rows, cols = w.shape
    w = w.reshape(rows // P, P, cols // COLS, COLS).transpose(2, 1, 0, 3)
    return w.reshape(cols // COLS, P, -1)


def ffn_units(w_in, w_out):
    pairs = [units(w_in[:, :DFF]), units(w_in[:, DFF:])]
    both = np.stack(pairs, axis=1).reshape(IN_UNITS, P, UNIT)
    return both, units(w_out[:FT_A * P]), units(w_out[FT_A * P:])


def mix1_units(w_in, w_out):
    sgu = D // 2
    u, v_a, q, k, v = (w_in[:, i * sgu:(i + 1) * sgu] for i in range(5))
    at = 5 * sgu
    iq, ik, iw = w_in[:, at:at + 256], w_in[:, at + 256:at + 320], w_in[:, at + 320:at + 324]
    first = np.concatenate([ik, ik, iw, np.zeros((D, COLS - 132), w_in.dtype)], axis=1)
    return units(np.concatenate([first, iq, v_a, u, q, k, v, w_out], axis=1))


def mix2_units(w_in, w_out):
    x, g, q, k, v, cq = np.split(w_in, [512, 1024, 1280, 1536, 1792], axis=1)
    return units(np.concatenate([x, q, k, cq, g, v, w_out], axis=1))


def block_diagonal(w):
    out = np.zeros((P, 4, P), w.dtype)
    for n in range(8):
        lo = 64 * (n % 2)
        out[lo:lo + 64, n // 2, lo:lo + 64] = w[n]
    return out


def constants():
    c = np.zeros((P, C_WIDTH), np.float32)
    c[:, C_IDENT:C_IDENT + P] = np.eye(P)
    half = HD // 8
    q, k = np.arange(P)[:, None], np.arange(P)[None, :]
    c[:, C_TRI:C_TRI + P] = np.where(k <= q, BIG, BELOW)
    c[:HD, C_SEL] = 1.0
    c[HD:, C_SEL + 1] = 1.0
    inv = np.float32(500000.0) ** (-np.arange(0, 2 * half, 2, dtype=np.float32) / np.float32(2 * half))
    for d in range(P):
        if d % HD < 2 * half:
            c[d, C_FREQ] = inv[d % half] * (-1 if d % HD < half else 1)
    causal = np.where(k <= q, 0.0, NEG).astype(np.float32)
    alibi = np.zeros((P, MASKS), np.float32)
    for i in range(TT):
        keys = np.arange((i + 1) * P)[None, :]
        away = i * P + q - keys
        alibi[:, ALIBI_AT[i]:ALIBI_AT[i] + (i + 1) * P] = np.where(away >= 0, -8.0 * away, NEG)
    return c, causal, alibi


def in_order_of_use(chunks):
    return np.concatenate([chunks[:, 2:], np.roll(chunks[:, :2], -1, axis=0)], axis=1)


def lay_out(v):
    ffns = [ffn_units(v[f"ffn{n}_w_in"][l], v[f"ffn{n}_w_out"][l]) for l in range(LAYERS) for n in (1, 2)]
    ffns += [ffn_units(v[f"ffn{n}_w_in_2"][0], v[f"ffn{n}_w_out_2"][0]) for n in (1, 2)]
    cst, causal, alibi = constants()
    vec = [column(v["final_norm"], 8), column(v["mem_norm_2"][0], 8), column(v["ffn1_norm_2"][0], 8),
           column(v["mix_norm_2"][0], 8), column(v["ffn2_norm_2"][0], 8)]
    vec += [column(v["lru_conv_w_2"][0][j], 4) for j in range(4)]
    vec += [column(v["lru_conv_b_2"][0], 4), column(v["lru_a_b_2"][0].reshape(-1), 4),
            column(v["lru_x_b_2"][0].reshape(-1), 4), column(v["lru_lambda_2"][0], 4)]
    vec += [column(np.tile(v[n][0], 2), 1) for n in ("moba_q_norm_2", "moba_k_norm_2", "mem_q_norm_2", "mem_k_norm_2")]
    return {
        "x": tiles_of(v["x"][0].T),
        "c": v["c"].reshape(1, D),
        "positions": v["positions"].reshape(1, T),
        "constants": cst, "causal": causal, "alibi": alibi,
        "ada_w": in_order_of_use(v["ada_w"].transpose(0, 2, 1).reshape(LAYERS, N_MOD, KD, P, D)),
        "ada_b": in_order_of_use(v["ada_b"].reshape(LAYERS, N_MOD, KD, P)).reshape(LAYERS, N_MOD * KD, P).transpose(0, 2, 1),
        "gains": np.stack([np.concatenate([column(v[n][l], KD) for n in ("norm_ffn1", "norm_mix", "norm_ffn2")], axis=1)
                           for l in range(LAYERS)]),
        "ffn_in": np.concatenate([x[0] for x in ffns]),
        "ffn_out_a": np.concatenate([x[1] for x in ffns]),
        "ffn_out_b": np.concatenate([x[2] for x in ffns]),
        "mix": np.stack([mix1_units(v["mix_w_in"][l], v["mix_w_out"][l]) for l in range(LAYERS)]),
        "sgu_w": v["sgu_w"].transpose(0, 3, 1, 2),
        "sgu_b": v["sgu_b"].reshape(LAYERS, 1, 4, P),
        "mem": tiles_of(v["mem_2"][0].T),
        "mem_kv": units(v["mem_w_kv_2"][0]),
        "mix_2": mix2_units(v["w_in_2"][0], v["w_out_2"][0]),
        "vec": np.concatenate(vec, axis=1),
        "gate_w": np.stack([block_diagonal(v["lru_a_w_2"][0]), block_diagonal(v["lru_x_w_2"][0])], axis=1),
    }


def kernel(**inputs):
    import concourse.bacc as _bacc
    from concourse.bass_utils import run_bass_kernel_spmd as _run

    nc = _bacc.Bacc("TRN2", target_bir_lowering=False, num_devices=1)
    arrays, aps = {}, {}
    for name, x in lay_out({k: np.asarray(x) for k, x in inputs.items()}).items():
        x = np.ascontiguousarray(x)
        arrays[f"in_{name}"] = x
        aps[name] = nc.dram_tensor(f"in_{name}", x.shape, mybir.dt.from_np(x.dtype), kind="ExternalInput").ap()
    aps["out"] = nc.dram_tensor("out_0", (P, KD, T), F32, kind="ExternalOutput").ap()
    program(nc, aps)
    r = _run(nc, [arrays], core_ids=[0])
    got = r.results[0]["out_0"]
    return np.ascontiguousarray(got.transpose(1, 0, 2).reshape(D, T).T).reshape(1, T, D)
```
